# Optimizing a Trainium2 kernel written in Bass

```python
import jax, jax.numpy as jnp
from jax import lax
import numpy as np

D_MODEL = 1024
BATCH = 1
SEQ = 512
DEPTH = 1

N_META = 16
EPS = 1e-6
NEG_INF = -1e30
FOX_HEADS = 8
FOX_HEAD_DIM = 64
FOX_BLOCK = 128
FOX_W = FOX_HEADS * FOX_HEAD_DIM
GDN_HEADS = 8
GDN_HEAD_DIM = 128
GDN_CHUNK = 64
GDN_CONV = 4
GDN_W = GDN_HEADS * GDN_HEAD_DIM
N_BRANCH = 2
D_FF = 2816
FFN_CONV = 3
IN_SIZES = [FOX_W, FOX_W, FOX_W, FOX_HEADS,
            GDN_W, GDN_W, GDN_W, GDN_HEADS, GDN_HEADS,
            GDN_W,
            N_BRANCH * D_MODEL]
D_IN = int(sum(IN_SIZES))
IN_SPLIT = [int(c) for c in np.cumsum(IN_SIZES)[:-1]]

kernel_name = "hybrid_fox_gdn_convffn_trunk"

def rmsnorm(x, g):
    xf = x.astype(jnp.float32)
    y = xf * lax.rsqrt(jnp.mean(xf * xf, axis=-1, keepdims=True) + EPS)
    return (y * g.astype(jnp.float32)).astype(x.dtype)

def l2norm(x):
    return x * lax.rsqrt(jnp.sum(x * x, axis=-1, keepdims=True) + EPS)

def causal_dwconv(x, w):
    K, C = w.shape
    return lax.conv_general_dilated(x, w[:, None, :].astype(x.dtype), window_strides=(1,),
                                    padding=[(K - 1, 0)], dimension_numbers=('NWC', 'WIO', 'NWC'),
                                    feature_group_count=C)

def fox_attention(q, k, v, log_f):
    B_, L, H, Dh = q.shape
    pad = (-L) % FOX_BLOCK
    Lp = L + pad
    nb = Lp // FOX_BLOCK
    p4 = ((0, 0), (pad, 0), (0, 0), (0, 0))
    qp, kp, vp = jnp.pad(q, p4), jnp.pad(k, p4), jnp.pad(v, p4)
    F = jnp.cumsum(jnp.pad(log_f, ((0, 0), (pad, 0), (0, 0))), axis=1)
    Fk = F.transpose(0, 2, 1)
    kpos = jnp.arange(Lp)
    key_valid = kpos >= pad
    qb = qp.reshape(B_, nb, FOX_BLOCK, H, Dh).transpose(1, 0, 2, 3, 4)
    Fq = Fk.reshape(B_, H, nb, FOX_BLOCK).transpose(2, 0, 1, 3)
    scale = Dh ** -0.5

    def block(args):
        i, q_blk, F_blk = args
        qpos = i * FOX_BLOCK + jnp.arange(FOX_BLOCK)
        s = jnp.einsum('bqhd,bkhd->bhqk', q_blk, kp, preferred_element_type=jnp.float32) * scale
        s = s + F_blk[..., :, None] - Fk[:, :, None, :]
        mask = (kpos[None, :] <= qpos[:, None]) & key_valid[None, :]
        p = jax.nn.softmax(jnp.where(mask, s, NEG_INF), axis=-1)
        return jnp.einsum('bhqk,bkhd->bqhd', p.astype(vp.dtype), vp)

    out = lax.map(block, (jnp.arange(nb), qb, Fq))
    return out.transpose(1, 0, 2, 3, 4).reshape(B_, Lp, H, Dh)[:, pad:]

def gated_delta_rule(q, k, v, beta, g):
    B_, L, H, Dk = q.shape
    Dv = v.shape[-1]
    C = GDN_CHUNK
    pad = (-L) % C
    Lp = L + pad
    N = Lp // C
    p4 = ((0, 0), (pad, 0), (0, 0), (0, 0))
    p3 = ((0, 0), (pad, 0), (0, 0))

    def chunks4(t):
        return jnp.pad(t, p4).reshape(B_, N, C, H, t.shape[-1]).transpose(0, 3, 1, 2, 4)

    def chunks3(t):
        return jnp.pad(t, p3).reshape(B_, N, C, H).transpose(0, 3, 1, 2)

    qc, kc, vc = chunks4(q), chunks4(k), chunks4(v)
    bc, gc = chunks3(beta), chunks3(g)
    G = jnp.cumsum(gc, axis=-1)
    idx = jnp.arange(C)
    incl = idx[:, None] >= idx[None, :]
    strict = idx[:, None] > idx[None, :]
    diff = G[..., :, None] - G[..., None, :]
    decay_incl = jnp.exp(jnp.where(incl, diff, -jnp.inf))
    decay_strict = jnp.where(strict, decay_incl, 0.0)
    kb = kc * bc[..., None]
    M = jnp.einsum('bhncd,bhnsd->bhncs', kb, kc) * decay_strict
    A = M + jnp.eye(C, dtype=M.dtype)
    u_hat = lax.linalg.triangular_solve(A, vc * bc[..., None], left_side=True, lower=True, unit_diagonal=True)
    w = lax.linalg.triangular_solve(A, kb * jnp.exp(G)[..., None], left_side=True, lower=True, unit_diagonal=True)
    qg = qc * jnp.exp(G)[..., None]
    aqk = jnp.einsum('bhncd,bhnsd->bhncs', qc, kc) * decay_incl
    kd = kc * jnp.exp(G[..., -1:] - G)[..., None]
    gC = jnp.exp(G[..., -1])

    def to_front(t):
        return jnp.moveaxis(t, 2, 0)

    def step(S, xs):
        u_c, w_c, qg_c, a_c, kd_c, g_c = xs
        U = u_c - jnp.einsum('bhck,bhkv->bhcv', w_c, S)
        o = jnp.einsum('bhck,bhkv->bhcv', qg_c, S) + jnp.einsum('bhcs,bhsv->bhcv', a_c, U)
        S = S * g_c[..., None, None] + jnp.einsum('bhck,bhcv->bhkv', kd_c, U)
        return S, o

    S0 = jnp.zeros((B_, H, Dk, Dv), jnp.float32)
    _, o = lax.scan(step, S0, (to_front(u_hat), to_front(w), to_front(qg), to_front(aqk), to_front(kd), to_front(gC)))
    return o.transpose(1, 0, 3, 2, 4).reshape(B_, Lp, H, Dv)[:, pad:]

def setup_inputs(seed: int = 0) -> dict:
    key = jax.random.key(seed)
    ks = jax.random.split(key, 20)
    f32 = jnp.float32

    def nrm(k, shape, scale):
        return jax.random.normal(k, shape, f32) * scale

    dt = jnp.exp(jax.random.uniform(ks[7], (DEPTH, GDN_HEADS), f32, np.log(1e-3), np.log(1e-1)))
    return {
        "x": nrm(ks[0], (BATCH, SEQ, D_MODEL), 1.0),
        "meta_tokens": nrm(ks[1], (N_META, D_MODEL), 1.0),
        "norm1_g": 1.0 + nrm(ks[2], (DEPTH, D_MODEL), 0.02),
        "w_in": nrm(ks[3], (DEPTH, D_MODEL, D_IN), D_MODEL ** -0.5),
        "fox_f_bias": 2.0 + nrm(ks[4], (DEPTH, FOX_HEADS), 0.5),
        "fox_q_norm_g": 1.0 + nrm(ks[5], (DEPTH, FOX_HEAD_DIM), 0.02),
        "fox_k_norm_g": 1.0 + nrm(ks[6], (DEPTH, FOX_HEAD_DIM), 0.02),
        "gdn_conv_w": nrm(ks[8], (DEPTH, GDN_CONV, 3 * GDN_W), GDN_CONV ** -0.5),
        "gdn_a_log": jnp.log(jax.random.uniform(ks[9], (DEPTH, GDN_HEADS), f32, 1.0, 16.0)),
        "gdn_dt_bias": jnp.log(jnp.expm1(dt)),
        "gdn_norm_g": 1.0 + nrm(ks[10], (DEPTH, GDN_HEAD_DIM), 0.02),
        "w_branch_a": nrm(ks[11], (DEPTH, FOX_W, D_MODEL), FOX_W ** -0.5),
        "w_branch_b": nrm(ks[12], (DEPTH, GDN_W, D_MODEL), GDN_W ** -0.5),
        "w_out": nrm(ks[13], (DEPTH, D_MODEL, D_MODEL), D_MODEL ** -0.5),
        "norm2_g": 1.0 + nrm(ks[14], (DEPTH, D_MODEL), 0.02),
        "w_up": nrm(ks[15], (DEPTH, D_MODEL, 2 * D_FF), D_MODEL ** -0.5),
        "ffn_conv_w": nrm(ks[16], (DEPTH, FFN_CONV, 2 * D_FF), FFN_CONV ** -0.5),
        "w_down": nrm(ks[17], (DEPTH, D_FF, D_MODEL), D_FF ** -0.5),
    }

def reference(x, meta_tokens, norm1_g, w_in, fox_f_bias, fox_q_norm_g, fox_k_norm_g, gdn_conv_w,
              gdn_a_log, gdn_dt_bias, gdn_norm_g, w_branch_a, w_branch_b, w_out, norm2_g, w_up,
              ffn_conv_w, w_down):
    B_, S_, D = x.shape
    meta = jnp.broadcast_to(meta_tokens.astype(x.dtype)[None], (B_, N_META, D))
    h_res = jnp.concatenate([meta, x], axis=1)
    L = h_res.shape[1]
    f32 = jnp.float32
    for l in range(DEPTH):
        h = rmsnorm(h_res, norm1_g[l])
        proj = h @ w_in[l]
        (fq, fk, fv, f_logit, gq, gk, gv, b_logit, a_logit, gz, gate_logit) = jnp.split(proj, IN_SPLIT, axis=-1)

        fq = rmsnorm(fq.reshape(B_, L, FOX_HEADS, FOX_HEAD_DIM), fox_q_norm_g[l])
        fk = rmsnorm(fk.reshape(B_, L, FOX_HEADS, FOX_HEAD_DIM), fox_k_norm_g[l])
        fv = fv.reshape(B_, L, FOX_HEADS, FOX_HEAD_DIM)
        log_f = jax.nn.log_sigmoid(f_logit.astype(f32) + fox_f_bias[l].astype(f32))
        y_a = fox_attention(fq, fk, fv, log_f).reshape(B_, L, FOX_W) @ w_branch_a[l]

        qkv = jax.nn.silu(causal_dwconv(jnp.concatenate([gq, gk, gv], axis=-1), gdn_conv_w[l]))
        gq, gk, gv = jnp.split(qkv.astype(f32), 3, axis=-1)
        gq = l2norm(gq.reshape(B_, L, GDN_HEADS, GDN_HEAD_DIM)) * (GDN_HEAD_DIM ** -0.5)
        gk = l2norm(gk.reshape(B_, L, GDN_HEADS, GDN_HEAD_DIM))
        gv = gv.reshape(B_, L, GDN_HEADS, GDN_HEAD_DIM)
        beta = jax.nn.sigmoid(b_logit.astype(f32))
        g = -jnp.exp(gdn_a_log[l].astype(f32)) * jax.nn.softplus(a_logit.astype(f32) + gdn_dt_bias[l].astype(f32))
        o_b = gated_delta_rule(gq, gk, gv, beta, g)
        o_b = rmsnorm(o_b, gdn_norm_g[l]).astype(x.dtype) * jax.nn.silu(gz.reshape(B_, L, GDN_HEADS, GDN_HEAD_DIM))
        y_b = o_b.reshape(B_, L, GDN_W) @ w_branch_b[l]

        gates = jax.nn.sigmoid(gate_logit).reshape(B_, L, N_BRANCH, D)
        mixed = gates[:, :, 0] * y_a + gates[:, :, 1] * y_b
        h_res = h_res + mixed @ w_out[l]

        h = rmsnorm(h_res, norm2_g[l])
        up = causal_dwconv(h @ w_up[l], ffn_conv_w[l])
        u_gate, u_val = jnp.split(up, 2, axis=-1)
        h_res = h_res + (jax.nn.silu(u_gate) * u_val) @ w_down[l]
    return h_res[:, N_META:]


_drawn_inputs = setup_inputs


def setup_inputs(seed=0):
    import zlib

    import numpy as np

    out = dict(_drawn_inputs(seed))
    spreads = {}
    factors = {'norm1_g': 4.06,
     'fox_q_norm_g': 8.0,
     'fox_k_norm_g': 8.0,
     'gdn_norm_g': 7.487,
     'norm2_g': 12.74}
    for name, (base, spread) in spreads.items():
        noise = np.random.default_rng([zlib.crc32(name.encode()), seed]).standard_normal(out[name].shape)
        drawn = base * np.exp(spread * noise) if base else spread * noise
        out[name] = __import__('jax').numpy.asarray(drawn.astype(out[name].dtype))
    for name, factor in factors.items():
        out[name] = (out[name] * factor).astype(out[name].dtype)
    return out
```

```python
from contextlib import ExitStack

import numpy as np

import concourse.bass as bass
import concourse.mybir as mybir

F32 = mybir.dt.float32
F32R = mybir.dt.float32r
ACT = mybir.ActivationFunctionType
ALU = mybir.AluOpType
AX = mybir.AxisListType

P = 128
D = 1024
SEQ = 512
N_META = 16
L = SEQ + N_META
HL = L // 2
T = 88
NT = L // T
TH = NT // 2
KD = D // P
EPS = 1e-6
FOX_HEADS, FOX_DIM = 8, 64
FOX_BLOCKS = FOX_HEADS * FOX_DIM // P
HEADS, DH = 8, 128
HH = HEADS // 2
D_FF = 2816
FF_BLOCKS = D_FF // P
GDN_TAPS, FFN_TAPS = 4, 3
UNIT = KD * P

U_QK = 0
U_V = U_QK + 2 * FOX_BLOCKS
U_GDN = U_V + FOX_BLOCKS
U_Z = U_GDN + 3 * HEADS
U_MIX = U_Z + HEADS
MIX_UNITS = 4
U_OUT = U_MIX + MIX_UNITS * KD
U_UP = U_OUT + KD
U_DOWN = U_UP + 2 * FF_BLOCKS
DOWN_UNITS = 3
N_UNITS = U_DOWN + DOWN_UNITS * KD

R_F, R_B, R_G, R_END = 0, 32, 64, 96
LEVELS = [2, 4, 8, 16, 32, 64]


def side_by_side(widths):
    at, out = 0, {}
    for name, w in widths:
        out[name] = at
        at += w
    return out, at


CONST, C_COLS = side_by_side([("ident", P), ("ones", P), ("ones64", P), ("incl", T), ("strict", T), ("pair", T),
                              ("neg", T), ("levels", len(LEVELS) * T), ("sel", HEADS * P)])
PARAM, P_COLS = side_by_side([("norm1", KD), ("norm2", KD), ("gdn_norm", 1), ("stat_bias", 1), ("stat_sign", 1),
                              ("a_log", 1), ("eps", 1), ("eps_dh", 1), ("qk", 3 * 2 * FOX_BLOCKS),
                              ("gdn_taps", GDN_TAPS * 3 * HEADS), ("ffn_taps", FFN_TAPS * 2 * FF_BLOCKS)])


def build_trunk(nc, x_t, w_small, w_units, params, consts, out_t):
    ctx = ExitStack()
    with ctx:
        def sb(scope, name, shape, dt=F32):
            return scope.enter_context(nc.sbuf_tensor(name, shape, dt))

        sems = {}

        def sem(name):
            if name not in sems:
                sems[name] = ctx.enter_context(nc.semaphore(name))
            return sems[name]

        cst = sb(ctx, "cst", [P, C_COLS])
        prm = sb(ctx, "prm", [P, P_COLS])
        w_raw = sb(ctx, "w_raw", [P, 2, UNIT])
        w_hi = sb(ctx, "w_hi", [P, 2, UNIT], F32R)
        w_lo = sb(ctx, "w_lo", [P, 2, UNIT], F32R)
        h_hi = sb(ctx, "h_hi", [P, KD, L], F32R)
        h_lo = sb(ctx, "h_lo", [P, KD, L], F32R)
        with ExitStack() as mixing:
            fox_o = sb(mixing, "fox_o", [P, FOX_BLOCKS, L])
            o_raw = sb(mixing, "o_raw", [P, HEADS, L])
            tok = sb(mixing, "tok", [T, NT, R_END])
            stat = sb(mixing, "stat", [R_END, L])
            with ExitStack() as fox:
                st = [sb(fox, f"st{i}", [R_END, L]) for i in range(4)]
                f_sum = sb(fox, "f_sum", [FOX_HEADS, L])
                nf_sum = sb(fox, "nf_sum", [FOX_HEADS, L])
                coef = sb(fox, "coef", [R_END, 2])
                with ExitStack() as early:
                    x_in = sb(early, "x_in", [P, KD, L])
                    sq = sb(early, "sq", [P, 2, L])
                    root1 = sb(early, "root1", [P, L])
                    h32 = sb(early, "h32", [P, 2, L])
                    small_raw = sb(early, "small_raw", [P, KD, R_END])
                    small_hi = sb(early, "small_hi", [P, KD, R_END], F32R)
                    small_lo = sb(early, "small_lo", [P, KD, R_END], F32R)
                qk = sb(fox, "qk", [P, 2 * FOX_BLOCKS, L])
                f_row = sb(fox, "f_row", [2, FOX_HEADS, L])
                nf_row = sb(fox, "nf_row", [2, FOX_HEADS, L])
                v_tok = sb(fox, "v_tok", [T, NT, FOX_HEADS * FOX_DIM])
                v_chan = sb(fox, "v_chan", [P, 2, L])
                qk_sq = sb(fox, "qk_sq", [P, 2, L])
                qk_root = sb(fox, "qk_root", [P, 2, L])
                prob = sb(fox, "prob", [T, 3, L])
                prob_t = sb(fox, "prob_t", [T, 2, L])
                neg_max = sb(fox, "neg_max", [T, NT * FOX_HEADS])
                p_sum = sb(fox, "p_sum", [T, NT * FOX_HEADS])
                p_rec = sb(fox, "p_rec", [T, NT * FOX_HEADS])
            with ExitStack() as gdn:
                qkv = sb(gdn, "qkv", [P, 3 * HH, L])
                conv_in = sb(gdn, "conv_in", [P, 2, GDN_TAPS - 1 + L])
                conv_out = sb(gdn, "conv_out", [P, 2, L])
                k_bg = sb(gdn, "k_bg", [P, HH, L])
                k_b = sb(gdn, "k_b", [P, L])
                e_g = sb(gdn, "e_g", [P, L])
                g_end = sb(gdn, "g_end", [P, HH, NT])
                a_t = sb(gdn, "a_t", [T, NT, HH, T])
                inv_t = sb(gdn, "inv_t", [T, NT, HH, T])
                with ExitStack() as inverse:
                    decay = sb(inverse, "decay", [T, NT, T])
                    decay_s = sb(inverse, "decay_s", [T, NT, T])
                    m_t = sb(inverse, "m_t", [T, NT, HH, T])
                    inv = sb(inverse, "inv", [T, NT, HH, T])
                    mx = sb(inverse, "mx", [T, 3, HH, T])
                v_b = sb(gdn, "v_b", [T, NT, HH, DH])
                k_d = sb(gdn, "k_d", [T, NT, HH, DH])
                state = sb(gdn, "state", [P, 2, HH, DH])
                resid = sb(gdn, "resid", [T, HH, DH])
                u_new = sb(gdn, "u_new", [T, HH, DH])
            with ExitStack() as merge:
                fox_hi = sb(merge, "fox_hi", [P, FOX_BLOCKS, L], F32R)
                fox_lo = sb(merge, "fox_lo", [P, FOX_BLOCKS, L], F32R)
                ob_hi = sb(merge, "ob_hi", [P, HEADS, L], F32R)
                ob_lo = sb(merge, "ob_lo", [P, HEADS, L], F32R)
                mix_hi = sb(merge, "mix_hi", [P, KD, L], F32R)
                mix_lo = sb(merge, "mix_lo", [P, KD, L], F32R)
                zg = sb(merge, "zg", [P, 2, L])
                gate_a = sb(merge, "gate_a", [P, L])
                gate_b = sb(merge, "gate_b", [P, L])
                merge_end = nc.sbuf_base
        u_hi = sb(ctx, "u_hi", [P, FF_BLOCKS, L], F32R)
        u_lo = sb(ctx, "u_lo", [P, FF_BLOCKS, L], F32R)
        ff_in = sb(ctx, "ff_in", [P, 2, FFN_TAPS - 1 + L])
        ff_conv = sb(ctx, "ff_conv", [P, 2, L])
        ff_silu = sb(ctx, "ff_silu", [P, L])
        ff_u = sb(ctx, "ff_u", [P, 2, L])
        y_out = sb(ctx, "y_out", [P, 2, L])
        if nc.sbuf_base < merge_end:
            sb(ctx, "gap", [P, (merge_end - nc.sbuf_base) // 4 + 8])
        x_res = sb(ctx, "x_res", [P, KD, L])
        ps = ctx.enter_context(nc.psum_tensor("ps", [P, 8, 512], F32))

        def const(name, rows=P, cols=None, base=0):
            at = CONST[name]
            width = cols if cols else {"incl": T, "strict": T, "pair": T, "neg": T}.get(name, P)
            return cst[base:base + rows, at:at + width]

        def param(name, i=0, rows=P):
            return prm[0:rows, bass.ds(i + PARAM[name], 1)]

        def pair(a, rows=P):
            return ps[0:rows, 2 * a:2 * a + 2, 0:HL]

        def halves(ap):
            return ap.rearrange("p (h n) -> p h n", h=2)

        def tiles_of(ap, w):
            return ap.rearrange("p h (t c) -> p h t c", c=w)

        def block_of(buf, i):
            return buf[:, bass.ds(i, 1), :].rearrange("p o (h n) -> p (o h) n", h=2)

        def flat(buf, i):
            return buf[:, bass.ds(i, 1), :].rearrange("p o n -> p (o n)")

        def over_heads(ap):
            return ap.unsqueeze(1).broadcast_to([T, HH, T])

        def level_mask(n):
            at = CONST["levels"] + n * T
            return cst[0:T, at:at + T]

        def sel(head, base):
            at = CONST["sel"] + head * P
            return cst[base:base + HEADS, at:at + P]

        W_LOADED = [sem("w_loaded0"), sem("w_loaded1")]
        HI_READY, LO_READY = sem("hi_ready"), sem("lo_ready")
        UNIT_USED = sem("unit_used")
        ACC_FREE = [sem("acc_free0"), sem("acc_free1")]

        def split_hi(act, p, s, first=False):
            act.wait_ge(W_LOADED[s], p * 16 + 16)
            if not first:
                act.wait_ge(UNIT_USED, p * 2 + (s - 1))
            nc.scalar.copy(w_hi[:, s, :], w_raw[:, s, :]).then_inc(HI_READY, 1)

        def split_lo(dve, p, s):
            dve.wait_ge(HI_READY, p * 2 + (s + 1))
            nc.vector.tensor_tensor(w_lo[:, s, :], w_raw[:, s, :], w_hi[:, s, :].bitcast(F32),
                                    ALU.subtract).then_inc(LO_READY, 1)

        def products(acc, s, hi, lo, tiles, start, stop, at=0):
            for k in range(tiles):
                for n, (w, x) in enumerate(((w_hi, hi), (w_hi, lo), (w_lo, hi))):
                    for half in range(2):
                        mm = nc.tensor.matmul(
                            ps[:, 2 * acc + half, 0:HL], w[:, s, k * P:(k + 1) * P],
                            x[:, at + k, half * HL:(half + 1) * HL],
                            start=start and k == 0 and n == 0, stop=stop and k == tiles - 1 and n == 2)
            return mm

        def sums(stationary, buf, s, bank):
            for half in range(2):
                mm = nc.tensor.matmul(ps[:, bank + half, 0:HL], stationary, buf[:, s, half * HL:(half + 1) * HL],
                                      start=True, stop=True)
            return mm

        fox_items = [(h, t) for h in range(FOX_HEADS) for t in range(NT)]
        N = len(fox_items)
        PAIR_ITEMS = 2 * NT
        TURNS = NT * len(LEVELS)
        UPDATES = NT * (len(LEVELS) + 1)

        block = ctx.enter_context(nc.Block())

        @block.sync
        def _(sp):
            def load_unit(u, s):
                sp.dma_start(w_raw[:, s, :], w_units[bass.ds(u, 1)].rearrange("o p n -> p (o n)")
                             ).then_inc(W_LOADED[s], 16)

            sp.dma_start(x_in[:], x_t).then_inc(sem("x_loaded"), 16)
            sp.dma_start(small_raw[:], w_small).then_inc(sem("small_loaded"), 16)
            for s in range(2):
                load_unit(s, s)
            with sp.Fori(1, N_UNITS // 2) as p:
                for s in range(2):
                    sp.wait_ge(LO_READY, p * 2 + (s - 1))
                    load_unit(p * 2 + s, s)

        @block.gpsimd
        def _(pool):
            pool.dma_start(cst[:], consts).then_inc(sem("const_loaded"), 16)
            pool.dma_start(prm[:], params).then_inc(sem("params_loaded"), 16)
            pool.wait_ge(sem("rows_ones"), 2)
            pool.wait_ge(sem("f_ready"), 2)
            pool.dma_start(f_row[0:1, :, :], f_sum[:, :]).then_inc(sem("f_rows"), 16)
            pool.dma_start(nf_row[1:2, :, :], nf_sum[:, :]).then_inc(sem("f_rows"), 16)
            pool.wait_ge(sem("o_normed"), HEADS)
            pool.dma_start(x_res[:], x_t).then_inc(sem("x_reloaded"), 16)
            for j in range(KD):
                pool.wait_ge(sem("y_ready"), j + 1)
                pool.dma_start(out_t[j], y_out[:, j % 2, N_META:L]).then_inc(sem(f"stored{j % 2}"), 16)
            for s in range(2):
                pool.wait_ge(sem(f"stored{s}"), 16 * KD // 2)

        @block.tensor
        def _(pe):
            def norm_sums(tag, buf):
                for k in range(KD):
                    pe.wait_ge(sem(tag + "_sq"), k + 1)
                    for half in range(2):
                        mm = nc.tensor.matmul(ps[:, 4 + half, 0:HL], const("ones"),
                                              buf[:, k % 2, half * HL:(half + 1) * HL],
                                              start=(k == 0), stop=(k == KD - 1))
                    mm.then_inc(sem(tag + "_sq_used"), 1)

            def dense_unit(p, s, hi, lo, slot_tiles=KD):
                pe.wait_ge(LO_READY, p * 2 + (s + 1))
                if not (isinstance(p, int) and p == 0):
                    pe.wait_ge(ACC_FREE[s], p)
                products(s, s, hi, lo, slot_tiles, True, True).then_inc(UNIT_USED, 1)

            def dense_loop(first, count, hi, lo):
                with pe.Fori(first // 2, (first + count) // 2) as p:
                    for s in range(2):
                        dense_unit(p, s, hi, lo)

            pe.wait_ge(sem("const_loaded"), 16)
            norm_sums("n1", sq)
            pe.wait_ge(sem("small_lo"), 1)
            pe.wait_ge(sem("n1_lo"), KD)
            for k in range(KD):
                for n, (w, x) in enumerate(((small_hi, h_hi), (small_hi, h_lo), (small_lo, h_hi))):
                    for half in range(2):
                        mm = nc.tensor.matmul(ps[0:R_END, 6 + half, 0:HL], w[:, k, :],
                                              x[:, k, half * HL:(half + 1) * HL],
                                              start=(k == 0 and n == 0), stop=(k == KD - 1 and n == 2))
            mm.then_inc(sem("small_done"), 1)

            def qk_sums(n, s):
                pe.wait_ge(sem("qk_sq"), n + 1)
                sums(const("ones64"), qk_sq, s, 4 + 2 * s).then_inc(sem("qk_sum"), 1)

            dense_unit(0, 0, h_hi, h_lo)
            dense_unit(0, 1, h_hi, h_lo)
            pe.wait_ge(sem("stat_in"), 1)
            qk_sums(0, 0)
            dense_unit(1, 0, h_hi, h_lo)
            qk_sums(1, 1)
            dense_unit(1, 1, h_hi, h_lo)
            pe.wait_ge(sem("qk_rooted"), 1)
            qk_sums(2, 0)
            with pe.Fori(2, FOX_BLOCKS) as p:
                for s in range(2):
                    dense_unit(p, s, h_hi, h_lo)
                    pe.wait_ge(sem("qk_rooted"), p * 2 + (s - 2))
                    qk_sums(p * 2 + (s - 1), 1 - s)
            pe.wait_ge(sem("qk_rooted"), 2 * FOX_BLOCKS - 2)
            qk_sums(2 * FOX_BLOCKS - 1, 1)

            pe.wait_ge(sem("qk_rooted"), 2 * FOX_BLOCKS)

            def turn_v(b):
                pe.wait_ge(ACC_FREE[b % 2], (U_V + b) // 2 + 1)
                if b >= 2:
                    pe.wait_ge(sem("v_tok"), b - 1)
                for t in range(NT):
                    mm = nc.tensor.transpose(ps[0:T, 4 + 2 * (b % 2) + t // TH, (t % TH) * P:(t % TH + 1) * P],
                                             v_chan[:, b % 2, t * T:(t + 1) * T], const("ident"))
                mm.then_inc(sem("v_turned"), 1)

            for b in range(FOX_BLOCKS):
                dense_unit((U_V + b) // 2, b % 2, h_hi, h_lo)
                if b:
                    turn_v(b - 1)
            turn_v(FOX_BLOCKS - 1)

            pe.wait_ge(sem("v_tok"), FOX_BLOCKS)
            pe.wait_ge(sem("stat_rows"), 3)
            for t in range(NT):
                mm = nc.tensor.transpose(ps[0:T, 4 + t // TH, (t % TH) * R_END:(t % TH + 1) * R_END],
                                         stat[:, t * T:(t + 1) * T], const("ident", R_END, R_END))
            mm.then_inc(sem("tok_turned"), 1)
            pe.wait_ge(sem("tok_ready"), 1)

            pe.wait_ge(sem("qk_normed"), 2 * FOX_BLOCKS)
            pe.wait_ge(sem("f_rows"), 32)

            def scores(n):
                h, t = fox_items[n]
                rows = slice(FOX_DIM * (h % 2), FOX_DIM * (h % 2) + FOX_DIM)
                if n >= 2:
                    pe.wait_ge(sem("prob_ready"), n - 1)
                a = 2 * (n % 2)
                at = slice(t * T, (t + 1) * T)
                keys = (t + 1) * T
                for bank, k0, k1 in [(a, 0, keys)] if keys <= 512 else [(a, 0, HL), (a + 1, HL, L)]:
                    o = ps[0:T, bank, 0:k1 - k0]
                    last = k1 == keys
                    nc.tensor.matmul(o, qk[rows, h // 2, at], qk[rows, FOX_BLOCKS + h // 2, k0:k1],
                                     start=True, stop=False)
                    mm = nc.tensor.matmul(o, f_row[0:2, h, at], nf_row[0:2, h, k0:k1], start=False, stop=not last)
                    if last:
                        mm = nc.tensor.matmul(ps[0:T, bank, k1 - k0 - T:k1 - k0], const("ident", T, T),
                                              const("neg", T), start=False, stop=True)
                mm.then_inc(sem("scored"), 1)

            def turn_probs(n):
                t = fox_items[n][1]
                pe.wait_ge(sem("prob_scaled"), n + 1)
                if n >= 1:
                    pe.wait_ge(sem("prob_t"), n)
                for j in range(t + 1):
                    mm = nc.tensor.transpose(ps[0:T, 4 + j // TH, (j % TH) * T:(j % TH + 1) * T],
                                             prob[:, n % 3, j * T:(j + 1) * T], const("ident", T, T))
                mm.then_inc(sem("prob_turned"), 1)

            def weigh_values(n):
                h, t = fox_items[n]
                pe.wait_ge(sem("prob_t"), n + 1)
                if n % PAIR_ITEMS == 0 and n:
                    pe.wait_ge(sem("fox_taken"), n // PAIR_ITEMS)
                r0 = FOX_DIM * (h % 2)
                o = ps[r0:r0 + FOX_DIM, 6 + t // TH, (t % TH) * T:(t % TH + 1) * T]
                for j in range(t + 1):
                    mm = nc.tensor.matmul(o, v_tok[:, j, h * FOX_DIM:(h + 1) * FOX_DIM],
                                          prob_t[:, n % 2, j * T:(j + 1) * T], start=(j == 0), stop=(j == t))
                mm.then_inc(sem("weighed"), 1)

            for n in range(N + 3):
                if n < N:
                    scores(n)
                if 0 <= n - 2 < N:
                    turn_probs(n - 2)
                if 0 <= n - 3 < N:
                    weigh_values(n - 3)
            pe.wait_ge(sem("fox_taken"), FOX_BLOCKS)

            for half_no in range(2):
                dense_loop(U_GDN + half_no * 3 * HH, 3 * HH, h_hi, h_lo)
                m0 = half_no * HH
                for n in range(2 * HH):
                    pe.wait_ge(sem("gn_sq"), 2 * m0 + n + 1)
                    if n >= 2:
                        pe.wait_ge(sem("gn_rooted"), 2 * m0 + n - 1)
                    sums(const("ones"), conv_out, n % 2, 4 + 2 * (n % 2)).then_inc(sem("gn_sum"), 1)
                pe.wait_ge(sem("gn_normed"), 2 * m0 + 2 * HH)
                for s in range(2):
                    pe.wait_ge(ACC_FREE[s], (U_GDN + 3 * (m0 + HH)) // 2)
                for j in range(HH):
                    m = m0 + j
                    if j:
                        pe.wait_ge(sem("e_g"), 2 * m)
                        pe.wait_ge(sem("decay_diff"), m)
                        pe.wait_ge(sem("k_b"), m)
                    for bank, base in ((0, 0), (2, R_B)):
                        for half in range(2):
                            mm = nc.tensor.matmul(ps[:, bank + half, 0:HL], sel(m, base),
                                                  stat[base:base + HEADS, half * HL:(half + 1) * HL],
                                                  start=True, stop=True)
                        mm.then_inc(sem("spread"), 1)
                    pe.wait_ge(sem("k_b"), m + 1)
                    if j:
                        pe.wait_ge(sem("mat_taken"), 2 * m)
                    for which in range(2):
                        for t in range(NT):
                            at = slice(t * T, (t + 1) * T)
                            mm = nc.tensor.matmul(
                                ps[0:T, 4 + 2 * which + t // TH, (t % TH) * T:(t % TH + 1) * T],
                                qkv[:, HH + j, at], k_b[:, at] if which else qkv[:, j, at], start=True, stop=True)
                        mm.then_inc(sem("mats"), 1)

                def turn_inv(c, bank):
                    for j in range(HH):
                        mm = nc.tensor.transpose(ps[0:T, bank, j * T:(j + 1) * T], inv_t[:, c, j, :],
                                                 const("ident", T, T))
                    mm.then_inc(sem("inv_turned"), 1)

                turned, updated = half_no * TURNS, half_no * UPDATES
                pe.wait_ge(sem("mat_taken"), 2 * (m0 + HH))
                pe.wait_ge(sem("e_g"), 2 * (m0 + HH))
                pe.wait_ge(sem("decay_diff"), m0 + HH)
                for c in range(NT):
                    pe.wait_ge(sem("inv_t"), updated + c + 1)
                    if c >= 2:
                        pe.wait_ge(sem("inv"), turned + c - 1)
                    turn_inv(c, 6 + c % 2)
                for lv in range(len(LEVELS)):
                    for step in range(NT + 4):
                        if step < NT:
                            c, n = step, lv * NT + step
                            pe.wait_ge(sem("inv"), turned + n + 1)
                            if n >= 3:
                                pe.wait_ge(sem("mx"), turned + n - 2)
                            for j in range(HH):
                                mm = nc.tensor.matmul(ps[0:T, n % 3, j * T:(j + 1) * T], m_t[:, c, j, :],
                                                      inv[:, c, j, :], start=True, stop=True)
                            mm.then_inc(sem("mx_done"), 1)
                        if 0 <= step - 2 < NT:
                            c, n = step - 2, lv * NT + step - 2
                            pe.wait_ge(sem("mx"), turned + n + 1)
                            if n >= 3:
                                pe.wait_ge(sem("inv_t"), updated + NT + n - 2)
                            for j in range(HH):
                                mm = nc.tensor.matmul(ps[0:T, 3 + n % 3, j * T:(j + 1) * T], mx[:, n % 3, j, :],
                                                      inv_t[:, c, j, :], start=True, stop=True)
                            mm.then_inc(sem("change"), 1)
                        if 0 <= step - 4 < NT and lv < len(LEVELS) - 1:
                            c, n = step - 4, lv * NT + step - 4
                            pe.wait_ge(sem("inv_t"), updated + NT + n + 1)
                            pe.wait_ge(sem("inv"), turned + NT + n - 1)
                            turn_inv(c, 6 + n % 2)
                pe.wait_ge(sem("inv_t"), updated + UPDATES)
                pe.wait_ge(sem("inv"), turned + TURNS)
                for j in range(HH):
                    for which, src in ((0, 2 * HH + j), (1, HH + j)):
                        if j:
                            pe.wait_ge(sem("vk_taken"), 2 * (m0 + j) - 1 + which)
                        for t in range(NT):
                            mm = nc.tensor.transpose(
                                ps[0:T, 4 + 2 * which + t // TH, (t % TH) * P:(t % TH + 1) * P],
                                qkv[:, src, t * T:(t + 1) * T], const("ident"))
                        mm.then_inc(sem("vk_turned"), 1)
                pe.wait_ge(sem("vk_taken"), 2 * (m0 + HH))
                pe.wait_ge(sem("q_g"), m0 + HH)

                for c in range(NT):
                    n = half_no * NT + c
                    at = slice(c * T, (c + 1) * T)
                    if c:
                        pe.wait_ge(sem("state"), (half_no * (NT - 1) + c) * HH)
                        for j in range(HH):
                            mm = nc.tensor.matmul(ps[0:T, 0, j * DH:(j + 1) * DH], k_bg[:, j, at],
                                                  state[:, c % 2, j, :], start=True, stop=True)
                        mm.then_inc(sem("ks_done"), 1)
                        pe.wait_ge(sem("resid"), half_no * (NT - 1) + c)
                    for j in range(HH):
                        mm = nc.tensor.matmul(ps[0:T, 1, j * DH:(j + 1) * DH], inv_t[:, c, j, :],
                                              resid[:, j, :] if c else v_b[:, 0, j, :], start=True, stop=True)
                    mm.then_inc(sem("u_done"), 1)
                    pe.wait_ge(sem("u_new"), n + 1)
                    if c < NT - 1:
                        for j in range(HH):
                            mm = nc.tensor.matmul(ps[:, 2, j * DH:(j + 1) * DH], k_d[:, c, j, :], u_new[:, j, :],
                                                  start=True, stop=True)
                        mm.then_inc(sem("grown"), 1)
                    if c >= 2:
                        pe.wait_ge(sem("o_raw"), n - 1)
                    for j in range(HH):
                        o = ps[:, 3 + c % 2, j * T:(j + 1) * T]
                        if c:
                            nc.tensor.matmul(o, state[:, c % 2, j, :], qkv[:, j, at], start=True, stop=False)
                        mm = nc.tensor.matmul(o, u_new[:, j, :], a_t[:, c, j, :], start=(c == 0), stop=True)
                    mm.then_inc(sem("o_done"), 1)
                pe.wait_ge(sem("o_raw"), (half_no + 1) * NT)
                for j in range(HH):
                    pe.wait_ge(sem("on_sq"), m0 + j + 1)
                    if j >= 2:
                        pe.wait_ge(sem("on_rooted"), m0 + j - 1)
                    sums(const("ones"), conv_out, j % 2, 4 + 2 * (j % 2)).then_inc(sem("on_sum"), 1)
                pe.wait_ge(sem("on_rooted"), m0 + HH)

            dense_loop(U_Z, HEADS, h_hi, h_lo)
            pe.wait_ge(sem("fox_split"), 2)
            pe.wait_ge(sem("ob_lo"), HEADS)
            with pe.Fori(U_MIX // 2, U_OUT // 2 - 1, 2) as p:
                for n, (hi, lo, tiles) in enumerate(((h_hi, h_lo, KD), (h_hi, h_lo, KD), (ob_hi, ob_lo, KD),
                                                     (fox_hi, fox_lo, FOX_BLOCKS))):
                    dense_unit(p + n // 2, n % 2, hi, lo, tiles)
            pe.wait_ge(sem("mix_lo"), KD)
            dense_loop(U_OUT, KD, mix_hi, mix_lo)
            norm_sums("n2", ff_u)
            pe.wait_ge(sem("n2_lo"), KD)

            dense_loop(U_UP, 2 * FF_BLOCKS, h_hi, h_lo)
            pe.wait_ge(sem("u_lo"), FF_BLOCKS)
            with pe.Fori(0, KD // 2) as q:
                for s in range(2):
                    pe.wait_ge(ACC_FREE[s], q + U_DOWN // 2)
                    for part in range(DOWN_UNITS):
                        n = s * DOWN_UNITS + part
                        pe.wait_ge(LO_READY, q * 2 * DOWN_UNITS + (U_DOWN + n + 1))
                        tiles = min(KD, FF_BLOCKS - part * KD)
                        mm = products(s, n % 2, u_hi, u_lo, tiles, part == 0, part == DOWN_UNITS - 1, at=part * KD)
                        mm.then_inc(UNIT_USED, 1)

        @block.scalar
        def _(act):
            def norm(tag, x, buf, root, h):
                for k in range(KD):
                    if k >= 2:
                        act.wait_ge(sem(tag + "_sq_used"), k - 1)
                    nc.scalar.activation(buf[:, k % 2, :], x[:, k, :], ACT.Square).then_inc(sem(tag + "_sq"), 1)
                act.wait_ge(sem(tag + "_sq_used"), KD)
                nc.scalar.activation(halves(root), pair(2), ACT.Sqrt, bias=param("eps"),
                                     scale=1.0 / D).then_inc(sem(tag + "_rooted"), 1)
                for k in range(KD):
                    act.wait_ge(sem(tag + "_h"), k + 1)
                    nc.scalar.copy(h_hi[:, k, :], h[:, k % 2, :]).then_inc(sem(tag + "_hi"), 1)

            act.wait_ge(sem("small_loaded"), 16)
            nc.scalar.copy(small_hi[:], small_raw[:]).then_inc(sem("small_hi"), 1)
            for s in range(2):
                split_hi(act, 0, s, first=True)
            act.wait_ge(sem("params_loaded"), 16)
            act.wait_ge(sem("x_loaded"), 16)
            norm("n1", x_in, sq, root1[:], h32)

            act.wait_ge(sem("n1_lo"), KD)
            act.wait_ge(sem("small_done"), 1)

            def qk_take(p, s, n, first):
                act.wait_ge(UNIT_USED, p * 2 + (s + 1))
                nc.scalar.copy(block_of(qk, n), pair(s)).then_inc(sem("qk_raw"), 1)
                if not first:
                    act.wait_ge(sem("qk_sum"), n - 1)
                nc.scalar.activation(halves(qk_sq[:, s, :]), pair(s), ACT.Square).then_inc(sem("qk_sq"), 1)
                act.wait_ge(sem("qk_sq"), n + 1)
                nc.scalar.sem_inc(ACC_FREE[s], 1)
                split_hi(act, p + 1, s)

            def qk_take_root(n, s, first):
                act.wait_ge(sem("qk_sum"), n + 1)
                if not first:
                    act.wait_ge(sem("qk_normed"), n - 1)
                nc.scalar.activation(halves(qk_root[:, s, :]), pair(2 + s), ACT.Sqrt, bias=param("qk", n * 3 + 2),
                                     scale=param("qk", n * 3 + 1)).then_inc(sem("qk_rooted"), 1)

            qk_take(0, 0, 0, True)
            qk_take(0, 1, 1, True)
            qk_take_root(0, 0, True)
            qk_take(1, 0, 2, False)
            qk_take_root(1, 1, True)
            qk_take(1, 1, 3, False)
            qk_take_root(2, 0, False)
            with act.Fori(2, FOX_BLOCKS) as p:
                for s in range(2):
                    qk_take(p, s, p * 2 + s, False)
                    qk_take_root(p * 2 + (s - 1), 1 - s, False)
            qk_take_root(2 * FOX_BLOCKS - 1, 1, False)

            act.wait_ge(sem("stat_in"), 1)
            nc.scalar.activation(st[1][:], st[0][:], ACT.Abs).then_inc(sem("stat_abs"), 1)
            act.wait_ge(sem("stat_abs"), 1)
            nc.scalar.activation(st[2][:], st[1][:], ACT.Exp, scale=-1.0).then_inc(sem("stat_exp"), 1)
            nc.scalar.activation(st[3][R_B:R_G, :], st[0][R_B:R_G, :], ACT.Exp).then_inc(sem("beta_exp"), 1)
            nc.scalar.activation(coef[:, 0:1], param("a_log", rows=R_END), ACT.Exp).then_inc(sem("coef"), 1)
            act.wait_ge(sem("stat_exp"), 1)
            nc.scalar.activation(st[1][:], st[2][:], ACT.Ln, bias=1.0).then_inc(sem("stat_ln"), 1)

            for b in range(FOX_BLOCKS):
                p, s = (U_V + b) // 2, b % 2
                act.wait_ge(UNIT_USED, U_V + b + 1)
                if b >= 2:
                    act.wait_ge(sem("v_turned"), b - 1)
                nc.scalar.copy(halves(v_chan[:, s, :]), pair(s)).then_inc(ACC_FREE[s], 1)
                split_hi(act, p + 1, s)
            act.wait_ge(sem("to_end"), 1)
            nc.scalar.activation(stat[R_G:R_END, :], st[1][R_G:R_END, :], ACT.Exp).then_inc(sem("stat_rows"), 1)

            def exponentials(n):
                t = fox_items[n][1]
                keys = (t + 1) * T
                a = 2 * (n % 2)
                act.wait_ge(sem("neg_max"), n + 1)
                if n >= 3:
                    act.wait_ge(sem("prob_turned"), n - 2)
                src, dst = (ps[0:T, a, 0:keys], prob[:, n % 3, 0:keys]) if keys <= 512 else (
                    pair(n % 2, T), halves(prob[:, n % 3, :]))
                nc.scalar.activation(dst, src, ACT.Exp, bias=neg_max[:, n:n + 1],
                                     accum_out=p_sum[:, n:n + 1]).then_inc(sem("prob_ready"), 1)

            def take_turned(n):
                keys = (fox_items[n][1] + 1) * T
                act.wait_ge(sem("prob_turned"), n + 1)
                if n >= 2:
                    act.wait_ge(sem("weighed"), n - 1)
                if keys <= HL:
                    mm = nc.scalar.copy(prob_t[:, n % 2, 0:keys], ps[0:T, 4, 0:keys])
                else:
                    nc.scalar.copy(prob_t[:, n % 2, 0:HL], ps[0:T, 4, 0:HL])
                    mm = nc.scalar.copy(prob_t[:, n % 2, HL:keys], ps[0:T, 5, 0:keys - HL])
                mm.then_inc(sem("prob_t"), 1)

            for n in range(N + 2):
                if n < N:
                    exponentials(n)
                if n >= 2:
                    take_turned(n - 2)

            act.wait_ge(sem("fox_taken"), FOX_BLOCKS)
            act.wait_ge(sem("pads"), 1)
            for half_no in range(2):
                p0 = (U_GDN + half_no * 3 * HH) // 2
                c0 = half_no * 3 * HH
                m0 = half_no * HH

                def conv_silu(p, n, s, first):
                    act.wait_ge(UNIT_USED, p * 2 + (s + 1))
                    nc.scalar.copy(halves(conv_in[:, s, GDN_TAPS - 1:]), pair(s)).then_inc(ACC_FREE[s], 1)
                    split_hi(act, p + 1, s)
                    act.wait_ge(sem("conv3"), n + (c0 + 1))
                    nc.scalar.activation(flat(qkv, n), conv_out[:, s, :], ACT.Silu).then_inc(sem("qkv_ready"), 1)

                with act.Fori(p0, p0 + 3 * HH // 2) as p:
                    for s in range(2):
                        conv_silu(p, p * 2 + (s - 2 * p0), s, False)
                act.wait_ge(sem("qkv_ready"), c0 + 3 * HH)

                def gn_root(n):
                    act.wait_ge(sem("gn_sum"), 2 * m0 + n + 1)
                    if n >= 2:
                        act.wait_ge(sem("gn_normed"), 2 * m0 + n - 1)
                    is_q = n < HH
                    nc.scalar.activation(halves(conv_in[:, n % 2, GDN_TAPS - 1:]), pair(2 + n % 2), ACT.Sqrt,
                                         bias=param("eps_dh" if is_q else "eps"), scale=float(DH) if is_q else 1.0
                                         ).then_inc(sem("gn_rooted"), 1)

                for n in range(2 * HH + 1):
                    if n < 2 * HH:
                        if n >= 2:
                            act.wait_ge(sem("gn_sum"), 2 * m0 + n - 1)
                        nc.scalar.activation(conv_out[:, n % 2, :], qkv[:, n, :], ACT.Square
                                             ).then_inc(sem("gn_sq"), 1)
                    if n:
                        gn_root(n - 1)
                for j in range(HH):
                    m = m0 + j
                    act.wait_ge(sem("spread"), 2 * m + 1)
                    if j:
                        act.wait_ge(sem("q_g"), m)
                        act.wait_ge(sem("k_bg"), m)
                    nc.scalar.activation(halves(e_g[:]), pair(0), ACT.Exp).then_inc(sem("e_g"), 1)
                    nc.scalar.activation(g_end[:, j, :].rearrange("p (h t) -> p h t", h=2),
                                         pair(0)[:, :, T - 1::T], ACT.Exp).then_inc(sem("e_g"), 1)
                    act.wait_ge(sem("decay_diff"), m + 1)
                    nc.scalar.activation(decay[:], decay[:], ACT.Exp).then_inc(sem("decay_exp"), 1)
                turned = half_no * TURNS

                def take_inv(c, n):
                    act.wait_ge(sem("inv_turned"), turned + n + 1)
                    nc.scalar.copy(inv[:, c, :, :].rearrange("p j t -> p (j t)"), ps[0:T, 6 + n % 2, 0:HH * T]
                                   ).then_inc(sem("inv"), 1)

                for n in range(TURNS):
                    take_inv(n % NT, n)
                for c in range(NT):
                    n = half_no * NT + c
                    act.wait_ge(sem("u_done"), n + 1)
                    if n:
                        act.wait_ge(sem("o_done"), n)
                    nc.scalar.copy(u_new[:].rearrange("p j d -> p (j d)"), ps[0:T, 1, :]).then_inc(sem("u_new"), 1)
                    act.wait_ge(sem("o_done"), n + 1)
                    nc.scalar.copy(o_raw[:, m0:m0 + HH, c * T:(c + 1) * T],
                                   ps[:, 3 + c % 2, 0:HH * T].rearrange("p (j t) -> p j t", j=HH)
                                   ).then_inc(sem("o_raw"), 1)
                act.wait_ge(sem("o_raw"), (half_no + 1) * NT)

                def on_root(j):
                    act.wait_ge(sem("on_sum"), m0 + j + 1)
                    if j >= 2:
                        act.wait_ge(sem("o_normed"), m0 + j - 1)
                    nc.scalar.activation(halves(conv_in[:, j % 2, GDN_TAPS - 1:]), pair(2 + j % 2), ACT.Sqrt,
                                         bias=param("eps"), scale=1.0 / DH).then_inc(sem("on_rooted"), 1)

                for j in range(HH + 1):
                    if j < HH:
                        if j >= 2:
                            act.wait_ge(sem("on_sum"), m0 + j - 1)
                        nc.scalar.activation(conv_out[:, j % 2, :], o_raw[:, m0 + j, :], ACT.Square
                                             ).then_inc(sem("on_sq"), 1)
                    if j:
                        on_root(j - 1)
                act.wait_ge(sem("o_normed"), m0 + HH)

            nc.scalar.copy(fox_hi[:], fox_o[:]).then_inc(sem("fox_split"), 1)

            def gate_z(p, n, s, first):
                act.wait_ge(UNIT_USED, p * 2 + (s + 1))
                if not first:
                    act.wait_ge(sem("ob_lo"), n - 1)
                nc.scalar.activation(halves(zg[:, s, :]), pair(s), ACT.Silu).then_inc(ACC_FREE[s], 1)
                split_hi(act, p + 1, s)
                act.wait_ge(sem("gated"), n + 1)
                nc.scalar.copy(flat(ob_hi, n), zg[:, s, :]).then_inc(sem("ob_hi"), 1)

            for s in range(2):
                gate_z(U_Z // 2, s, s, True)
            with act.Fori(U_Z // 2 + 1, (U_Z + HEADS) // 2) as p:
                for s in range(2):
                    gate_z(p, p * 2 + (s - U_Z), s, False)

            def mixing_block(p, j, first):
                for s, gate in enumerate((gate_a, gate_b)):
                    act.wait_ge(UNIT_USED, p * 2 + (s + 1))
                    if not first:
                        act.wait_ge(sem("mix_lo"), j)
                    nc.scalar.activation(halves(gate[:]), pair(s), ACT.Tanh, scale=0.5).then_inc(ACC_FREE[s], 1)
                    split_hi(act, p + 1, s)
                for s in range(2):
                    split_hi(act, p + 2, s)
                act.wait_ge(sem("mixed"), j + 1)
                nc.scalar.activation(flat(mix_hi, j), gate_a[:], ACT.Copy, scale=0.5).then_inc(sem("mix_hi"), 1)

            mixing_block(U_MIX // 2, 0, True)
            with act.Fori(1, KD) as j:
                mixing_block(j * (MIX_UNITS // 2) + U_MIX // 2, j, False)
            with act.Fori(U_OUT // 2 + 1, (U_OUT + KD) // 2 + 1) as p:
                for s in range(2):
                    split_hi(act, p, s)

            for s in range(2):
                act.wait_ge(ACC_FREE[s], U_UP // 2)
            norm("n2", x_res, ff_u, ff_silu[:], ff_conv)

            def up_block(p, b, first):
                act.wait_ge(UNIT_USED, p * 2 + 1)
                if not first:
                    act.wait_ge(sem("ff_g"), b * 3)
                nc.scalar.copy(halves(ff_in[:, 0, FFN_TAPS - 1:]), pair(0)).then_inc(ACC_FREE[0], 1)
                split_hi(act, p + 1, 0)
                act.wait_ge(sem("ff_g"), b * 3 + 3)
                if not first:
                    act.wait_ge(sem("ff_u"), b)
                nc.scalar.activation(ff_silu[:], ff_conv[:, 0, :], ACT.Silu).then_inc(sem("ff_silu"), 1)
                act.wait_ge(UNIT_USED, p * 2 + 2)
                if not first:
                    act.wait_ge(sem("ff_v"), b * 3)
                nc.scalar.copy(halves(ff_in[:, 1, FFN_TAPS - 1:]), pair(1)).then_inc(ACC_FREE[1], 1)
                split_hi(act, p + 1, 1)
                act.wait_ge(sem("ff_u"), b + 1)
                nc.scalar.copy(flat(u_hi, b), ff_u[:, 0, :]).then_inc(sem("u_hi"), 1)

            act.wait_ge(sem("ff_pads"), 1)
            up_block(U_UP // 2, 0, True)
            with act.Fori(1, FF_BLOCKS) as b:
                up_block(b + U_UP // 2, b, False)
            with act.Fori(U_DOWN // 2 + 1, N_UNITS // 2) as p:
                for s in range(2):
                    split_hi(act, p, s)

        @block.vector
        def _(dve):
            def norm(tag, x, gain, root, h):
                dve.wait_ge(sem(tag + "_rooted"), 1)
                nc.vector.reciprocal(root, root).then_inc(sem(tag + "_rec"), 1)
                dve.wait_ge(sem(tag + "_rec"), 1)
                for k in range(KD + 1):
                    if k < KD:
                        if k >= 2:
                            dve.wait_ge(sem(tag + "_lo"), k - 1)
                        nc.vector.scalar_tensor_tensor(h[:, k % 2, :], x[:, k, :], param(gain, k), root,
                                                       ALU.mult, ALU.mult).then_inc(sem(tag + "_h"), 1)
                    if k:
                        dve.wait_ge(sem(tag + "_hi"), k)
                        nc.vector.tensor_tensor(h_lo[:, k - 1, :], h[:, (k - 1) % 2, :],
                                                h_hi[:, k - 1, :].bitcast(F32), ALU.subtract
                                                ).then_inc(sem(tag + "_lo"), 1)

            dve.wait_ge(sem("small_hi"), 1)
            nc.vector.tensor_tensor(small_lo[:], small_raw[:], small_hi[:].bitcast(F32),
                                    ALU.subtract).then_inc(sem("small_lo"), 1)
            for s in range(2):
                split_lo(dve, 0, s)
            dve.wait_ge(sem("params_loaded"), 16)
            norm("n1", x_in, "norm1", root1[:], h32)
            dve.wait_ge(sem("small_done"), 1)
            nc.vector.tensor_scalar(halves(st[0][:]), pair(3, R_END), param("stat_bias", rows=R_END),
                                    param("stat_sign", rows=R_END), ALU.add, ALU.mult).then_inc(sem("stat_in"), 1)

            def qk_normalize(n, s):
                dve.wait_ge(sem("qk_rooted"), n + 1)
                nc.vector.reciprocal(qk_root[:, s, :], qk_root[:, s, :]).then_inc(sem("qk_rec"), 1)
                dve.wait_ge(sem("qk_rec"), n + 1)
                nc.vector.scalar_tensor_tensor(flat(qk, n), flat(qk, n), param("qk", n * 3), qk_root[:, s, :],
                                               ALU.mult, ALU.mult).then_inc(sem("qk_normed"), 1)

            split_lo(dve, 1, 0)
            split_lo(dve, 1, 1)
            qk_normalize(0, 0)
            with dve.Fori(1, FOX_BLOCKS) as p:
                for s in range(2):
                    split_lo(dve, p + 1, s)
                    qk_normalize(p * 2 + (s - 1), 1 - s)
            qk_normalize(2 * FOX_BLOCKS - 1, 1)

            dve.wait_ge(sem("small_done"), 1)
            nc.vector.memset(f_row[:], 1.0).then_inc(sem("rows_ones"), 1)
            nc.vector.memset(nf_row[:], 1.0).then_inc(sem("rows_ones"), 1)
            dve.wait_ge(sem("stat_ln"), 1)
            nc.vector.scalar_tensor_tensor(st[2][:], st[0][:], 0.0, st[1][:], ALU.max, ALU.add
                                           ).then_inc(sem("softplus"), 1)
            dve.wait_ge(sem("coef"), 1)
            nc.vector.tensor_scalar(coef[:, 1:2], coef[:, 0:1], -1.0, None, ALU.mult).then_inc(sem("coef"), 1)
            dve.wait_ge(sem("softplus"), 1)
            dve.wait_ge(sem("coef"), 2)
            nc.vector.tensor_scalar(st[1][:], st[2][:], coef[:, 1:2], None, ALU.mult).then_inc(sem("log_gates"), 1)
            dve.wait_ge(sem("beta_exp"), 1)
            nc.vector.tensor_scalar(st[3][R_B:R_G, :], st[3][R_B:R_G, :], 1.0, None, ALU.add
                                    ).then_inc(sem("beta"), 1)
            dve.wait_ge(sem("beta"), 1)
            nc.vector.reciprocal(stat[R_B:R_G, :], st[3][R_B:R_G, :]).then_inc(sem("stat_rows"), 1)
            dve.wait_ge(sem("log_gates"), 1)
            src, dst, shift, steps = 1, 2, 1, 0
            while shift < T:
                a, b = (st[i][:].rearrange("p (t c) -> p t c", c=T) for i in (src, dst))
                nc.vector.tensor_tensor(b[:, :, shift:], a[:, :, shift:], a[:, :, :T - shift], ALU.add
                                        ).then_inc(sem("cumsum"), 1)
                nc.vector.tensor_copy(b[:, :, :shift], a[:, :, :shift]).then_inc(sem("cumsum"), 1)
                steps += 1
                dve.wait_ge(sem("cumsum"), 2 * steps)
                src, dst, shift = dst, src, 2 * shift
            g_rows = st[src][R_G:R_END, :].rearrange("p (t c) -> p t c", c=T)
            nc.vector.tensor_copy(stat[0:R_B, :], st[src][R_G:R_END, :]).then_inc(sem("stat_rows"), 1)
            nc.vector.tensor_tensor(st[dst][R_G:R_END, :].rearrange("p (t c) -> p t c", c=T),
                                    g_rows[:, :, T - 1:T].broadcast_to([R_END - R_G, NT, T]), g_rows, ALU.subtract
                                    ).then_inc(sem("to_end"), 1)
            nc.vector.tensor_copy(f_sum[:, 0:T], st[src][0:FOX_HEADS, 0:T]).then_inc(sem("f_tile"), 1)
            for t in range(1, NT):
                dve.wait_ge(sem("f_tile"), t)
                nc.vector.tensor_scalar(f_sum[:, t * T:(t + 1) * T], st[src][0:FOX_HEADS, t * T:(t + 1) * T],
                                        f_sum[:, t * T - 1:t * T], None, ALU.add).then_inc(sem("f_tile"), 1)
            dve.wait_ge(sem("f_tile"), NT)
            nc.vector.tensor_scalar(nf_sum[:], f_sum[:], -1.0, None, ALU.mult).then_inc(sem("f_ready"), 2)

            def take_v(b):
                dve.wait_ge(sem("v_turned"), b + 1)
                nc.vector.tensor_copy(v_tok[:, :, b * P:(b + 1) * P].rearrange("p (h t) c -> p h t c", h=2),
                                      tiles_of(ps[0:T, 4 + 2 * (b % 2):6 + 2 * (b % 2), 0:TH * P], P)
                                      ).then_inc(sem("v_tok"), 1)

            for b in range(FOX_BLOCKS):
                split_lo(dve, (U_V + b) // 2 + 1, b % 2)
                if b:
                    take_v(b - 1)
            take_v(FOX_BLOCKS - 1)
            dve.wait_ge(sem("tok_turned"), 1)
            nc.vector.tensor_copy(tok[:].rearrange("p (h t) r -> p h t r", h=2),
                                  tiles_of(ps[0:T, 4:6, 0:TH * R_END], R_END)).then_inc(sem("tok_ready"), 1)

            for n in range(N + 5):
                if n < N:
                    keys = (fox_items[n][1] + 1) * T
                    a = 2 * (n % 2)
                    dve.wait_ge(sem("scored"), n + 1)
                    if keys <= 512:
                        nc.vector.tensor_reduce(neg_max[:, n:n + 1], ps[0:T, a, 0:keys], AX.X, ALU.max,
                                                negate=True).then_inc(sem("neg_max"), 1)
                    else:
                        nc.vector.tensor_reduce(neg_max[:, n:n + 1], pair(n % 2, T), AX.XY, ALU.max,
                                                negate=True).then_inc(sem("neg_max"), 1)
                if 1 <= n <= N:
                    i = n - 1
                    keys = (fox_items[i][1] + 1) * T
                    dve.wait_ge(sem("prob_ready"), i + 1)
                    nc.vector.reciprocal(p_rec[:, i:i + 1], p_sum[:, i:i + 1]).then_inc(sem("p_rec"), 1)
                    dve.wait_ge(sem("p_rec"), i + 1)
                    nc.vector.tensor_scalar(prob[:, i % 3, 0:keys], prob[:, i % 3, 0:keys], p_rec[:, i:i + 1], None,
                                            ALU.mult).then_inc(sem("prob_scaled"), 1)
                if n >= 4 and (n - 4) % PAIR_ITEMS == PAIR_ITEMS - 1:
                    b = (n - 4) // PAIR_ITEMS
                    dve.wait_ge(sem("weighed"), (b + 1) * PAIR_ITEMS)
                    nc.vector.tensor_copy(halves(fox_o[:, b, :]), pair(3)).then_inc(sem("fox_taken"), 1)

            nc.vector.memset(conv_in[:, :, 0:GDN_TAPS - 1], 0.0).then_inc(sem("pads"), 1)
            dve.wait_ge(sem("pads"), 1)
            for half_no in range(2):
                p0 = (U_GDN + half_no * 3 * HH) // 2
                c0 = half_no * 3 * HH
                m0 = half_no * HH
                with dve.Fori(p0, p0 + 3 * HH // 2) as p:
                    for s in range(2):
                        n = p * 2 + (s - U_GDN)
                        split_lo(dve, p + 1, s)
                        dve.wait_ge(ACC_FREE[s], p + 1)
                        taps = [param("gdn_taps", n * GDN_TAPS + i) for i in range(GDN_TAPS)]
                        o = conv_out[:, s, :]
                        nc.vector.tensor_scalar(o, conv_in[:, s, GDN_TAPS - 1:], taps[-1], None, ALU.mult
                                                ).then_inc(sem("conv0"), 1)
                        for i in range(1, GDN_TAPS):
                            at = GDN_TAPS - 1 - i
                            dve.wait_ge(sem(f"conv{i - 1}"), n + 1)
                            nc.vector.scalar_tensor_tensor(o, conv_in[:, s, at:at + L], taps[at], o, ALU.mult,
                                                           ALU.add).then_inc(sem(f"conv{i}"), 1)
                for n in range(2 * HH):
                    r = conv_in[:, n % 2, GDN_TAPS - 1:]
                    dve.wait_ge(sem("gn_rooted"), 2 * m0 + n + 1)
                    nc.vector.reciprocal(r, r).then_inc(sem("gn_rec"), 1)
                    dve.wait_ge(sem("gn_rec"), 2 * m0 + n + 1)
                    nc.vector.tensor_tensor(qkv[:, n, :], qkv[:, n, :], r, ALU.mult).then_inc(sem("gn_normed"), 1)
                dve.wait_ge(sem("tok_ready"), 1)
                for j in range(HH):
                    m = m0 + j
                    dve.wait_ge(sem("gn_normed"), 2 * m0 + 2 * HH)
                    dve.wait_ge(sem("spread"), 2 * m + 2)
                    if j:
                        dve.wait_ge(sem("mats"), 2 * m)
                    nc.vector.tensor_tensor(halves(k_b[:]), pair(1), halves(qkv[:, HH + j, :]), ALU.mult
                                            ).then_inc(sem("k_b"), 1)
                    dve.wait_ge(sem("e_g"), 2 * m + 2)
                    for t in range(NT):
                        mm = nc.vector.tensor_scalar(decay[:, t, :], ps[0:T, t // TH, (t % TH) * T:(t % TH + 1) * T],
                                                     tok[:, t, m:m + 1], 0.0, ALU.subtract, ALU.min)
                    mm.then_inc(sem("decay_diff"), 1)
                    dve.wait_ge(sem("k_b"), m + 1)
                    nc.vector.tensor_tensor(k_bg[:, j, :], k_b[:], e_g[:], ALU.mult).then_inc(sem("k_bg"), 1)
                    dve.wait_ge(sem("decay_exp"), m + 1)
                    by_tile = lambda name: const(name, T).unsqueeze(1).broadcast_to([T, NT, T])
                    nc.vector.tensor_tensor(decay_s[:], decay[:], by_tile("strict"), ALU.mult
                                            ).then_inc(sem("decay_s"), 1)
                    nc.vector.tensor_tensor(decay[:], decay[:], by_tile("incl"), ALU.mult
                                            ).then_inc(sem("decay_i"), 1)
                    dve.wait_ge(sem("decay_s"), m + 1)
                    dve.wait_ge(sem("decay_i"), m + 1)
                    dve.wait_ge(sem("mats"), 2 * m + 2)
                    for which, (o, d) in enumerate(((a_t, decay), (m_t, decay_s))):
                        nc.vector.tensor_tensor(o[:, :, j, :].rearrange("p (h t) c -> p h t c", h=2),
                                                tiles_of(pair(2 + which, T), T),
                                                d[:].rearrange("p (h t) c -> p h t c", h=2), ALU.mult
                                                ).then_inc(sem("mat_taken"), 1)
                    nc.vector.tensor_tensor(qkv[:, j, :], qkv[:, j, :], e_g[:], ALU.mult).then_inc(sem("q_g"), 1)
                turned, updated = half_no * TURNS, half_no * UPDATES
                dve.wait_ge(sem("mat_taken"), 2 * (m0 + HH))
                for c in range(NT):
                    nc.vector.tensor_tensor(mx[:, c % 3, :, :], m_t[:, c, :, :], over_heads(const("pair", T)),
                                            ALU.mult).then_inc(sem("pair_m"), 1)
                    dve.wait_ge(sem("pair_m"), half_no * NT + c + 1)
                    nc.vector.tensor_tensor(inv_t[:, c, :, :], over_heads(const("ident", T, T)), mx[:, c % 3, :, :],
                                            ALU.subtract).then_inc(sem("inv_t"), 1)
                for lv in range(len(LEVELS)):
                    for step in range(NT + 2):
                        if step < NT:
                            n = lv * NT + step
                            dve.wait_ge(sem("mx_done"), turned + n + 1)
                            if n >= 3:
                                dve.wait_ge(sem("change"), turned + n - 2)
                            nc.vector.tensor_tensor(mx[:, n % 3, :, :],
                                                    ps[0:T, n % 3, 0:HH * T].rearrange("p (j t) -> p j t", j=HH),
                                                    over_heads(level_mask(lv)), ALU.mult).then_inc(sem("mx"), 1)
                        if step >= 2:
                            c, n = step - 2, lv * NT + step - 2
                            dve.wait_ge(sem("change"), turned + n + 1)
                            nc.vector.tensor_tensor(inv_t[:, c, :, :], inv_t[:, c, :, :],
                                                    ps[0:T, 3 + n % 3, 0:HH * T].rearrange("p (j t) -> p j t", j=HH),
                                                    ALU.subtract).then_inc(sem("inv_t"), 1)
                for j in range(HH):
                    for which, (o, row) in enumerate(((v_b, R_B), (k_d, R_G))):
                        dve.wait_ge(sem("vk_turned"), 2 * (m0 + j) + which + 1)
                        scale = tok[:, :, row + m0 + j:row + m0 + j + 1].broadcast_to([T, NT, DH])
                        nc.vector.tensor_tensor(o[:, :, j, :].rearrange("p (h t) c -> p h t c", h=2),
                                                tiles_of(ps[0:T, 4 + 2 * which:6 + 2 * which, 0:TH * DH], DH),
                                                scale.rearrange("p (h t) c -> p h t c", h=2), ALU.mult
                                                ).then_inc(sem("vk_taken"), 1)
                dve.wait_ge(sem("e_g"), 2 * (m0 + HH))
                dve.wait_ge(sem("vk_taken"), 2 * (m0 + HH))
                for c in range(NT):
                    if c:
                        dve.wait_ge(sem("ks_done"), half_no * (NT - 1) + c)
                        nc.vector.tensor_tensor(resid[:].rearrange("p j d -> p (j d)"),
                                                v_b[:, c, :, :].rearrange("p j d -> p (j d)"), ps[0:T, 0, :],
                                                ALU.subtract).then_inc(sem("resid"), 1)
                    if c < NT - 1:
                        dve.wait_ge(sem("grown"), half_no * (NT - 1) + c + 1)
                        if c:
                            dve.wait_ge(sem("state"), (half_no * (NT - 1) + c) * HH)
                        for j in range(HH):
                            new = state[:, (c + 1) % 2, j, :]
                            grown = ps[:, 2, j * DH:(j + 1) * DH]
                            if c:
                                nc.vector.scalar_tensor_tensor(new, state[:, c % 2, j, :], g_end[:, j, c:c + 1],
                                                               grown, ALU.mult, ALU.add).then_inc(sem("state"), 1)
                            else:
                                nc.vector.tensor_copy(new, grown).then_inc(sem("state"), 1)
                for j in range(HH):
                    m = m0 + j
                    r = conv_in[:, j % 2, GDN_TAPS - 1:]
                    dve.wait_ge(sem("on_rooted"), m + 1)
                    nc.vector.reciprocal(r, r).then_inc(sem("on_rec"), 1)
                    dve.wait_ge(sem("on_rec"), m + 1)
                    nc.vector.scalar_tensor_tensor(o_raw[:, m, :], o_raw[:, m, :], param("gdn_norm"), r, ALU.mult,
                                                   ALU.mult).then_inc(sem("o_normed"), 1)

            dve.wait_ge(sem("o_normed"), HEADS)
            dve.wait_ge(sem("fox_split"), 1)
            nc.vector.tensor_tensor(fox_lo[:], fox_o[:], fox_hi[:].bitcast(F32), ALU.subtract
                                    ).then_inc(sem("fox_split"), 1)
            with dve.Fori(U_Z // 2, (U_Z + HEADS) // 2) as p:
                for s in range(2):
                    n = p * 2 + (s - U_Z)
                    split_lo(dve, p + 1, s)
                    dve.wait_ge(ACC_FREE[s], p + 1)
                    nc.vector.tensor_tensor(zg[:, s, :], zg[:, s, :], flat(o_raw, n), ALU.mult
                                            ).then_inc(sem("gated"), 1)
                    dve.wait_ge(sem("ob_hi"), n + 1)
                    nc.vector.tensor_tensor(flat(ob_lo, n), zg[:, s, :], flat(ob_hi, n).bitcast(F32), ALU.subtract
                                            ).then_inc(sem("ob_lo"), 1)

            with dve.Fori(0, KD) as j:
                p = j * (MIX_UNITS // 2) + U_MIX // 2
                for s in range(2):
                    split_lo(dve, p + 1, s)
                for s, gate in enumerate((gate_b, gate_a)):
                    split_lo(dve, p + 2, s)
                    dve.wait_ge(ACC_FREE[1 - s], p + 1)
                    dve.wait_ge(UNIT_USED, p * 2 + (s + 3))
                    nc.vector.scalar_tensor_tensor(halves(gate[:]), halves(gate[:]), 1.0, pair(s), ALU.add, ALU.mult
                                                   ).then_inc(ACC_FREE[s], 1)
                for s in range(2):
                    dve.wait_ge(ACC_FREE[s], p + 2)
                nc.vector.tensor_tensor(gate_a[:], gate_a[:], gate_b[:], ALU.add).then_inc(sem("mixed"), 1)
                dve.wait_ge(sem("mix_hi"), j + 1)
                nc.vector.scalar_tensor_tensor(flat(mix_lo, j), gate_a[:], 0.5, flat(mix_hi, j).bitcast(F32),
                                               ALU.mult, ALU.subtract).then_inc(sem("mix_lo"), 1)

            dve.wait_ge(sem("x_reloaded"), 16)
            with dve.Fori(U_OUT // 2, (U_OUT + KD) // 2) as p:
                for s in range(2):
                    j = p * 2 + (s - U_OUT)
                    split_lo(dve, p + 1, s)
                    dve.wait_ge(UNIT_USED, p * 2 + (s + 1))
                    nc.vector.tensor_tensor(block_of(x_res, j), pair(s), block_of(x_res, j), ALU.add
                                            ).then_inc(ACC_FREE[s], 1)
            nc.vector.memset(ff_in[:, :, 0:FFN_TAPS - 1], 0.0).then_inc(sem("ff_pads"), 1)
            for s in range(2):
                dve.wait_ge(ACC_FREE[s], U_UP // 2)
            norm("n2", x_res, "norm2", ff_silu[:], ff_conv)

            dve.wait_ge(sem("ff_pads"), 1)
            dve.wait_ge(sem("n2_lo"), KD)

            def ff_conv_block(p, b, s, name, first):
                split_lo(dve, p + 1, s)
                dve.wait_ge(ACC_FREE[s], p + 1)
                taps = [param("ffn_taps", b * (2 * FFN_TAPS) + (s * FFN_TAPS + i)) for i in range(FFN_TAPS)]
                o = ff_conv[:, s, :]
                if s == 0 and not first:
                    dve.wait_ge(sem("ff_silu"), b)
                nc.vector.tensor_scalar(o, ff_in[:, s, FFN_TAPS - 1:], taps[-1], None, ALU.mult
                                        ).then_inc(sem(name), 1)
                for i in range(1, FFN_TAPS):
                    at = FFN_TAPS - 1 - i
                    dve.wait_ge(sem(name), b * FFN_TAPS + i)
                    nc.vector.scalar_tensor_tensor(o, ff_in[:, s, at:at + L], taps[at], o, ALU.mult, ALU.add
                                                   ).then_inc(sem(name), 1)

            def up_block(p, b, first):
                ff_conv_block(p, b, 0, "ff_g", first)
                ff_conv_block(p, b, 1, "ff_v", first)
                dve.wait_ge(sem("ff_silu"), b + 1)
                dve.wait_ge(sem("ff_v"), b * FFN_TAPS + FFN_TAPS)
                nc.vector.tensor_tensor(ff_u[:, 0, :], ff_silu[:], ff_conv[:, 1, :], ALU.mult
                                        ).then_inc(sem("ff_u"), 1)
                dve.wait_ge(sem("u_hi"), b + 1)
                nc.vector.tensor_tensor(flat(u_lo, b), ff_u[:, 0, :], flat(u_hi, b).bitcast(F32), ALU.subtract
                                        ).then_inc(sem("u_lo"), 1)

            up_block(U_UP // 2, 0, True)
            with dve.Fori(1, FF_BLOCKS) as b:
                up_block(b + U_UP // 2, b, False)

            def down_block(q, s, first, last):
                for part in range(DOWN_UNITS):
                    n = s * DOWN_UNITS + part
                    if not (last and n + 2 >= 2 * DOWN_UNITS):
                        split_lo(dve, q * DOWN_UNITS + (U_DOWN // 2 + n // 2 + 1), n % 2)
                dve.wait_ge(UNIT_USED, q * 2 * DOWN_UNITS + (U_DOWN + (s + 1) * DOWN_UNITS))
                if not first:
                    dve.wait_ge(sem(f"stored{s}"), q * 16)
                nc.vector.tensor_tensor(halves(y_out[:, s, :]), pair(s), block_of(x_res, q * 2 + s), ALU.add
                                        ).then_inc(sem("y_ready"), 1)
                dve.wait_ge(sem("y_ready"), q * 2 + (s + 1))
                nc.vector.sem_inc(ACC_FREE[s], 1)

            for s in range(2):
                down_block(0, s, True, False)
            with dve.Fori(1, KD // 2 - 1) as q:
                for s in range(2):
                    down_block(q, s, False, False)
            for s in range(2):
                down_block(KD // 2 - 1, s, False, True)


def constants():
    c = np.zeros((P, C_COLS), np.float32)

    def put(name, value):
        c[:value.shape[0], CONST[name]:CONST[name] + value.shape[1]] = value

    r, k = np.arange(T)[:, None], np.arange(T)[None, :]
    put("ident", np.eye(P, dtype=np.float32))
    put("ones", np.ones((P, P), np.float32))
    put("ones64", np.kron(np.eye(2), np.ones((FOX_DIM, FOX_DIM))).astype(np.float32))
    put("incl", (r <= k).astype(np.float32))
    put("strict", (r < k).astype(np.float32))
    put("pair", ((k % 2 == 1) & (r == k - 1)).astype(np.float32))
    put("neg", np.where(k > r, np.float32(-1e30), np.float32(0)))
    put("levels", np.concatenate([((r // n % 2 == 1) & (k // n == r // n - 1)) for n in LEVELS], 1
                                 ).astype(np.float32))
    for h in range(HEADS):
        for base in (0, R_B):
            c[base + h, CONST["sel"] + h * P:CONST["sel"] + (h + 1) * P] = 1
    return c


def lay_out(inputs):
    a = {k: np.asarray(v) for k, v in inputs.items()}
    tokens = np.concatenate([a["meta_tokens"], a["x"][0]])
    x_t = np.ascontiguousarray(tokens.T.reshape(KD, P, L).transpose(1, 0, 2))
    w_in = a["w_in"][0]
    fox_w, gdn_w = FOX_HEADS * FOX_DIM, HEADS * DH
    o_f = 3 * fox_w
    o_g = o_f + FOX_HEADS
    o_b = o_g + 3 * gdn_w
    o_z = o_b + 2 * HEADS
    o_gate = o_z + gdn_w

    def rows(w):
        return w.reshape(-1, P, w.shape[1]).transpose(1, 0, 2)

    def unit(w):
        u = np.zeros((P, UNIT), w.dtype)
        u[:, :w.shape[0]] = rows(w).reshape(P, -1)
        return u

    small = np.zeros((D, R_END), w_in.dtype)
    small[:, R_F:R_F + HEADS] = w_in[:, o_f:o_f + HEADS]
    small[:, R_B:R_B + HEADS] = w_in[:, o_b:o_b + HEADS]
    small[:, R_G:R_G + HEADS] = w_in[:, o_b + HEADS:o_z]

    units = [w_in[:, b * P:(b + 1) * P] for b in range(3 * FOX_BLOCKS)]
    gdn_cols = [which * gdn_w + (half * HH + j) * DH for half in range(2) for which in range(3) for j in range(HH)]
    units += [w_in[:, o_g + c:o_g + c + P] for c in gdn_cols]
    units += [w_in[:, o_z + j * P:o_z + (j + 1) * P] for j in range(HEADS)]
    for j in range(KD):
        at = slice(j * P, (j + 1) * P)
        units += [w_in[:, o_gate:o_gate + D][:, at], w_in[:, o_gate + D:][:, at],
                  a["w_branch_b"][0][:, at], a["w_branch_a"][0][:, at]]
    units += [a["w_out"][0][:, j * P:(j + 1) * P] for j in range(KD)]
    for b in range(FF_BLOCKS):
        for s in range(2):
            units.append(a["w_up"][0][:, s * D_FF + b * P:s * D_FF + (b + 1) * P])
    for j in range(KD):
        for part in range(DOWN_UNITS):
            units.append(a["w_down"][0][part * D:(part + 1) * D, j * P:(j + 1) * P])
    w_units = np.stack([unit(u) for u in units])

    prm = np.zeros((P, P_COLS), np.float32)

    def put(name, value, i=0, rows_at=0):
        prm[rows_at:rows_at + value.shape[0], PARAM[name] + i:PARAM[name] + i + value.shape[1]] = value

    put("norm1", a["norm1_g"][0].reshape(KD, P).T)
    put("norm2", a["norm2_g"][0].reshape(KD, P).T)
    put("gdn_norm", a["gdn_norm_g"][0][:, None])
    put("stat_bias", a["fox_f_bias"][0][:, None], rows_at=R_F)
    put("stat_bias", a["gdn_dt_bias"][0][:, None], rows_at=R_G)
    for at, sign in ((R_F, -1), (R_B, -1), (R_G, 1)):
        put("stat_sign", np.full((HEADS, 1), sign, np.float32), rows_at=at)
    put("a_log", a["gdn_a_log"][0][:, None], rows_at=R_G)
    put("eps", np.full((P, 1), EPS, np.float32))
    put("eps_dh", np.full((P, 1), EPS * DH, np.float32))
    for b in range(2 * FOX_BLOCKS):
        is_q = b < FOX_BLOCKS
        gain = a["fox_q_norm_g" if is_q else "fox_k_norm_g"][0]
        put("qk", np.concatenate([gain, gain])[:, None], 3 * b)
        put("qk", np.full((P, 1), 1.0 if is_q else 1.0 / FOX_DIM, np.float32), 3 * b + 1)
        put("qk", np.full((P, 1), EPS * FOX_DIM if is_q else EPS, np.float32), 3 * b + 2)
    for n, c in enumerate(gdn_cols):
        put("gdn_taps", a["gdn_conv_w"][0][:, c:c + P].T, GDN_TAPS * n)
    for b in range(FF_BLOCKS):
        for s in range(2):
            c = s * D_FF + b * P
            put("ffn_taps", a["ffn_conv_w"][0][:, c:c + P].T, FFN_TAPS * (2 * b + s))
    return {"x_t": x_t, "w_small": np.ascontiguousarray(rows(small)), "w_units": w_units, "params": prm,
            "consts": constants()}


def kernel(**inputs):
    import concourse.bacc as bacc
    from concourse.bass_utils import run_bass_kernel_spmd

    nc = bacc.Bacc("TRN2", target_bir_lowering=False, num_devices=1)
    arrays = {f"in_{k}": v for k, v in lay_out(inputs).items()}
    args = [nc.dram_tensor(k, v.shape, mybir.dt.from_np(v.dtype), kind="ExternalInput").ap()
            for k, v in arrays.items()]
    out = nc.dram_tensor("out_y", (KD, P, SEQ), F32, kind="ExternalOutput").ap()
    build_trunk(nc, *args, out)
    r = run_bass_kernel_spmd(nc, [arrays], core_ids=[0])
    return np.ascontiguousarray(r.results[0]["out_y"].reshape(1, D, SEQ).transpose(0, 2, 1))
```

```python
from contextlib import ExitStack

import numpy as np

import concourse.bass as bass
import concourse.mybir as mybir

F32 = mybir.dt.float32
F32R = mybir.dt.float32r
ACT = mybir.ActivationFunctionType
ALU = mybir.AluOpType
AX = mybir.AxisListType

P = 128
D = 1024
SEQ = 512
N_META = 16
L = SEQ + N_META
HL = L // 2
T = 88
NT = L // T
TH = NT // 2
KD = D // P
EPS = 1e-6
FOX_HEADS, FOX_DIM = 8, 64
FOX_BLOCKS = FOX_HEADS * FOX_DIM // P
HEADS, DH = 8, 128
HH = HEADS // 2
D_FF = 2816
FF_BLOCKS = D_FF // P
GDN_TAPS, FFN_TAPS = 4, 3
X_PARTS = 4
UNIT = KD * P

U_QK = 0
U_V = U_QK + 2 * FOX_BLOCKS
U_GDN = U_V + FOX_BLOCKS
U_Z = U_GDN + 3 * HEADS
U_MIX = U_Z + HEADS
MIX_UNITS = 4
U_OUT = U_MIX + MIX_UNITS * KD
U_UP = U_OUT + KD
U_DOWN = U_UP + 2 * FF_BLOCKS
DOWN_UNITS = 3
N_UNITS = U_DOWN + DOWN_UNITS * KD

R_F, R_B, R_G, R_END = 0, 32, 64, 96
R_GRP = 32
R_BE, S_END = 96, 128
LEVELS = [2, 4, 8, 16, 32, 64]


def side_by_side(widths):
    at, out = 0, {}
    for name, w in widths:
        out[name] = at
        at += w
    return out, at


CONST, C_COLS = side_by_side([("ident", P), ("ones", P), ("row_of", 2 * R_GRP), ("row_of64", 2 * R_GRP),
                              ("incl", T), ("pair", T), ("neg", T), ("levels", len(LEVELS) * T)])
PARAM, P_COLS = side_by_side([("norm1", KD), ("norm2", KD), ("gdn_norm", 1), ("stat_bias", 1), ("stat_sign", 1),
                              ("a_log", 1), ("eps", 1), ("gn_scale", 1), ("gn_bias", 1),
                              ("qk_scale", 1), ("qk_bias", 1), ("qk", 2 * FOX_BLOCKS),
                              ("gdn_taps", GDN_TAPS * 3 * HEADS), ("ffn_taps", FFN_TAPS * 2 * FF_BLOCKS)])


def build_trunk(nc, x_t, w_small, w_units, params, consts, selects, out_t):
    ctx = ExitStack()
    with ctx:
        def sb(scope, name, shape, dt=F32):
            return scope.enter_context(nc.sbuf_tensor(name, shape, dt))

        sems = {}

        def sem(name):
            if name not in sems:
                sems[name] = ctx.enter_context(nc.semaphore(name))
            return sems[name]

        cst = sb(ctx, "cst", [P, C_COLS])
        prm = sb(ctx, "prm", [P, P_COLS])
        w_raw = sb(ctx, "w_raw", [P, 2, UNIT])
        w_hi = sb(ctx, "w_hi", [P, 2, UNIT], F32R)
        w_lo = sb(ctx, "w_lo", [P, 2, UNIT], F32R)
        h_hi = sb(ctx, "h_hi", [P, KD, L], F32R)
        h_lo = sb(ctx, "h_lo", [P, KD, L], F32R)
        sel_r = sb(ctx, "sel_r", [P, HEADS, P], F32R)
        with ExitStack() as mixing:
            fox_o = sb(mixing, "fox_o", [P, FOX_BLOCKS, L])
            o_raw = sb(mixing, "o_raw", [P, HEADS, L])
            tok = sb(mixing, "tok", [T, NT, S_END])
            g_hl = sb(mixing, "g_hl", [2 * R_GRP, L], F32R)
            b_hl = sb(mixing, "b_hl", [2 * R_GRP, L], F32R)
            with ExitStack() as first_half:
                qkv0 = sb(first_half, "qkv0", [P, 3 * HH, L])
                conv_in = sb(first_half, "conv_in", [P, GDN_TAPS - 1 + L])
                conv_out = sb(first_half, "conv_out", [P, L])
                tanh_out = sb(first_half, "tanh_out", [P, L])
                with ExitStack() as fox:
                    st = [sb(fox, f"st{i}", [R_END, L]) for i in range(4)]
                    stat = sb(fox, "stat", [S_END, L])
                    f_sum = sb(fox, "f_sum", [R_GRP, L])
                    nf_sum = sb(fox, "nf_sum", [R_GRP, L])
                    nf_hl = sb(fox, "nf_hl", [P, L], F32R)
                    coef = sb(fox, "coef", [R_END, 2])
                    sel_qk = sb(fox, "sel_qk", [2 * R_GRP, 2 * FOX_BLOCKS, P], F32R)
                    ident_r = sb(fox, "ident_r", [T, T], F32R)
                    neg_r = sb(fox, "neg_r", [T, T], F32R)
                    with ExitStack() as early:
                        x_in = sb(early, "x_in", [P, KD, L])
                        sq = sb(early, "sq", [P, 2, L])
                        root1 = sb(early, "root1", [P, L])
                        h32 = sb(early, "h32", [P, 2, L])
                        small_raw = sb(early, "small_raw", [P, KD, R_END])
                        small_hi = sb(early, "small_hi", [P, KD, R_END], F32R)
                        small_lo = sb(early, "small_lo", [P, KD, R_END], F32R)
                        sel_raw = sb(early, "sel_raw", [P, 2, 8 * P])
                    qk = sb(fox, "qk", [P, 2 * FOX_BLOCKS, L])
                    v_tok = sb(fox, "v_tok", [T, NT, FOX_HEADS * FOX_DIM])
                    v_chan = sb(fox, "v_chan", [P, 2, L])
                    qk_sq = sb(fox, "qk_sq", [P, 2, L])
                    qk_root = sb(fox, "qk_root", [R_GRP, L])
                    qk_hl = sb(fox, "qk_hl", [2 * R_GRP, L], F32R)
                    prob = sb(fox, "prob", [T, 3, L])
                    prob_t = sb(fox, "prob_t", [T, 2, L])
                    neg_max = sb(fox, "neg_max", [T, NT * FOX_HEADS])
                    p_sum = sb(fox, "p_sum", [T, NT * FOX_HEADS])
                    p_rec = sb(fox, "p_rec", [T, NT * FOX_HEADS])
                qkv1 = sb(first_half, "qkv1", [P, 3 * HH, L])
                work = sb(first_half, "work", [P, 2, L])
                n_root = sb(first_half, "n_root", [R_GRP, L])
                n_hl = sb(first_half, "n_hl", [2 * R_GRP, L], F32R)
                g_end = sb(first_half, "g_end", [P, HH, NT])
                a_t = sb(first_half, "a_t", [T, NT, HH, T])
                inv_t = sb(first_half, "inv_t", [T, NT, HH, T])
                with ExitStack() as inverse:
                    decay = sb(inverse, "decay", [T, NT, T])
                    m_t = sb(inverse, "m_t", [T, NT, HH, T])
                    inv = sb(inverse, "inv", [T, NT, HH, T])
                    mx = sb(inverse, "mx", [T, 3, HH, T])
                v_b = sb(first_half, "v_b", [T, 2, HH, DH])
                k_d = sb(first_half, "k_d", [T, 2, HH, DH])
                state = sb(first_half, "state", [P, 2, HH, DH])
                resid = sb(first_half, "resid", [T, HH, DH])
                u_new = sb(first_half, "u_new", [T, HH, DH])
            z = sb(mixing, "z", [P, HEADS, L])
            fox_hi = sb(mixing, "fox_hi", [P, FOX_BLOCKS, L], F32R)
            fox_lo = sb(mixing, "fox_lo", [P, FOX_BLOCKS, L], F32R)
            ob_hi = sb(mixing, "ob_hi", [P, HEADS, L], F32R)
            ob_lo = sb(mixing, "ob_lo", [P, HEADS, L], F32R)
            mix_hi = sb(mixing, "mix_hi", [P, KD, L], F32R)
            mix_lo = sb(mixing, "mix_lo", [P, KD, L], F32R)
            zg = sb(mixing, "zg", [P, 2, L])
            gate_a = sb(mixing, "gate_a", [P, L])
            gate_b = sb(mixing, "gate_b", [P, L])
        x_res = sb(ctx, "x_res", [P, KD, L])
        u_hi = sb(ctx, "u_hi", [P, FF_BLOCKS, L], F32R)
        u_lo = sb(ctx, "u_lo", [P, FF_BLOCKS, L], F32R)
        ff_in = sb(ctx, "ff_in", [P, 2, FFN_TAPS - 1 + L])
        ff_conv = sb(ctx, "ff_conv", [P, 2, L])
        ff_silu = sb(ctx, "ff_silu", [P, L])
        ff_u = sb(ctx, "ff_u", [P, 2, L])
        y_out = sb(ctx, "y_out", [P, 2, L])
        ps = ctx.enter_context(nc.psum_tensor("ps", [P, 8, 512], F32))

        def const(name, rows=P, cols=None, base=0):
            at = CONST[name]
            width = cols if cols else {"incl": T, "pair": T, "neg": T}.get(name, P)
            return cst[base:base + rows, at:at + width]

        def param(name, i=0, rows=P):
            return prm[0:rows, bass.ds(i + PARAM[name], 1)]

        def pair(a, rows=P):
            return ps[0:rows, 2 * a:2 * a + 2, 0:HL]

        def halves(ap):
            return ap.rearrange("p (h n) -> p h n", h=2)

        def tiles_of(ap, w):
            return ap.rearrange("p h (t c) -> p h t c", c=w)

        def block_of(buf, i):
            return buf[:, bass.ds(i, 1), :].rearrange("p o (h n) -> p (o h) n", h=2)

        def flat(buf, i):
            return buf[:, bass.ds(i, 1), :].rearrange("p o n -> p (o n)")

        def over_heads(ap):
            return ap.unsqueeze(1).broadcast_to([T, HH, T])

        def level_mask(n):
            at = CONST["levels"] + n * T
            return cst[0:T, at:at + T]

        def row_of(n, name="row_of", width=1):
            at = CONST[name] + R_GRP - 1 - n * width
            return cst[:, at:at + R_GRP]

        W_LOADED = [sem("w_loaded0"), sem("w_loaded1")]
        HI_READY, LO_READY = sem("hi_ready"), sem("lo_ready")
        UNIT_USED = sem("unit_used")
        ACC_FREE = [sem("acc_free0"), sem("acc_free1")]

        def split_hi(act, p, s, first=False):
            act.wait_ge(W_LOADED[s], p * 16 + 16)
            if not first:
                act.wait_ge(UNIT_USED, p * 2 + (s - 1))
            nc.scalar.copy(w_hi[:, s, :], w_raw[:, s, :]).then_inc(HI_READY, 1)

        def split_lo(dve, p, s):
            dve.wait_ge(HI_READY, p * 2 + (s + 1))
            nc.vector.tensor_tensor(w_lo[:, s, :], w_raw[:, s, :], w_hi[:, s, :].bitcast(F32),
                                    ALU.subtract).then_inc(LO_READY, 1)

        def products(acc, s, hi, lo, tiles, start, stop, at=0):
            for k in range(tiles):
                for n, (w, x) in enumerate(((w_hi, hi), (w_hi, lo), (w_lo, hi))):
                    for half in range(2):
                        mm = nc.tensor.matmul(
                            ps[:, 2 * acc + half, 0:HL], w[:, s, k * P:(k + 1) * P],
                            x[:, at + k, half * HL:(half + 1) * HL],
                            start=start and k == 0 and n == 0, stop=stop and k == tiles - 1 and n == 2)
            return mm

        def sums(stationary, buf, s, bank):
            for half in range(2):
                mm = nc.tensor.matmul(ps[:, bank + half, 0:HL], stationary, buf[:, s, half * HL:(half + 1) * HL],
                                      start=True, stop=True)
            return mm

        def spread(bank, select, rows):
            for half in range(2):
                mm = nc.tensor.matmul(ps[:, bank + half, 0:HL], select, rows[:, half * HL:(half + 1) * HL],
                                      start=True, stop=True)
            return mm

        def weave(first, count, quarter):
            calls = [0]

            def fill(times=1):
                for _ in range(times):
                    b, q = divmod(calls[0], 4)
                    if calls[0] < 4 * count + 5:
                        quarter(first + b, q, b < count, 1 <= b <= count, 2 <= b)
                        calls[0] += 1

            def finish():
                fill(4 * count + 5 - calls[0])

            return fill, finish

        def woven_target(u):
            if u >= U_Z:
                return z[:, u - U_Z, :]
            return (qkv0 if u < U_GDN + 3 * HH else qkv1)[:, (u - U_GDN) % (3 * HH), :]

        GDN_FILLS = [dict(sums=4, norm_wait=5, spread=2, head=3, level=1, chunk=2, out_wait=6),
                     dict(sums=2, norm_wait=4, spread=0, head=2, level=1, chunk=1, out_wait=6)]
        GDN_WEAVES = [(U_GDN + 3 * HH, 3 * HH), (U_Z, HEADS)]
        n_scan = (T - 1).bit_length()
        st_sum, to_end = st[1 + n_scan % 2], st[2 - n_scan % 2]
        QK_ORDER = [b + which * FOX_BLOCKS for b in range(FOX_BLOCKS) for which in range(2)]

        fox_items = [(h, t) for h in range(FOX_HEADS) for t in range(NT)]
        N = len(fox_items)
        PAIR_ITEMS = 2 * NT
        TURNS = NT * len(LEVELS)
        UPDATES = NT * (len(LEVELS) + 1)
        STEPS = NT - 1

        block = ctx.enter_context(nc.Block())

        @block.sync
        def _(sp):
            def load_unit(u, s):
                sp.dma_start(w_raw[:, s, :], w_units[bass.ds(u, 1)].rearrange("o p n -> p (o n)")
                             ).then_inc(W_LOADED[s], 16)

            for i in range(X_PARTS):
                at = slice(i * KD // X_PARTS, (i + 1) * KD // X_PARTS)
                sp.dma_start(x_in[:, at, :], x_t[:, at, :]).then_inc(sem(f"x_loaded{i}"), 16)
            sp.dma_start(small_raw[:], w_small).then_inc(sem("small_loaded"), 16)
            for s in range(2):
                load_unit(s, s)
            with sp.Fori(1, N_UNITS // 2) as p:
                for s in range(2):
                    sp.wait_ge(LO_READY, p * 2 + (s - 1))
                    load_unit(p * 2 + s, s)

        @block.gpsimd
        def _(pool):
            pool.dma_start(cst[:], consts).then_inc(sem("const_loaded"), 16)
            pool.dma_start(prm[:], params).then_inc(sem("params_loaded"), 16)
            pool.wait_ge(sem("small_loaded"), 16)
            pool.dma_start(sel_raw[:], selects).then_inc(sem("selects_loaded"), 16)
            pool.wait_ge(sem("gated"), HEADS)
            pool.wait_ge(sem("fox_split"), 2)
            pool.dma_start(x_res[:], x_t).then_inc(sem("x_reloaded"), 16)
            for j in range(KD):
                pool.wait_ge(sem("y_ready"), j + 1)
                pool.dma_start(out_t[j], y_out[:, j % 2, N_META:L]).then_inc(sem(f"stored{j % 2}"), 16)
            for s in range(2):
                pool.wait_ge(sem(f"stored{s}"), 16 * KD // 2)

        @block.tensor
        def _(pe):
            def norm_sums(tag, buf):
                for k in range(KD):
                    pe.wait_ge(sem(tag + "_sq"), k + 1)
                    for half in range(2):
                        mm = nc.tensor.matmul(ps[:, 4 + half, 0:HL], const("ones"),
                                              buf[:, k % 2, half * HL:(half + 1) * HL],
                                              start=(k == 0), stop=(k == KD - 1))
                    mm.then_inc(sem(tag + "_sq_used"), 1)

            def dense_unit(p, s, hi, lo, slot_tiles=KD):
                pe.wait_ge(LO_READY, p * 2 + (s + 1))
                if not (isinstance(p, int) and p == 0):
                    pe.wait_ge(ACC_FREE[s], p)
                products(s, s, hi, lo, slot_tiles, True, True).then_inc(UNIT_USED, 1)

            def dense_loop(first, count, hi, lo):
                with pe.Fori(first // 2, (first + count) // 2) as p:
                    for s in range(2):
                        dense_unit(p, s, hi, lo)

            pe.wait_ge(sem("const_loaded"), 16)
            norm_sums("n1", sq)
            def stat_logits(k):
                for n, (w, x) in enumerate(((small_hi, h_hi), (small_hi, h_lo), (small_lo, h_hi))):
                    for half in range(2):
                        mm = nc.tensor.matmul(ps[0:R_END, 6 + half, 0:HL], w[:, k, :],
                                              x[:, k, half * HL:(half + 1) * HL],
                                              start=(k == 0 and n == 0), stop=(k == KD - 1 and n == 2))
                if k == KD - 1:
                    mm.then_inc(sem("small_done"), 1)

            def rising_pair(p, name, beside=None):
                for s in range(2):
                    pe.wait_ge(LO_READY, p * 2 + s + 1)
                    if p:
                        pe.wait_ge(ACC_FREE[s], p)
                for k in range(KD):
                    pe.wait_ge(sem(name), k + 1)
                    if beside:
                        beside(k)
                    for s in range(2):
                        for n, (w, x) in enumerate(((w_hi, h_hi), (w_hi, h_lo), (w_lo, h_hi))):
                            for half in range(2):
                                mm = nc.tensor.matmul(ps[:, 2 * s + half, 0:HL], w[:, s, k * P:(k + 1) * P],
                                                      x[:, k, half * HL:(half + 1) * HL],
                                                      start=(k == 0 and n == 0), stop=(k == KD - 1 and n == 2))
                        if k == KD - 1:
                            mm.then_inc(UNIT_USED, 1)

            pe.wait_ge(sem("small_lo"), 1)
            rising_pair(0, "n1_lo", stat_logits)

            def quarter(u, q, multiplies, takes, finishes):
                if not multiplies:
                    return
                if q == 0:
                    pe.wait_ge(LO_READY, u + 1)
                    pe.wait_ge(ACC_FREE[(u - 1) % 2], (u + 1) // 2)
                for k in range(q * KD // 4, (q + 1) * KD // 4):
                    for n, (w, x) in enumerate(((w_hi, h_hi), (w_hi, h_lo), (w_lo, h_hi))):
                        for half in range(2):
                            mm = nc.tensor.matmul(ps[:, half, 0:HL], w[:, u % 2, k * P:(k + 1) * P],
                                                  x[:, k, half * HL:(half + 1) * HL],
                                                  start=(k == 0 and n == 0), stop=(k == KD - 1 and n == 2))
                if q == 3:
                    mm.then_inc(UNIT_USED, 1)

            def row_sums(stationary, buf, s, first, last):
                for half in range(2):
                    mm = nc.tensor.matmul(ps[0:R_GRP, 2 + half, 0:HL], stationary,
                                          buf[:, s, half * HL:(half + 1) * HL], start=first, stop=last)
                return mm

            def qk_sums(n):
                pe.wait_ge(sem("qk_sq"), n + 1)
                for half in range(2):
                    mm = nc.tensor.matmul(ps[0:R_GRP, 4 + half, 0:HL], row_of(n, "row_of64", 2),
                                          qk_sq[:, n % 2, half * HL:(half + 1) * HL],
                                          start=(n == 0), stop=(n == 2 * FOX_BLOCKS - 1))
                mm.then_inc(sem("qk_sum"), 1)

            qk_sums(0)
            for n in range(2, 2 * FOX_BLOCKS):
                dense_unit(n // 2, n % 2, h_hi, h_lo)
                qk_sums(n - 1)

            pe.wait_ge(sem("stat_in"), 1)

            def turn_v(b):
                pe.wait_ge(ACC_FREE[b % 2], (U_V + b) // 2 + 1)
                if b:
                    pe.wait_ge(sem("v_tok"), b)
                for t in range(NT):
                    mm = nc.tensor.transpose(ps[0:T, 6 + t // TH, (t % TH) * P:(t % TH + 1) * P],
                                             v_chan[:, b % 2, t * T:(t + 1) * T], const("ident"))
                mm.then_inc(sem("v_turned"), 1)

            for b in range(FOX_BLOCKS):
                dense_unit((U_V + b) // 2, b % 2, h_hi, h_lo)
                if b:
                    turn_v(b - 1)
                else:
                    qk_sums(2 * FOX_BLOCKS - 1)
            fill, finish = weave(U_GDN, 3 * HH, quarter)
            fill()
            turn_v(FOX_BLOCKS - 1)
            fill()

            pe.wait_ge(sem("qk_rooted"), 1)
            pe.wait_ge(sem("stat_rows"), 4)
            for t in range(NT):
                mm = nc.tensor.transpose(ps[0:T, 4 + t // TH, (t % TH) * S_END:(t % TH + 1) * S_END],
                                         stat[:, t * T:(t + 1) * T], const("ident"))
            mm.then_inc(sem("tok_turned"), 1)
            pe.wait_ge(sem("v_tok"), FOX_BLOCKS)
            pe.wait_ge(sem("qk_split"), 2)
            for i, n in enumerate(QK_ORDER):
                if i == 1:
                    pe.wait_ge(sem("tok_ready"), 1)
                if i >= 2:
                    pe.wait_ge(sem("qk_normed"), i - 1)
                spread(6 - 2 * (i % 2), sel_qk[:, n, :], qk_hl).then_inc(sem("qk_spread"), 1)
                if i % 4 != 3:
                    fill()

            pe.wait_ge(sem("qk_normed"), 2 * FOX_BLOCKS)
            pe.wait_ge(sem("nf_split"), 2)
            pe.wait_ge(sem("masks_r"), 3)
            pe.wait_ge(ACC_FREE[1], U_GDN // 2)

            def scores(n):
                h, t = fox_items[n]
                rows = slice(FOX_DIM * (h % 2), FOX_DIM * (h % 2) + FOX_DIM)
                keys = (t + 1) * T
                wide = keys > 512
                if n:
                    before = n if wide or t == 0 else n - 1
                    if before:
                        pe.wait_ge(sem("prob_ready"), before)
                at = slice(t * T, (t + 1) * T)
                for bank, k0, k1 in [(2, 0, HL), (3, HL, L)] if wide else [(2 + t % 2, 0, keys)]:
                    o = ps[0:T, bank, 0:k1 - k0]
                    last = k1 == keys
                    nc.tensor.matmul(o, qk[rows, h // 2, at], qk[rows, FOX_BLOCKS + h // 2, k0:k1],
                                     start=True, stop=False)
                    mm = nc.tensor.matmul(o, sel_r[:, h, 0:T], nf_hl[:, k0:k1], start=False, stop=not last)
                    if last:
                        mm = nc.tensor.matmul(ps[0:T, bank, k1 - k0 - T:k1 - k0], ident_r[:], neg_r[:],
                                              start=False, stop=True)
                mm.then_inc(sem("scored"), 1)

            def turn_probs(n):
                t = fox_items[n][1]
                pe.wait_ge(sem("prob_scaled"), n + 1)
                if n >= 1:
                    pe.wait_ge(sem("prob_t"), n)
                for j in range(t + 1):
                    mm = nc.tensor.transpose(ps[0:T, 4 + j // TH, (j % TH) * T:(j % TH + 1) * T],
                                             prob[:, n % 3, j * T:(j + 1) * T], const("ident", T, T))
                mm.then_inc(sem("prob_turned"), 1)

            def weigh_values(n):
                h, t = fox_items[n]
                pe.wait_ge(sem("prob_t"), n + 1)
                if n % PAIR_ITEMS == 0 and n:
                    pe.wait_ge(sem("fox_taken"), n // PAIR_ITEMS)
                r0 = FOX_DIM * (h % 2)
                o = ps[r0:r0 + FOX_DIM, 6 + t // TH, (t % TH) * T:(t % TH + 1) * T]
                for j in range(t + 1):
                    mm = nc.tensor.matmul(o, v_tok[:, j, h * FOX_DIM:(h + 1) * FOX_DIM],
                                          prob_t[:, n % 2, j * T:(j + 1) * T], start=(j == 0), stop=(j == t))
                mm.then_inc(sem("weighed"), 1)

            for n in range(N + 3):
                if n < N:
                    scores(n)
                fill()
                if 0 <= n - 2 < N:
                    turn_probs(n - 2)
                if 0 <= n - 3 < N:
                    weigh_values(n - 3)
            finish()
            pe.wait_ge(sem("prob_ready"), N)
            pe.wait_ge(sem("fox_taken"), FOX_BLOCKS)

            for half_no, qkv in enumerate((qkv0, qkv1)):
                m0 = half_no * HH
                plan = GDN_FILLS[half_no]
                fill, finish = weave(*GDN_WEAVES[half_no], quarter)
                for n in range(2 * HH):
                    pe.wait_ge(sem("gn_sq"), 2 * m0 + n + 1)
                    row_sums(row_of(n), work, n % 2, n == 0, n == 2 * HH - 1).then_inc(sem("gn_sum"), 1)
                    if n % (2 * HH // plan["sums"]) == 0:
                        fill()
                fill(plan["norm_wait"])
                pe.wait_ge(sem("gn_split"), 2 * half_no + 2)
                for n in range(2 * HH):
                    if n >= 2:
                        pe.wait_ge(sem("gn_normed"), 2 * m0 + n - 1)
                    spread(4 + 2 * (n % 2), sel_r[0:2 * R_GRP, n, :], n_hl).then_inc(sem("gn_spread"), 1)
                    if n in (2, 5) and plan["spread"]:
                        fill()
                pe.wait_ge(sem("gn_normed"), 2 * m0 + 2 * HH)
                for j in range(HH):
                    m = m0 + j
                    if j:
                        pe.wait_ge(sem("e_g"), 2 * m)
                        pe.wait_ge(sem("decay_diff"), m)
                    spread(2, sel_r[0:2 * R_GRP, m, :], g_hl).then_inc(sem("spread"), 1)
                    if j:
                        pe.wait_ge(sem("mat_taken"), 2 * m)
                    spread(4, sel_r[0:2 * R_GRP, m, :], b_hl).then_inc(sem("spread"), 1)
                    fill()
                    pe.wait_ge(sem("k_b"), m + 1)
                    for which in range(2):
                        for t in range(NT):
                            at = slice(t * T, (t + 1) * T)
                            mm = nc.tensor.matmul(
                                ps[0:T, 6 - 2 * which + t // TH, (t % TH) * T:(t % TH + 1) * T],
                                qkv[:, HH + j, at], work[:, 0, at] if which else qkv[:, j, at],
                                start=True, stop=True)
                        mm.then_inc(sem("mats"), 1)
                    fill(plan["head"] - 1)

                def turn_inv(c, bank):
                    for j in range(HH):
                        mm = nc.tensor.transpose(ps[0:T, bank, j * T:(j + 1) * T], inv_t[:, c, j, :],
                                                 const("ident", T, T))
                    mm.then_inc(sem("inv_turned"), 1)

                turned, updated = half_no * TURNS, half_no * UPDATES
                pe.wait_ge(sem("mat_taken"), 2 * (m0 + HH))
                pe.wait_ge(sem("e_g"), 2 * (m0 + HH))
                pe.wait_ge(sem("decay_diff"), m0 + HH)
                for c in range(NT):
                    pe.wait_ge(sem("inv_t"), updated + c + 1)
                    if c >= 2:
                        pe.wait_ge(sem("inv"), turned + c - 1)
                    turn_inv(c, 6 + c % 2)
                for lv in range(len(LEVELS)):
                    for step in range(NT + 4):
                        if step < NT:
                            c, n = step, lv * NT + step
                            pe.wait_ge(sem("inv"), turned + n + 1)
                            if n >= 2:
                                pe.wait_ge(sem("mx"), turned + n - 1)
                            for j in range(HH):
                                mm = nc.tensor.matmul(ps[0:T, 2 + n % 2, j * T:(j + 1) * T], m_t[:, c, j, :],
                                                      inv[:, c, j, :], start=True, stop=True)
                            mm.then_inc(sem("mx_done"), 1)
                        if 0 <= step - 2 < NT:
                            c, n = step - 2, lv * NT + step - 2
                            pe.wait_ge(sem("mx"), turned + n + 1)
                            if n >= 2:
                                pe.wait_ge(sem("inv_t"), updated + NT + n - 1)
                            for j in range(HH):
                                mm = nc.tensor.matmul(ps[0:T, 4 + n % 2, j * T:(j + 1) * T], mx[:, n % 3, j, :],
                                                      inv_t[:, c, j, :], start=True, stop=True)
                            mm.then_inc(sem("change"), 1)
                        if 0 <= step - 4 < NT and lv < len(LEVELS) - 1:
                            c, n = step - 4, lv * NT + step - 4
                            pe.wait_ge(sem("inv_t"), updated + NT + n + 1)
                            pe.wait_ge(sem("inv"), turned + NT + n - 1)
                            turn_inv(c, 6 + n % 2)
                        if step == NT + 1:
                            fill(plan["level"])
                pe.wait_ge(sem("inv_t"), updated + UPDATES)
                pe.wait_ge(sem("inv"), turned + TURNS)
                pe.wait_ge(sem("q_g"), m0 + HH)

                def turn_block(c, which):
                    n = half_no * NT + c
                    if 2 * n + which:
                        pe.wait_ge(sem("vk_taken"), 2 * n + which)
                    for j in range(HH):
                        mm = nc.tensor.transpose(ps[0:T, 7, j * P:(j + 1) * P],
                                                 qkv[:, (HH if which else 2 * HH) + j, c * T:(c + 1) * T],
                                                 const("ident"))
                    mm.then_inc(sem("vk_turned"), 1)

                for which in range(2):
                    turn_block(0, which)
                for c in range(NT):
                    n = half_no * NT + c
                    at = slice(c * T, (c + 1) * T)
                    if c:
                        pe.wait_ge(sem("state"), (half_no * STEPS + c) * HH)
                        for j in range(HH):
                            mm = nc.tensor.matmul(ps[0:T, 2, j * DH:(j + 1) * DH], qkv[:, HH + j, at],
                                                  state[:, c % 2, j, :], start=True, stop=True)
                        mm.then_inc(sem("ks_done"), 1)
                    if c + 1 < NT:
                        turn_block(c + 1, 0)
                    if c:
                        pe.wait_ge(sem("resid"), (half_no * STEPS + c) * HH)
                    else:
                        pe.wait_ge(sem("vk_taken"), 2 * n + 2)
                    for j in range(HH):
                        mm = nc.tensor.matmul(ps[0:T, 3, j * DH:(j + 1) * DH], inv_t[:, c, j, :],
                                              resid[:, j, :] if c else v_b[:, 0, j, :], start=True, stop=True)
                    mm.then_inc(sem("u_done"), 1)
                    if c + 1 < NT:
                        turn_block(c + 1, 1)
                    fill()
                    pe.wait_ge(sem("u_new"), n + 1)
                    if c + 1 < NT:
                        pe.wait_ge(sem("vk_taken"), 2 * n + 2)
                        for j in range(HH):
                            mm = nc.tensor.matmul(ps[:, 4, j * DH:(j + 1) * DH], k_d[:, c % 2, j, :], u_new[:, j, :],
                                                  start=True, stop=True)
                        mm.then_inc(sem("grown"), 1)
                    if c >= 2:
                        pe.wait_ge(sem("o_raw"), n - 1)
                    for j in range(HH):
                        o = ps[:, 5 + c % 2, j * T:(j + 1) * T]
                        if c:
                            nc.tensor.matmul(o, state[:, c % 2, j, :], qkv[:, j, at], start=True, stop=False)
                        mm = nc.tensor.matmul(o, u_new[:, j, :], a_t[:, c, j, :], start=(c == 0), stop=True)
                    mm.then_inc(sem("o_done"), 1)
                    fill(plan["chunk"] - 1)
                pe.wait_ge(sem("o_raw"), (half_no + 1) * NT)
                for j in range(HH):
                    pe.wait_ge(sem("on_sq"), m0 + j + 1)
                    row_sums(row_of(j), work, j % 2, j == 0, j == HH - 1).then_inc(sem("on_sum"), 1)
                fill(plan["out_wait"])
                pe.wait_ge(sem("on_split"), 2 * half_no + 2)
                for j in range(HH):
                    if j >= 2:
                        pe.wait_ge(sem("o_normed"), m0 + j - 1)
                    spread(4 + 2 * (j % 2), sel_r[0:2 * R_GRP, j, :], n_hl).then_inc(sem("on_spread"), 1)
                finish()
                pe.wait_ge(sem("o_normed"), m0 + HH)
            pe.wait_ge(ACC_FREE[1], U_MIX // 2)

            with pe.Fori(U_MIX // 2, U_OUT // 2 - 1, 2) as p:
                for n, (hi, lo, tiles) in enumerate(((h_hi, h_lo, KD), (h_hi, h_lo, KD), (ob_hi, ob_lo, KD),
                                                     (fox_hi, fox_lo, FOX_BLOCKS))):
                    if n == 2:
                        pe.wait_ge(sem("ob_lo"), HEADS)
                    if n == 3:
                        pe.wait_ge(sem("fox_split"), 2)
                    dense_unit(p + n // 2, n % 2, hi, lo, tiles)
            def square_sums(s, first, last):
                for half in range(2):
                    mm = nc.tensor.matmul(ps[:, 4 + half, 0:HL], const("ones"),
                                          z[:, s, half * HL:(half + 1) * HL], start=first, stop=last)
                mm.then_inc(sem("n2_sq_used"), 1)

            pe.wait_ge(LO_READY, U_OUT + 1)
            pe.wait_ge(ACC_FREE[0], U_OUT // 2)
            for k in range(KD):
                pe.wait_ge(sem("mix_lo"), k + 1)
                for n, (w, x) in enumerate(((w_hi, mix_hi), (w_hi, mix_lo), (w_lo, mix_hi))):
                    for half in range(2):
                        mm = nc.tensor.matmul(ps[:, half, 0:HL], w[:, 0, k * P:(k + 1) * P],
                                              x[:, k, half * HL:(half + 1) * HL],
                                              start=(k == 0 and n == 0), stop=(k == KD - 1 and n == 2))
            mm.then_inc(UNIT_USED, 1)
            dense_unit(U_OUT // 2, 1, mix_hi, mix_lo)
            pe.wait_ge(sem("n2_sq"), 1)
            square_sums(0, True, False)
            with pe.Fori(1, KD // 2) as p:
                for s in range(2):
                    dense_unit(p + U_OUT // 2, s, mix_hi, mix_lo)
                    pe.wait_ge(sem("n2_sq"), p * 2 + s)
                    square_sums(1 - s, False, False)
            pe.wait_ge(sem("n2_sq"), KD)
            square_sums((KD - 1) % 2, False, True)

            rising_pair(U_UP // 2, "n2_lo")
            dense_loop(U_UP + 2, 2 * FF_BLOCKS - 2, h_hi, h_lo)
            pe.wait_ge(sem("u_lo"), (DOWN_UNITS - 1) * KD)
            with pe.Fori(0, KD // 2) as q:
                for s in range(2):
                    pe.wait_ge(ACC_FREE[s], q + U_DOWN // 2)
                    for part in range(DOWN_UNITS):
                        n = s * DOWN_UNITS + part
                        if part == DOWN_UNITS - 1:
                            pe.wait_ge(sem("u_lo"), FF_BLOCKS)
                        pe.wait_ge(LO_READY, q * 2 * DOWN_UNITS + (U_DOWN + n + 1))
                        tiles = min(KD, FF_BLOCKS - part * KD)
                        mm = products(s, n % 2, u_hi, u_lo, tiles, part == 0, part == DOWN_UNITS - 1, at=part * KD)
                        mm.then_inc(UNIT_USED, 1)

        @block.scalar
        def _(act):
            def norm(tag, root, h):
                act.wait_ge(sem(tag + "_sq_used"), KD)
                nc.scalar.activation(halves(root), pair(2), ACT.Sqrt, bias=param("eps"),
                                     scale=1.0 / D).then_inc(sem(tag + "_rooted"), 1)
                for k in range(KD):
                    act.wait_ge(sem(tag + "_h"), k + 1)
                    nc.scalar.copy(h_hi[:, k, :], h[:, k % 2, :]).then_inc(sem(tag + "_hi"), 1)

            act.wait_ge(sem("params_loaded"), 16)
            for k in range(KD):
                if k % (KD // X_PARTS) == 0:
                    act.wait_ge(sem(f"x_loaded{k * X_PARTS // KD}"), 16)
                if k >= 2:
                    act.wait_ge(sem("n1_sq_used"), k - 1)
                nc.scalar.activation(sq[:, k % 2, :], x_in[:, k, :], ACT.Square).then_inc(sem("n1_sq"), 1)
            act.wait_ge(sem("small_loaded"), 16)
            nc.scalar.copy(small_hi[:], small_raw[:]).then_inc(sem("small_hi"), 1)
            for s in range(2):
                split_hi(act, 0, s, first=True)
            norm("n1", root1[:], h32)

            def split_rows(src, dst, base, name):
                nc.scalar.copy(dst[base:base + R_GRP, :], src).then_inc(sem(name), 1)

            act.wait_ge(sem("n1_lo"), KD)
            act.wait_ge(sem("small_done"), 1)
            act.wait_ge(sem("small_lo"), 1)
            act.wait_ge(sem("const_loaded"), 16)
            act.wait_ge(sem("selects_loaded"), 16)
            nc.scalar.copy(sel_r[:].rearrange("p h n -> p (h n)"), sel_raw[:, 0, :]).then_inc(sem("selects"), 1)
            nc.scalar.copy(sel_qk[:].rearrange("p h n -> p (h n)"), sel_raw[0:2 * R_GRP, 1, :]).then_inc(sem("selects"), 1)
            act.wait_ge(sem("selects"), 2)
            for n in range(2 * FOX_BLOCKS):
                act.wait_ge(UNIT_USED, n + 1)
                nc.scalar.copy(halves(qk[:, n, :]), pair(n % 2)).then_inc(sem("qk_raw"), 1)
                if n >= 2:
                    act.wait_ge(sem("qk_sum"), n - 1)
                nc.scalar.activation(halves(qk_sq[:, n % 2, :]), pair(n % 2), ACT.Square).then_inc(sem("qk_sq"), 1)
                act.wait_ge(sem("qk_sq"), n + 1)
                nc.scalar.sem_inc(ACC_FREE[n % 2], 1)
                split_hi(act, n // 2 + 1, n % 2)
                if n == 2:
                    nc.scalar.copy(ident_r[:], const("ident", T, T)).then_inc(sem("masks_r"), 1)
                    nc.scalar.copy(neg_r[:], const("neg", T)).then_inc(sem("masks_r"), 1)
                if n == 3:
                    act.wait_ge(sem("stat_in"), 1)
                    nc.scalar.activation(st[1][:], st[0][:], ACT.Abs).then_inc(sem("stat_abs"), 1)
                    act.wait_ge(sem("stat_abs"), 1)
                    nc.scalar.activation(st[2][:], st[1][:], ACT.Exp, scale=-1.0).then_inc(sem("stat_exp"), 1)
                    nc.scalar.activation(st[3][R_B:R_G, :], st[0][R_B:R_G, :], ACT.Exp).then_inc(sem("beta_exp"), 1)
                    nc.scalar.activation(coef[:, 0:1], param("a_log", rows=R_END), ACT.Exp).then_inc(sem("coef"), 1)
                    act.wait_ge(sem("stat_exp"), 1)
                    nc.scalar.activation(st[1][:], st[2][:], ACT.Ln, bias=1.0).then_inc(sem("stat_ln"), 1)

            for b in range(FOX_BLOCKS):
                p, s = (U_V + b) // 2, b % 2
                act.wait_ge(UNIT_USED, U_V + b + 1)
                if b >= 2:
                    act.wait_ge(sem("v_turned"), b - 1)
                nc.scalar.copy(halves(v_chan[:, s, :]), pair(s)).then_inc(ACC_FREE[s], 1)
                split_hi(act, p + 1, s)
                if b == 0:
                    act.wait_ge(sem("qk_sum"), 2 * FOX_BLOCKS)
                    nc.scalar.activation(halves(qk_root[:]), pair(2, R_GRP), ACT.Sqrt,
                                         bias=param("qk_bias", rows=R_GRP), scale=param("qk_scale", rows=R_GRP)
                                         ).then_inc(sem("qk_rooted"), 1)
                if b == 1:
                    act.wait_ge(sem("qk_rec"), 1)
                    split_rows(qk_root[:], qk_hl, 0, "qk_split")
                if b == 2:
                    act.wait_ge(sem("g_row"), 1)
                    act.wait_ge(sem("to_end"), 1)
                    nc.scalar.activation(st[3][R_B:R_G, :], stat[0:R_B, :], ACT.Exp).then_inc(sem("e_rows"), 1)
                    nc.scalar.activation(stat[R_G:R_END, :], to_end[R_G:R_END, :], ACT.Exp
                                         ).then_inc(sem("stat_rows"), 1)
                    split_rows(stat[0:R_B, :], g_hl, 0, "g_split")
                    split_rows(stat[R_B:R_G, :], b_hl, R_GRP, "b_split")
            act.wait_ge(sem("f_ready"), 1)
            split_rows(nf_sum[:], nf_hl, 0, "nf_split")

            def quarter(u, q, multiplies, takes, finishes):
                if not takes:
                    return
                v = u - 1
                b = v - U_GDN
                if q == 0:
                    act.wait_ge(UNIT_USED, v + 1)
                    if b:
                        act.wait_ge(sem("woven"), b)
                    if v < U_Z:
                        nc.scalar.copy(halves(conv_in[:, GDN_TAPS - 1:]), pair(0)).then_inc(ACC_FREE[v % 2], 1)
                    else:
                        nc.scalar.activation(halves(conv_out[:]), pair(0), ACT.Copy, scale=0.5
                                             ).then_inc(sem("z_half"), 1)
                        act.wait_ge(sem("z_half"), v - U_Z + 1)
                        nc.scalar.activation(halves(tanh_out[:]), pair(0), ACT.Tanh, scale=0.5
                                             ).then_inc(ACC_FREE[v % 2], 1)
                    split_hi(act, (v + 2) // 2, v % 2)
                if q == 3 and v < U_Z:
                    act.wait_ge(sem("conv"), (b + 1) * GDN_TAPS)
                    nc.scalar.activation(tanh_out[:], conv_out[:], ACT.Tanh).then_inc(sem("tanh"), 1)

            fill, finish = weave(U_GDN, 3 * HH, quarter)
            act.wait_ge(sem("pads"), 1)
            fill(2)
            for i in range(2 * FOX_BLOCKS):
                if i % 4 != 3:
                    fill()

            def exponentials(n):
                t = fox_items[n][1]
                keys = (t + 1) * T
                act.wait_ge(sem("neg_max"), n + 1)
                if n >= 3:
                    act.wait_ge(sem("prob_turned"), n - 2)
                src, dst = (ps[0:T, 2 + t % 2, 0:keys], prob[:, n % 3, 0:keys]) if keys <= 512 else (
                    pair(1, T), halves(prob[:, n % 3, :]))
                nc.scalar.activation(dst, src, ACT.Exp, bias=neg_max[:, n:n + 1],
                                     accum_out=p_sum[:, n:n + 1]).then_inc(sem("prob_ready"), 1)

            def take_turned(n):
                keys = (fox_items[n][1] + 1) * T
                act.wait_ge(sem("prob_turned"), n + 1)
                if n >= 2:
                    act.wait_ge(sem("weighed"), n - 1)
                if keys <= HL:
                    mm = nc.scalar.copy(prob_t[:, n % 2, 0:keys], ps[0:T, 4, 0:keys])
                else:
                    nc.scalar.copy(prob_t[:, n % 2, 0:HL], ps[0:T, 4, 0:HL])
                    mm = nc.scalar.copy(prob_t[:, n % 2, HL:keys], ps[0:T, 5, 0:keys - HL])
                mm.then_inc(sem("prob_t"), 1)

            for n in range(N + 3):
                if n < N:
                    exponentials(n)
                fill()
                if 0 <= n - 2 < N:
                    take_turned(n - 2)
            finish()

            act.wait_ge(sem("fox_taken"), FOX_BLOCKS)
            act.wait_ge(sem("woven"), 3 * HH)
            for half_no, qkv in enumerate((qkv0, qkv1)):
                m0 = half_no * HH
                plan = GDN_FILLS[half_no]
                fill, finish = weave(*GDN_WEAVES[half_no], quarter)
                for n in range(2 * HH):
                    if n >= 2:
                        act.wait_ge(sem("gn_sum"), 2 * m0 + n - 1)
                    nc.scalar.activation(work[:, n % 2, :], qkv[:, n, :], ACT.Square).then_inc(sem("gn_sq"), 1)
                    if n % (2 * HH // plan["sums"]) == 0:
                        fill()

                def norm_rows(tag, sums, bias, scale):
                    act.wait_ge(sem(tag + "_sum"), sums)
                    nc.scalar.activation(halves(n_root[:]), pair(1, R_GRP), ACT.Sqrt, bias=bias, scale=scale
                                         ).then_inc(sem(tag + "_rooted"), 1)
                    fill(1)
                    act.wait_ge(sem(tag + "_rec"), half_no + 1)
                    split_rows(n_root[:], n_hl, 0, tag + "_split")

                norm_rows("gn", 2 * m0 + 2 * HH, param("gn_bias", rows=R_GRP), param("gn_scale", rows=R_GRP))
                fill(plan["norm_wait"] - 1)
                for n in range(2 * HH):
                    if n in (2, 5) and plan["spread"]:
                        fill()
                act.wait_ge(sem("gn_normed"), 2 * m0 + 1)
                for j in range(HH):
                    m = m0 + j
                    act.wait_ge(sem("spread"), 2 * m + 1)
                    if j:
                        act.wait_ge(sem("q_g"), m)
                    nc.scalar.activation(halves(work[:, 1, :]), pair(1), ACT.Exp).then_inc(sem("e_g"), 1)
                    nc.scalar.activation(g_end[:, j, :].rearrange("p (h t) -> p h t", h=2),
                                         pair(1)[:, :, T - 1::T], ACT.Exp).then_inc(sem("e_g"), 1)
                    fill()
                    act.wait_ge(sem("decay_diff"), m + 1)
                    nc.scalar.activation(decay[:], decay[:], ACT.Exp).then_inc(sem("decay_exp"), 1)
                    fill(plan["head"] - 1)
                turned = half_no * TURNS

                def take_inv(c, n):
                    act.wait_ge(sem("inv_turned"), turned + n + 1)
                    nc.scalar.copy(inv[:, c, :, :].rearrange("p j t -> p (j t)"), ps[0:T, 6 + n % 2, 0:HH * T]
                                   ).then_inc(sem("inv"), 1)

                for c in range(NT):
                    take_inv(c, c)
                for lv in range(len(LEVELS)):
                    for step in range(NT + 4):
                        if 0 <= step - 4 < NT and lv < len(LEVELS) - 1:
                            c = step - 4
                            take_inv(c, (lv + 1) * NT + c)
                        if step == NT + 1:
                            fill(plan["level"])
                for c in range(NT):
                    n = half_no * NT + c
                    act.wait_ge(sem("u_done"), n + 1)
                    if n:
                        act.wait_ge(sem("o_done"), n)
                    nc.scalar.copy(u_new[:].rearrange("p j d -> p (j d)"), ps[0:T, 3, :]).then_inc(sem("u_new"), 1)
                    fill()
                    act.wait_ge(sem("o_done"), n + 1)
                    nc.scalar.copy(o_raw[:, m0:m0 + HH, c * T:(c + 1) * T],
                                   ps[:, 5 + c % 2, 0:HH * T].rearrange("p (j t) -> p j t", j=HH)
                                   ).then_inc(sem("o_raw"), 1)
                    fill(plan["chunk"] - 1)
                act.wait_ge(sem("o_raw"), (half_no + 1) * NT)
                for j in range(HH):
                    if j >= 2:
                        act.wait_ge(sem("on_sum"), m0 + j - 1)
                    nc.scalar.activation(work[:, j % 2, :], o_raw[:, m0 + j, :], ACT.Square
                                         ).then_inc(sem("on_sq"), 1)
                norm_rows("on", m0 + HH, param("eps", rows=R_GRP), 1.0 / DH)
                fill(plan["out_wait"] - 1)
                finish()
                act.wait_ge(sem("o_normed"), m0 + HH)
            act.wait_ge(sem("woven"), 3 * HEADS + HEADS)

            def split_ob(first):
                for n in range(first, first + HH):
                    act.wait_ge(sem("gated"), n + 1)
                    nc.scalar.copy(ob_hi[:, n, :], zg[:, n % 2, :]).then_inc(sem("ob_hi"), 1)

            def mixing_block(p, j, first):
                for s, gate in enumerate((gate_a, gate_b)):
                    if first:
                        split_ob(s * HH)
                    act.wait_ge(UNIT_USED, p * 2 + (s + 1))
                    if not first:
                        act.wait_ge(sem("mix_lo"), j)
                    nc.scalar.activation(halves(gate[:]), pair(s), ACT.Tanh, scale=0.5).then_inc(ACC_FREE[s], 1)
                    split_hi(act, p + 1, s)
                if first:
                    nc.scalar.copy(fox_hi[:], fox_o[:]).then_inc(sem("fox_split"), 1)
                for s in range(2):
                    split_hi(act, p + 2, s)
                act.wait_ge(sem("mixed"), j + 1)
                nc.scalar.activation(flat(mix_hi, j), gate_a[:], ACT.Copy, scale=0.5).then_inc(sem("mix_hi"), 1)

            mixing_block(U_MIX // 2, 0, True)
            with act.Fori(1, KD) as j:
                mixing_block(j * (MIX_UNITS // 2) + U_MIX // 2, j, False)

            def square_block(p, s, first):
                split_hi(act, p + (U_OUT // 2 + 1), s)
                act.wait_ge(ACC_FREE[s], p + (U_OUT // 2 + 1))
                if not first:
                    act.wait_ge(sem("n2_sq_used"), p * 2 + (s - 1))
                nc.scalar.activation(z[:, s, :], flat(x_res, p * 2 + s), ACT.Square).then_inc(sem("n2_sq"), 1)

            for s in range(2):
                square_block(0, s, True)
            with act.Fori(1, KD // 2) as p:
                for s in range(2):
                    square_block(p, s, False)

            norm("n2", ff_silu[:], ff_conv)

            def split_u(b):
                act.wait_ge(sem("ff_u"), b + 1)
                nc.scalar.copy(flat(u_hi, b), ff_u[:, 0, :]).then_inc(sem("u_hi"), 1)

            def up_block(p, b, first):
                act.wait_ge(UNIT_USED, p * 2 + 1)
                if not first:
                    act.wait_ge(sem("ff_g"), b * 3)
                nc.scalar.copy(halves(ff_in[:, 0, FFN_TAPS - 1:]), pair(0)).then_inc(ACC_FREE[0], 1)
                split_hi(act, p + 1, 0)
                if not first:
                    split_u(b - 1)
                act.wait_ge(sem("ff_g"), b * 3 + 3)
                nc.scalar.activation(ff_silu[:], ff_conv[:, 0, :], ACT.Silu).then_inc(sem("ff_silu"), 1)
                act.wait_ge(UNIT_USED, p * 2 + 2)
                if not first:
                    act.wait_ge(sem("ff_v"), b * 3)
                nc.scalar.copy(halves(ff_in[:, 1, FFN_TAPS - 1:]), pair(1)).then_inc(ACC_FREE[1], 1)
                split_hi(act, p + 1, 1)

            act.wait_ge(sem("ff_pads"), 1)
            act.wait_ge(sem("n2_lo"), KD)
            up_block(U_UP // 2, 0, True)
            with act.Fori(1, FF_BLOCKS) as b:
                up_block(b + U_UP // 2, b, False)
            split_u(FF_BLOCKS - 1)
            with act.Fori(U_DOWN // 2 + 1, N_UNITS // 2) as p:
                for s in range(2):
                    split_hi(act, p, s)

        @block.vector
        def _(dve):
            def norm(tag, x, gain, root, h):
                dve.wait_ge(sem(tag + "_rooted"), 1)
                nc.vector.reciprocal(root, root).then_inc(sem(tag + "_rec"), 1)
                dve.wait_ge(sem(tag + "_rec"), 1)
                for k in range(KD + 1):
                    if k < KD:
                        if k >= 2:
                            dve.wait_ge(sem(tag + "_lo"), k - 1)
                        nc.vector.scalar_tensor_tensor(h[:, k % 2, :], x[:, k, :], param(gain, k), root,
                                                       ALU.mult, ALU.mult).then_inc(sem(tag + "_h"), 1)
                    if k:
                        dve.wait_ge(sem(tag + "_hi"), k)
                        nc.vector.tensor_tensor(h_lo[:, k - 1, :], h[:, (k - 1) % 2, :],
                                                h_hi[:, k - 1, :].bitcast(F32), ALU.subtract
                                                ).then_inc(sem(tag + "_lo"), 1)

            dve.wait_ge(sem("small_hi"), 1)
            nc.vector.tensor_tensor(small_lo[:], small_raw[:], small_hi[:].bitcast(F32),
                                    ALU.subtract).then_inc(sem("small_lo"), 1)
            for s in range(2):
                split_lo(dve, 0, s)
            dve.wait_ge(sem("params_loaded"), 16)
            norm("n1", x_in, "norm1", root1[:], h32)
            dve.wait_ge(sem("small_done"), 1)
            nc.vector.tensor_scalar(halves(st[0][:]), pair(3, R_END), param("stat_bias", rows=R_END),
                                    param("stat_sign", rows=R_END), ALU.add, ALU.mult).then_inc(sem("stat_in"), 1)

            def split_rows(src, dst, hi, lo, name, wait):
                dve.wait_ge(sem(name), wait)
                nc.vector.tensor_tensor(dst[lo:lo + R_GRP, :], src, dst[hi:hi + R_GRP, :].bitcast(F32),
                                        ALU.subtract).then_inc(sem(name), 1)

            taps_at = slice(PARAM["gdn_taps"], PARAM["gdn_taps"] + GDN_TAPS * 3 * HEADS)
            nc.vector.tensor_scalar(prm[:, taps_at], prm[:, taps_at], 0.5, None, ALU.mult
                                    ).then_inc(sem("taps_halved"), 1)
            nc.vector.memset(nf_hl[2 * R_GRP:P, :].bitcast(F32), 0.0).then_inc(sem("masks_r"), 1)
            nc.vector.memset(conv_in[:, 0:GDN_TAPS - 1], 0.0).then_inc(sem("pads"), 1)

            def take_v(b):
                dve.wait_ge(sem("v_turned"), b + 1)
                nc.vector.tensor_copy(v_tok[:, :, b * P:(b + 1) * P].rearrange("p (h t) c -> p h t c", h=2),
                                      tiles_of(ps[0:T, 6:8, 0:TH * P], P)).then_inc(sem("v_tok"), 1)

            def log_gates():
                dve.wait_ge(sem("stat_ln"), 1)
                nc.vector.scalar_tensor_tensor(st[2][:], st[0][:], 0.0, st[1][:], ALU.max, ALU.add
                                               ).then_inc(sem("softplus"), 1)
                dve.wait_ge(sem("coef"), 1)
                nc.vector.tensor_scalar(coef[:, 1:2], coef[:, 0:1], -1.0, None, ALU.mult).then_inc(sem("coef"), 1)
                dve.wait_ge(sem("softplus"), 1)
                dve.wait_ge(sem("coef"), 2)
                nc.vector.tensor_scalar(st[1][:], st[2][:], coef[:, 1:2], None, ALU.mult
                                        ).then_inc(sem("log_gates"), 1)
                dve.wait_ge(sem("log_gates"), 1)

            def betas():
                dve.wait_ge(sem("beta_exp"), 1)
                nc.vector.tensor_scalar(st[3][R_B:R_G, :], st[3][R_B:R_G, :], 1.0, None, ALU.add
                                        ).then_inc(sem("beta"), 1)
                dve.wait_ge(sem("beta"), 1)
                nc.vector.reciprocal(stat[R_B:R_G, :], st[3][R_B:R_G, :]).then_inc(sem("stat_rows"), 1)

            def cumsum(steps):
                for i in steps:
                    src, dst, shift = 1 + i % 2, 2 - i % 2, 2 ** i
                    a, b = (st[k][:].rearrange("p (t c) -> p t c", c=T) for k in (src, dst))
                    nc.vector.tensor_tensor(b[:, :, shift:], a[:, :, shift:], a[:, :, :T - shift], ALU.add
                                            ).then_inc(sem("cumsum"), 1)
                    nc.vector.tensor_copy(b[:, :, :shift], a[:, :, :shift]).then_inc(sem("cumsum"), 1)
                    dve.wait_ge(sem("cumsum"), 2 * i + 2)

            def decay_rows():
                g_rows = st_sum[R_G:R_END, :].rearrange("p (t c) -> p t c", c=T)
                nc.vector.tensor_copy(stat[0:R_B, :], st_sum[R_G:R_END, :]).then_inc(sem("g_row"), 1)
                nc.vector.tensor_tensor(to_end[R_G:R_END, :].rearrange("p (t c) -> p t c", c=T),
                                        g_rows[:, :, T - 1:T].broadcast_to([R_END - R_G, NT, T]), g_rows,
                                        ALU.subtract).then_inc(sem("to_end"), 1)

            def forget_sums():
                nc.vector.tensor_copy(f_sum[:, 0:T], st_sum[0:R_GRP, 0:T]).then_inc(sem("f_tile"), 1)
                for t in range(1, NT):
                    dve.wait_ge(sem("f_tile"), t)
                    nc.vector.tensor_scalar(f_sum[:, t * T:(t + 1) * T], st_sum[0:R_GRP, t * T:(t + 1) * T],
                                            f_sum[:, t * T - 1:t * T], None, ALU.add).then_inc(sem("f_tile"), 1)
                dve.wait_ge(sem("f_tile"), NT)
                nc.vector.tensor_scalar(nf_sum[:], f_sum[:], -1.0, None, ALU.mult).then_inc(sem("f_ready"), 1)

            for n in range(2 * FOX_BLOCKS):
                split_lo(dve, n // 2 + 1, n % 2)
                if n == 4:
                    log_gates()
                    cumsum(range(0, 2))
                if n == 5:
                    cumsum(range(2, 5))
                if n == 6:
                    cumsum(range(5, n_scan))
                    decay_rows()
                if n == 7:
                    betas()
            for b in range(FOX_BLOCKS):
                split_lo(dve, (U_V + b) // 2 + 1, b % 2)
                if b:
                    take_v(b - 1)
                if b == 0:
                    dve.wait_ge(sem("qk_rooted"), 1)
                    nc.vector.reciprocal(qk_root[:], qk_root[:]).then_inc(sem("qk_rec"), 1)
                if b == 1:
                    forget_sums()
                if b == 2:
                    split_rows(qk_root[:], qk_hl, 0, R_GRP, "qk_split", 1)
            dve.wait_ge(sem("e_rows"), 1)
            dve.wait_ge(sem("stat_rows"), 2)
            nc.vector.scalar_tensor_tensor(stat[R_BE:S_END, :], st[3][R_B:R_G, :], -1.0, stat[R_B:R_G, :], ALU.mult,
                                           ALU.mult).then_inc(sem("stat_rows"), 2)
            take_v(FOX_BLOCKS - 1)
            split_rows(stat[0:R_B, :], g_hl, 0, R_GRP, "g_split", 1)
            split_rows(stat[R_B:R_G, :], b_hl, R_GRP, 0, "b_split", 1)
            split_rows(nf_sum[:], nf_hl, 0, R_GRP, "nf_split", 1)
            dve.wait_ge(sem("tok_turned"), 1)
            nc.vector.tensor_copy(tok[:].rearrange("p (h t) r -> p h t r", h=2),
                                  tiles_of(ps[0:T, 4:6, 0:TH * S_END], S_END)).then_inc(sem("tok_ready"), 1)

            def quarter(u, q, multiplies, takes, finishes):
                if finishes and q == 0:
                    v = u - 2
                    if v < U_Z:
                        dve.wait_ge(sem("tanh"), v - U_GDN + 1)
                        nc.vector.scalar_tensor_tensor(woven_target(v), tanh_out[:], 1.0, conv_out[:], ALU.add,
                                                       ALU.mult).then_inc(sem("woven"), 1)
                v = u - 1
                if not takes:
                    return
                b = v - U_GDN
                if q == 1:
                    split_lo(dve, (v + 2) // 2, v % 2)
                    dve.wait_ge(ACC_FREE[v % 2], v // 2 + 1)
                    if v >= U_Z:
                        nc.vector.scalar_tensor_tensor(woven_target(v), tanh_out[:], 1.0, conv_out[:], ALU.add,
                                                       ALU.mult).then_inc(sem("woven"), 1)
                if q in (1, 2) and v < U_Z:
                    for i in ((0, 1), (2, 3))[q - 1]:
                        at = GDN_TAPS - 1 - i
                        tap = param("gdn_taps", b * GDN_TAPS + at)
                        if i == 0:
                            nc.vector.tensor_scalar(conv_out[:], conv_in[:, at:at + L], tap, None, ALU.mult
                                                    ).then_inc(sem("conv"), 1)
                        else:
                            dve.wait_ge(sem("conv"), b * GDN_TAPS + i)
                            nc.vector.scalar_tensor_tensor(conv_out[:], conv_in[:, at:at + L], tap, conv_out[:],
                                                           ALU.mult, ALU.add).then_inc(sem("conv"), 1)

            fill, finish = weave(U_GDN, 3 * HH, quarter)
            dve.wait_ge(sem("taps_halved"), 1)
            fill(2)
            for i, n in enumerate(QK_ORDER):
                dve.wait_ge(sem("qk_spread"), i + 1)
                nc.vector.scalar_tensor_tensor(halves(qk[:, n, :]), halves(qk[:, n, :]), param("qk", n),
                                               pair(3 - i % 2), ALU.mult, ALU.mult).then_inc(sem("qk_normed"), 1)
                if i % 4 != 3:
                    fill()

            for n in range(N + 5):
                if n < N:
                    t = fox_items[n][1]
                    keys = (t + 1) * T
                    dve.wait_ge(sem("scored"), n + 1)
                    if keys <= 512:
                        nc.vector.tensor_reduce(neg_max[:, n:n + 1], ps[0:T, 2 + t % 2, 0:keys], AX.X, ALU.max,
                                                negate=True).then_inc(sem("neg_max"), 1)
                    else:
                        nc.vector.tensor_reduce(neg_max[:, n:n + 1], pair(1, T), AX.XY, ALU.max,
                                                negate=True).then_inc(sem("neg_max"), 1)
                if 1 <= n <= N:
                    i = n - 1
                    keys = (fox_items[i][1] + 1) * T
                    dve.wait_ge(sem("prob_ready"), i + 1)
                    nc.vector.reciprocal(p_rec[:, i:i + 1], p_sum[:, i:i + 1]).then_inc(sem("p_rec"), 1)
                    dve.wait_ge(sem("p_rec"), i + 1)
                    nc.vector.tensor_scalar(prob[:, i % 3, 0:keys], prob[:, i % 3, 0:keys], p_rec[:, i:i + 1], None,
                                            ALU.mult).then_inc(sem("prob_scaled"), 1)
                if n < N + 3:
                    fill()
                if n >= 4 and (n - 4) % PAIR_ITEMS == PAIR_ITEMS - 1:
                    b = (n - 4) // PAIR_ITEMS
                    dve.wait_ge(sem("weighed"), (b + 1) * PAIR_ITEMS)
                    nc.vector.tensor_copy(halves(fox_o[:, b, :]), pair(3)).then_inc(sem("fox_taken"), 1)
            finish()

            for half_no, qkv in enumerate((qkv0, qkv1)):
                m0 = half_no * HH
                plan = GDN_FILLS[half_no]
                fill, finish = weave(*GDN_WEAVES[half_no], quarter)

                def norm_rows(tag):
                    dve.wait_ge(sem(tag + "_rooted"), half_no + 1)
                    nc.vector.reciprocal(n_root[:], n_root[:]).then_inc(sem(tag + "_rec"), 1)
                    fill(1)
                    split_rows(n_root[:], n_hl, 0, R_GRP, tag + "_split", 2 * half_no + 1)

                fill(plan["sums"])
                norm_rows("gn")
                fill(plan["norm_wait"] - 1)
                for n in range(2 * HH):
                    dve.wait_ge(sem("gn_spread"), 2 * m0 + n + 1)
                    nc.vector.tensor_tensor(halves(qkv[:, n, :]), halves(qkv[:, n, :]), pair(2 + n % 2), ALU.mult
                                            ).then_inc(sem("gn_normed"), 1)
                    if n in (2, 5) and plan["spread"]:
                        fill()
                dve.wait_ge(sem("tok_ready"), 1)
                dve.wait_ge(sem("gn_normed"), 2 * m0 + 2 * HH)
                for j in range(HH):
                    m = m0 + j
                    dve.wait_ge(sem("spread"), 2 * m + 2)
                    if j:
                        dve.wait_ge(sem("mats"), 2 * m)
                    nc.vector.tensor_tensor(halves(work[:, 0, :]), pair(2), halves(qkv[:, HH + j, :]), ALU.mult
                                            ).then_inc(sem("k_b"), 1)
                    dve.wait_ge(sem("e_g"), 2 * m + 2)
                    for t in range(NT):
                        mm = nc.vector.tensor_scalar(decay[:, t, :],
                                                     ps[0:T, 2 + t // TH, (t % TH) * T:(t % TH + 1) * T],
                                                     tok[:, t, m:m + 1], 0.0, ALU.subtract, ALU.min)
                    mm.then_inc(sem("decay_diff"), 1)
                    fill()
                    dve.wait_ge(sem("decay_exp"), m + 1)
                    dve.wait_ge(sem("mats"), 2 * m + 2)
                    d = decay[:].rearrange("p (h t) c -> p h t c", h=2)
                    nc.vector.tensor_tensor(m_t[:, :, j, :].rearrange("p (h t) c -> p h t c", h=2),
                                            tiles_of(pair(2, T), T), d, ALU.mult).then_inc(sem("mat_taken"), 1)
                    nc.vector.tensor_tensor(decay[:], decay[:],
                                            const("incl", T).unsqueeze(1).broadcast_to([T, NT, T]), ALU.mult
                                            ).then_inc(sem("decay_i"), 1)
                    nc.vector.tensor_tensor(qkv[:, j, :], qkv[:, j, :], work[:, 1, :], ALU.mult
                                            ).then_inc(sem("q_g"), 1)
                    dve.wait_ge(sem("decay_i"), m + 1)
                    nc.vector.tensor_tensor(a_t[:, :, j, :].rearrange("p (h t) c -> p h t c", h=2),
                                            tiles_of(pair(3, T), T), d, ALU.mult).then_inc(sem("mat_taken"), 1)
                    fill(plan["head"] - 1)
                turned, updated = half_no * TURNS, half_no * UPDATES
                dve.wait_ge(sem("mat_taken"), 2 * (m0 + HH))
                for c in range(NT):
                    nc.vector.tensor_tensor(mx[:, c % 3, :, :], m_t[:, c, :, :], over_heads(const("pair", T)),
                                            ALU.mult).then_inc(sem("pair_m"), 1)
                    dve.wait_ge(sem("pair_m"), half_no * NT + c + 1)
                    nc.vector.tensor_tensor(inv_t[:, c, :, :], over_heads(const("ident", T, T)), mx[:, c % 3, :, :],
                                            ALU.subtract).then_inc(sem("inv_t"), 1)
                for lv in range(len(LEVELS)):
                    for step in range(NT + 2):
                        if step < NT:
                            n = lv * NT + step
                            dve.wait_ge(sem("mx_done"), turned + n + 1)
                            if n >= 3:
                                dve.wait_ge(sem("change"), turned + n - 2)
                            nc.vector.tensor_tensor(mx[:, n % 3, :, :],
                                                    ps[0:T, 2 + n % 2, 0:HH * T].rearrange("p (j t) -> p j t", j=HH),
                                                    over_heads(level_mask(lv)), ALU.mult).then_inc(sem("mx"), 1)
                        if step >= 2:
                            c, n = step - 2, lv * NT + step - 2
                            dve.wait_ge(sem("change"), turned + n + 1)
                            nc.vector.tensor_tensor(inv_t[:, c, :, :], inv_t[:, c, :, :],
                                                    ps[0:T, 4 + n % 2, 0:HH * T].rearrange("p (j t) -> p j t", j=HH),
                                                    ALU.subtract).then_inc(sem("inv_t"), 1)
                    fill(plan["level"])

                def take_block(c, which):
                    n = half_no * NT + c
                    o, row = ((v_b, R_B), (k_d, R_G))[which]
                    dve.wait_ge(sem("vk_turned"), 2 * n + which + 1)
                    scale = tok[:, c, row + m0:row + m0 + HH].unsqueeze(2).broadcast_to([T, HH, DH])
                    nc.vector.tensor_tensor(o[:, c % 2, :, :], ps[0:T, 7, :].rearrange("p (j d) -> p j d", j=HH),
                                            scale, ALU.mult).then_inc(sem("vk_taken"), 1)

                dve.wait_ge(sem("e_g"), 2 * (m0 + HH))
                for which in range(2):
                    take_block(0, which)
                for c in range(NT):
                    n = half_no * NT + c
                    if c:
                        dve.wait_ge(sem("ks_done"), half_no * STEPS + c)
                        dve.wait_ge(sem("vk_taken"), 2 * n + 1)
                        for j in range(HH):
                            nc.vector.scalar_tensor_tensor(resid[:, j, :], ps[0:T, 2, j * DH:(j + 1) * DH],
                                                           tok[:, c, R_BE + m0 + j:R_BE + m0 + j + 1],
                                                           v_b[:, c % 2, j, :], ALU.mult, ALU.add
                                                           ).then_inc(sem("resid"), 1)
                    if c + 1 < NT:
                        take_block(c + 1, 0)
                    fill()
                    if c + 1 < NT:
                        dve.wait_ge(sem("grown"), half_no * STEPS + c + 1)
                        if c:
                            dve.wait_ge(sem("state"), (half_no * STEPS + c) * HH)
                        for j in range(HH):
                            new = state[:, (c + 1) % 2, j, :]
                            grown = ps[:, 4, j * DH:(j + 1) * DH]
                            if c:
                                nc.vector.scalar_tensor_tensor(new, state[:, c % 2, j, :], g_end[:, j, c:c + 1],
                                                               grown, ALU.mult, ALU.add).then_inc(sem("state"), 1)
                            else:
                                nc.vector.tensor_copy(new, grown).then_inc(sem("state"), 1)
                        take_block(c + 1, 1)
                    fill(plan["chunk"] - 1)
                norm_rows("on")
                fill(plan["out_wait"] - 1)
                for j in range(HH):
                    m = m0 + j
                    dve.wait_ge(sem("on_spread"), m + 1)
                    nc.vector.scalar_tensor_tensor(halves(o_raw[:, m, :]), halves(o_raw[:, m, :]),
                                                   param("gdn_norm"), pair(2 + j % 2), ALU.mult, ALU.mult
                                                   ).then_inc(sem("o_normed"), 1)
                finish()

            dve.wait_ge(sem("o_normed"), HEADS)
            dve.wait_ge(sem("woven"), 4 * HEADS)

            def gate_outputs(first):
                for n in range(first, first + HH + 1):
                    if n < first + HH:
                        if n >= 2:
                            dve.wait_ge(sem("ob_lo"), n - 1)
                        nc.vector.tensor_tensor(zg[:, n % 2, :], z[:, n, :], o_raw[:, n, :], ALU.mult
                                                ).then_inc(sem("gated"), 1)
                    if n > first:
                        dve.wait_ge(sem("ob_hi"), n)
                        nc.vector.tensor_tensor(ob_lo[:, n - 1, :], zg[:, (n - 1) % 2, :],
                                                ob_hi[:, n - 1, :].bitcast(F32), ALU.subtract
                                                ).then_inc(sem("ob_lo"), 1)

            def mixing_block(p, j, first):
                for s in range(2):
                    if first:
                        gate_outputs(s * HH)
                    split_lo(dve, p + 1, s)
                if first:
                    dve.wait_ge(sem("fox_split"), 1)
                    nc.vector.tensor_tensor(fox_lo[:], fox_o[:], fox_hi[:].bitcast(F32), ALU.subtract
                                            ).then_inc(sem("fox_split"), 1)
                for s, gate in enumerate((gate_b, gate_a)):
                    split_lo(dve, p + 2, s)
                    dve.wait_ge(ACC_FREE[1 - s], p + 1)
                    dve.wait_ge(UNIT_USED, p * 2 + (s + 3))
                    nc.vector.scalar_tensor_tensor(halves(gate[:]), halves(gate[:]), 1.0, pair(s), ALU.add, ALU.mult
                                                   ).then_inc(ACC_FREE[s], 1)
                for s in range(2):
                    dve.wait_ge(ACC_FREE[s], p + 2)
                nc.vector.tensor_tensor(gate_a[:], gate_a[:], gate_b[:], ALU.add).then_inc(sem("mixed"), 1)
                dve.wait_ge(sem("mix_hi"), j + 1)
                nc.vector.scalar_tensor_tensor(flat(mix_lo, j), gate_a[:], 0.5, flat(mix_hi, j).bitcast(F32),
                                               ALU.mult, ALU.subtract).then_inc(sem("mix_lo"), 1)

            mixing_block(U_MIX // 2, 0, True)
            with dve.Fori(1, KD) as j:
                mixing_block(j * (MIX_UNITS // 2) + U_MIX // 2, j, False)

            dve.wait_ge(sem("x_reloaded"), 16)
            with dve.Fori(U_OUT // 2, (U_OUT + KD) // 2) as p:
                for s in range(2):
                    j = p * 2 + (s - U_OUT)
                    split_lo(dve, p + 1, s)
                    dve.wait_ge(UNIT_USED, p * 2 + (s + 1))
                    nc.vector.tensor_tensor(block_of(x_res, j), pair(s), block_of(x_res, j), ALU.add
                                            ).then_inc(ACC_FREE[s], 1)
            nc.vector.memset(ff_in[:, :, 0:FFN_TAPS - 1], 0.0).then_inc(sem("ff_pads"), 1)
            norm("n2", x_res, "norm2", ff_silu[:], ff_conv)

            dve.wait_ge(sem("ff_pads"), 1)
            dve.wait_ge(sem("n2_lo"), KD)

            def ff_conv_block(p, b, s, name, first):
                split_lo(dve, p + 1, s)
                dve.wait_ge(ACC_FREE[s], p + 1)
                taps = [param("ffn_taps", b * (2 * FFN_TAPS) + (s * FFN_TAPS + i)) for i in range(FFN_TAPS)]
                o = ff_conv[:, s, :]
                if s == 0 and not first:
                    dve.wait_ge(sem("ff_silu"), b)
                nc.vector.tensor_scalar(o, ff_in[:, s, FFN_TAPS - 1:], taps[-1], None, ALU.mult
                                        ).then_inc(sem(name), 1)
                for i in range(1, FFN_TAPS):
                    at = FFN_TAPS - 1 - i
                    dve.wait_ge(sem(name), b * FFN_TAPS + i)
                    nc.vector.scalar_tensor_tensor(o, ff_in[:, s, at:at + L], taps[at], o, ALU.mult, ALU.add
                                                   ).then_inc(sem(name), 1)

            def split_u(b):
                dve.wait_ge(sem("u_hi"), b + 1)
                nc.vector.tensor_tensor(flat(u_lo, b), ff_u[:, 0, :], flat(u_hi, b).bitcast(F32), ALU.subtract
                                        ).then_inc(sem("u_lo"), 1)

            def up_block(p, b, first):
                ff_conv_block(p, b, 0, "ff_g", first)
                if not first:
                    split_u(b - 1)
                ff_conv_block(p, b, 1, "ff_v", first)
                dve.wait_ge(sem("ff_silu"), b + 1)
                dve.wait_ge(sem("ff_v"), b * FFN_TAPS + FFN_TAPS)
                if not first:
                    dve.wait_ge(sem("u_lo"), b)
                nc.vector.tensor_tensor(ff_u[:, 0, :], ff_silu[:], ff_conv[:, 1, :], ALU.mult
                                        ).then_inc(sem("ff_u"), 1)

            up_block(U_UP // 2, 0, True)
            with dve.Fori(1, FF_BLOCKS) as b:
                up_block(b + U_UP // 2, b, False)
            split_u(FF_BLOCKS - 1)

            def down_block(q, s, first, last):
                for part in range(DOWN_UNITS):
                    n = s * DOWN_UNITS + part
                    if not (last and n + 2 >= 2 * DOWN_UNITS):
                        split_lo(dve, q * DOWN_UNITS + (U_DOWN // 2 + n // 2 + 1), n % 2)
                dve.wait_ge(UNIT_USED, q * 2 * DOWN_UNITS + (U_DOWN + (s + 1) * DOWN_UNITS))
                if not first:
                    dve.wait_ge(sem(f"stored{s}"), q * 16)
                nc.vector.tensor_tensor(halves(y_out[:, s, :]), pair(s), block_of(x_res, q * 2 + s), ALU.add
                                        ).then_inc(sem("y_ready"), 1)
                dve.wait_ge(sem("y_ready"), q * 2 + (s + 1))
                nc.vector.sem_inc(ACC_FREE[s], 1)

            for s in range(2):
                down_block(0, s, True, False)
            with dve.Fori(1, KD // 2 - 1) as q:
                for s in range(2):
                    down_block(q, s, False, False)
            for s in range(2):
                down_block(KD // 2 - 1, s, False, True)


def constants():
    c = np.zeros((P, C_COLS), np.float32)

    def put(name, value):
        c[:value.shape[0], CONST[name]:CONST[name] + value.shape[1]] = value

    r, k = np.arange(T)[:, None], np.arange(T)[None, :]
    put("ident", np.eye(P, dtype=np.float32))
    put("ones", np.ones((P, P), np.float32))
    put("row_of", np.eye(1, 2 * R_GRP, R_GRP - 1, dtype=np.float32).repeat(P, 0))
    put("row_of64", np.eye(2, 2 * R_GRP, R_GRP - 1, dtype=np.float32).repeat(FOX_DIM, 0))
    put("incl", (r <= k).astype(np.float32))
    put("pair", ((k % 2 == 1) & (r == k - 1)).astype(np.float32))
    put("neg", np.where(k > r, np.float32(-1e30), np.float32(0)))
    put("levels", np.concatenate([((r // n % 2 == 1) & (k // n == r // n - 1)) for n in LEVELS], 1
                                 ).astype(np.float32))
    return c


def row_selections():
    s = np.zeros((P, 2, 8, P), np.float32)
    for base in (0, R_GRP):
        for n in range(8):
            s[base + n, 0, n] = 1
            for side in range(2):
                s[base + 2 * n + side, 1, n, side * FOX_DIM:(side + 1) * FOX_DIM] = 1
    return s.reshape(P, 2, 8 * P)


def lay_out(inputs):
    a = {k: np.asarray(v) for k, v in inputs.items()}
    tokens = np.concatenate([a["meta_tokens"], a["x"][0]])
    x_t = np.ascontiguousarray(tokens.T.reshape(KD, P, L).transpose(1, 0, 2))
    w_in = a["w_in"][0]
    fox_w, gdn_w = FOX_HEADS * FOX_DIM, HEADS * DH
    o_f = 3 * fox_w
    o_g = o_f + FOX_HEADS
    o_b = o_g + 3 * gdn_w
    o_z = o_b + 2 * HEADS
    o_gate = o_z + gdn_w

    def rows(w):
        return w.reshape(-1, P, w.shape[1]).transpose(1, 0, 2)

    def unit(w):
        u = np.zeros((P, UNIT), w.dtype)
        u[:, :w.shape[0]] = rows(w).reshape(P, -1)
        return u

    small = np.zeros((D, R_END), w_in.dtype)
    small[:, R_F:R_F + HEADS] = w_in[:, o_f:o_f + HEADS]
    small[:, R_B:R_B + HEADS] = w_in[:, o_b:o_b + HEADS]
    small[:, R_G:R_G + HEADS] = w_in[:, o_b + HEADS:o_z]

    units = [w_in[:, b * P:(b + 1) * P] for b in range(3 * FOX_BLOCKS)]
    gdn_cols = [which * gdn_w + (half * HH + j) * DH for half in range(2) for which in range(3) for j in range(HH)]
    units += [w_in[:, o_g + c:o_g + c + P] for c in gdn_cols]
    units += [w_in[:, o_z + j * P:o_z + (j + 1) * P] for j in range(HEADS)]
    for j in range(KD):
        at = slice(j * P, (j + 1) * P)
        units += [w_in[:, o_gate:o_gate + D][:, at], w_in[:, o_gate + D:][:, at],
                  a["w_branch_b"][0][:, at], a["w_branch_a"][0][:, at]]
    units += [a["w_out"][0][:, j * P:(j + 1) * P] for j in range(KD)]
    for b in range(FF_BLOCKS):
        for s in range(2):
            units.append(a["w_up"][0][:, s * D_FF + b * P:s * D_FF + (b + 1) * P])
    for j in range(KD):
        for part in range(DOWN_UNITS):
            units.append(a["w_down"][0][part * D:(part + 1) * D, j * P:(j + 1) * P])
    w_units = np.stack([unit(u) for u in units])

    prm = np.zeros((P, P_COLS), np.float32)

    def put(name, value, i=0, rows_at=0):
        prm[rows_at:rows_at + value.shape[0], PARAM[name] + i:PARAM[name] + i + value.shape[1]] = value

    put("norm1", a["norm1_g"][0].reshape(KD, P).T)
    put("norm2", a["norm2_g"][0].reshape(KD, P).T)
    put("gdn_norm", a["gdn_norm_g"][0][:, None])
    put("stat_bias", a["fox_f_bias"][0][:, None], rows_at=R_F)
    put("stat_bias", a["gdn_dt_bias"][0][:, None], rows_at=R_G)
    for at, sign in ((R_F, -1), (R_B, -1), (R_G, 1)):
        put("stat_sign", np.full((HEADS, 1), sign, np.float32), rows_at=at)
    put("a_log", a["gdn_a_log"][0][:, None], rows_at=R_G)
    put("eps", np.full((P, 1), EPS, np.float32))
    put("gn_scale", np.where(np.arange(R_GRP) < HH, DH, 1)[:, None])
    put("gn_bias", np.where(np.arange(R_GRP) < HH, EPS * DH, EPS)[:, None])
    put("qk_scale", np.where(np.arange(R_GRP) < FOX_HEADS, 1, 1.0 / FOX_DIM)[:, None])
    put("qk_bias", np.where(np.arange(R_GRP) < FOX_HEADS, EPS * FOX_DIM, EPS)[:, None])
    for b in range(2 * FOX_BLOCKS):
        gain = a["fox_q_norm_g" if b < FOX_BLOCKS else "fox_k_norm_g"][0]
        put("qk", np.concatenate([gain, gain])[:, None], b)
    for n, c in enumerate(gdn_cols):
        put("gdn_taps", a["gdn_conv_w"][0][:, c:c + P].T, GDN_TAPS * n)
    for b in range(FF_BLOCKS):
        for s in range(2):
            c = s * D_FF + b * P
            put("ffn_taps", a["ffn_conv_w"][0][:, c:c + P].T, FFN_TAPS * (2 * b + s))
    return {"x_t": x_t, "w_small": np.ascontiguousarray(rows(small)), "w_units": w_units, "params": prm,
            "consts": constants(), "selects": row_selections()}


def kernel(**inputs):
    import concourse.bacc as bacc
    from concourse.bass_utils import run_bass_kernel_spmd

    nc = bacc.Bacc("TRN2", target_bir_lowering=False, num_devices=1)
    arrays = {f"in_{k}": v for k, v in lay_out(inputs).items()}
    args = [nc.dram_tensor(k, v.shape, mybir.dt.from_np(v.dtype), kind="ExternalInput").ap()
            for k, v in arrays.items()]
    out = nc.dram_tensor("out_y", (KD, P, SEQ), F32, kind="ExternalOutput").ap()
    build_trunk(nc, *args, out)
    r = run_bass_kernel_spmd(nc, [arrays], core_ids=[0])
    return np.ascontiguousarray(r.results[0]["out_y"].reshape(1, D, SEQ).transpose(0, 2, 1))
```

```python
from contextlib import ExitStack

import numpy as np

import concourse.bass as bass
import concourse.mybir as mybir

F32 = mybir.dt.float32
F32R = mybir.dt.float32r
ACT = mybir.ActivationFunctionType
ALU = mybir.AluOpType
AX = mybir.AxisListType

P = 128
D = 1024
SEQ = 512
N_META = 16
L = SEQ + N_META
HL = L // 2
T = 88
NT = L // T
TH = NT // 2
KD = D // P
EPS = 1e-6
FOX_HEADS, FOX_DIM = 8, 64
FOX_BLOCKS = FOX_HEADS * FOX_DIM // P
HEADS, DH = 8, 128
HH = HEADS // 2
D_FF = 2816
FF_BLOCKS = D_FF // P
GDN_TAPS, FFN_TAPS = 4, 3
X_PARTS = 4
UNIT = KD * P

U_QK = 0
U_V = U_QK + 2 * FOX_BLOCKS
U_GDN = U_V + FOX_BLOCKS
U_Z = U_GDN + 3 * HEADS
U_MIX = U_Z + HEADS
MIX_UNITS = 4
U_OUT = U_MIX + MIX_UNITS * KD
U_UP = U_OUT + KD
U_DOWN = U_UP + 2 * FF_BLOCKS
DOWN_UNITS = 3
N_UNITS = U_DOWN + DOWN_UNITS * KD

R_F, R_B, R_G, R_END = 0, 32, 64, 96
R_GRP = 32
R_BE, S_END = 96, 128
O_ROW = 2 * HH
SELECTS = O_ROW + HH
LEVELS = [2, 4, 8, 16, 32, 64]
MASKED = [n for n in LEVELS if n < 32]


def side_by_side(widths):
    at, out = 0, {}
    for name, w in widths:
        out[name] = at
        at += w
    return out, at


CONST, C_COLS = side_by_side([("ident", P), ("row_of", 2 * R_GRP), ("row_of64", 2 * R_GRP),
                              ("incl", T), ("pair", T), ("neg", T), ("levels", len(MASKED) * T)])
PARAM, P_COLS = side_by_side([("norm1", KD), ("norm2", KD), ("gdn_norm", 1), ("stat_bias", 1), ("stat_sign", 1),
                              ("a_log", 1), ("eps", 1), ("n_scale", 1), ("n_bias", 1),
                              ("qk_scale", 1), ("qk_bias", 1), ("qk", 2 * FOX_BLOCKS),
                              ("gdn_taps", GDN_TAPS * 3 * HEADS), ("ffn_taps", FFN_TAPS * 2 * FF_BLOCKS)])


def build_trunk(nc, x_t, w_small, w_units, params, consts, selects, out_t):
    ctx = ExitStack()
    with ctx:
        def sb(scope, name, shape, dt=F32):
            return scope.enter_context(nc.sbuf_tensor(name, shape, dt))

        sems = {}

        def sem(name):
            if name not in sems:
                sems[name] = ctx.enter_context(nc.semaphore(name))
            return sems[name]

        cst = sb(ctx, "cst", [P, C_COLS])
        prm = sb(ctx, "prm", [P, P_COLS])
        ones = sb(ctx, "ones", [P, P])
        w_raw = sb(ctx, "w_raw", [P, 2, UNIT])
        w_hi = sb(ctx, "w_hi", [P, 2, UNIT], F32R)
        w_lo = sb(ctx, "w_lo", [P, 2, UNIT], F32R)
        h_hi = sb(ctx, "h_hi", [P, KD, L], F32R)
        h_lo = sb(ctx, "h_lo", [P, KD, L], F32R)
        sel_r = sb(ctx, "sel_r", [P, SELECTS, P], F32R)
        with ExitStack() as mixing:
            fox_o = sb(mixing, "fox_o", [P, FOX_BLOCKS, L])
            o_raw = sb(mixing, "o_raw", [P, HEADS, L])
            tok = sb(mixing, "tok", [T, NT, S_END])
            with ExitStack() as rows:
                g_hl = sb(rows, "g_hl", [2 * R_GRP, L], F32R)
                b_hl = sb(rows, "b_hl", [2 * R_GRP, L], F32R)
                with ExitStack() as first_half:
                    qkv0 = sb(first_half, "qkv0", [P, 3 * HH, L])
                    conv_in = sb(first_half, "conv_in", [P, 2, GDN_TAPS - 1 + L])
                    conv_out = sb(first_half, "conv_out", [P, L])
                    tanh_out = sb(first_half, "tanh_out", [P, L])
                    with ExitStack() as fox:
                        st = [sb(fox, f"st{i}", [R_END, L]) for i in range(4)]
                        stat = sb(fox, "stat", [S_END, L])
                        f_sum = sb(fox, "f_sum", [R_GRP, L])
                        nf_sum = sb(fox, "nf_sum", [R_GRP, L])
                        nf_hl = sb(fox, "nf_hl", [P, L], F32R)
                        coef = sb(fox, "coef", [R_END, 2])
                        sel_qk = sb(fox, "sel_qk", [2 * R_GRP, 2 * FOX_BLOCKS, P], F32R)
                        ident_r = sb(fox, "ident_r", [T, T], F32R)
                        neg_r = sb(fox, "neg_r", [T, T], F32R)
                        with ExitStack() as early:
                            x_in = sb(early, "x_in", [P, KD, L])
                            sq = sb(early, "sq", [P, 3, L])
                            root1 = sb(early, "root1", [P, L])
                            h32 = sb(early, "h32", [P, 2, L])
                            small_raw = sb(early, "small_raw", [P, KD, R_END])
                            small_hi = sb(early, "small_hi", [P, KD, R_END], F32R)
                            small_lo = sb(early, "small_lo", [P, KD, R_END], F32R)
                            sel_raw = sb(early, "sel_raw", [P, SELECTS + 2 * FOX_BLOCKS, P])
                        qk = sb(fox, "qk", [P, 2 * FOX_BLOCKS, L])
                        v_tok = sb(fox, "v_tok", [T, NT, FOX_HEADS * FOX_DIM])
                        v_chan = sb(fox, "v_chan", [P, 2, L])
                        qk_sq = sb(fox, "qk_sq", [P, 2, L])
                        qk_root = sb(fox, "qk_root", [R_GRP, L])
                        qk_hl = sb(fox, "qk_hl", [2 * R_GRP, L], F32R)
                        prob = sb(fox, "prob", [T, 3, L])
                        prob_t = sb(fox, "prob_t", [T, 2, L])
                        neg_max = sb(fox, "neg_max", [T, NT * FOX_HEADS])
                        p_sum = sb(fox, "p_sum", [T, NT * FOX_HEADS])
                        p_rec = sb(fox, "p_rec", [T, NT * FOX_HEADS])
                    qkv1 = sb(first_half, "qkv1", [P, 3 * HH, L])
                    work = sb(first_half, "work", [P, 2, L])
                    n_root = sb(first_half, "n_root", [R_GRP, L])
                    n_hl = sb(first_half, "n_hl", [2 * R_GRP, L], F32R)
                    g_end = sb(first_half, "g_end", [P, HH, NT])
                    a_t = sb(first_half, "a_t", [T, NT, HH, T])
                    inv_t = sb(first_half, "inv_t", [T, NT, HH, T])
                    with ExitStack() as inverse:
                        decay = sb(inverse, "decay", [T, NT, T])
                        m_t = sb(inverse, "m_t", [T, NT, HH, T])
                        inv = sb(inverse, "inv", [T, NT, HH, T])
                        mx = sb(inverse, "mx", [T, 3, HH, T])
                    v_b = sb(first_half, "v_b", [T, 2, HH, DH])
                    k_d = sb(first_half, "k_d", [T, 2, HH, DH])
                    state = sb(first_half, "state", [P, 2, HH, DH])
                    resid = sb(first_half, "resid", [T, HH, DH])
                    u_new = sb(first_half, "u_new", [T, HH, DH])
            gate_a = sb(mixing, "gate_a", [P, L])
            gate_b = sb(mixing, "gate_b", [P, L])
            z = sb(mixing, "z", [P, HEADS, L])
            fox_hi = sb(mixing, "fox_hi", [P, FOX_BLOCKS, L], F32R)
            fox_lo = sb(mixing, "fox_lo", [P, FOX_BLOCKS, L], F32R)
            ob_hi = sb(mixing, "ob_hi", [P, HEADS, L], F32R)
            ob_lo = sb(mixing, "ob_lo", [P, HEADS, L], F32R)
            mix_hi = sb(mixing, "mix_hi", [P, KD, L], F32R)
            mix_lo = sb(mixing, "mix_lo", [P, KD, L], F32R)
            zg = sb(mixing, "zg", [P, 2, L])
        x_res = sb(ctx, "x_res", [P, KD, L])
        u_hi = sb(ctx, "u_hi", [P, FF_BLOCKS, L], F32R)
        u_lo = sb(ctx, "u_lo", [P, FF_BLOCKS, L], F32R)
        ff_in = sb(ctx, "ff_in", [P, 2, FFN_TAPS - 1 + L])
        ff_conv = sb(ctx, "ff_conv", [P, 2, L])
        ff_silu = sb(ctx, "ff_silu", [P, L])
        ff_u = sb(ctx, "ff_u", [P, 2, L])
        y_out = sb(ctx, "y_out", [P, 2, L])
        r_norm2 = sb(ctx, "r_norm2", [P, L])
        ps = ctx.enter_context(nc.psum_tensor("ps", [P, 8, 512], F32))

        def const(name, rows=P, cols=None, base=0):
            at = CONST[name]
            width = cols if cols else {"incl": T, "pair": T, "neg": T}.get(name, P)
            return cst[base:base + rows, at:at + width]

        def param(name, i=0, rows=P):
            return prm[0:rows, bass.ds(i + PARAM[name], 1)]

        def pair(a, rows=P):
            return ps[0:rows, 2 * a:2 * a + 2, 0:HL]

        def halves(ap):
            return ap.rearrange("p (h n) -> p h n", h=2)

        def tiles_of(ap, w):
            return ap.rearrange("p h (t c) -> p h t c", c=w)

        def block_of(buf, i):
            return buf[:, bass.ds(i, 1), :].rearrange("p o (h n) -> p (o h) n", h=2)

        def flat(buf, i):
            return buf[:, bass.ds(i, 1), :].rearrange("p o n -> p (o n)")

        def over_heads(ap):
            return ap.unsqueeze(1).broadcast_to([T, HH, T])

        def level_mask(n):
            at = CONST["levels"] + n * T
            return cst[0:T, at:at + T]

        def row_of(n, name="row_of", width=1):
            at = CONST[name] + R_GRP - 1 - n * width
            return cst[:, at:at + R_GRP]

        W_LOADED = [sem("w_loaded0"), sem("w_loaded1")]
        HI_READY, LO_READY = sem("hi_ready"), sem("lo_ready")
        UNIT_USED = sem("unit_used")
        ACC_FREE = [sem("acc_free0"), sem("acc_free1")]

        def split_hi(act, p, s, first=False):
            act.wait_ge(W_LOADED[s], p * 16 + 16)
            if not first:
                act.wait_ge(UNIT_USED, p * 2 + (s - 1))
            nc.scalar.copy(w_hi[:, s, :], w_raw[:, s, :]).then_inc(HI_READY, 1)

        def split_lo(dve, p, s):
            dve.wait_ge(HI_READY, p * 2 + (s + 1))
            nc.vector.tensor_tensor(w_lo[:, s, :], w_raw[:, s, :], w_hi[:, s, :].bitcast(F32),
                                    ALU.subtract).then_inc(LO_READY, 1)

        def products(acc, s, hi, lo, tiles, start, stop, at=0):
            for k in range(tiles):
                for n, (w, x) in enumerate(((w_hi, hi), (w_hi, lo), (w_lo, hi))):
                    for half in range(2):
                        mm = nc.tensor.matmul(
                            ps[:, 2 * acc + half, 0:HL], w[:, s, k * P:(k + 1) * P],
                            x[:, at + k, half * HL:(half + 1) * HL],
                            start=start and k == 0 and n == 0, stop=stop and k == tiles - 1 and n == 2)
            return mm

        def sums(stationary, buf, s, bank):
            for half in range(2):
                mm = nc.tensor.matmul(ps[:, bank + half, 0:HL], stationary, buf[:, s, half * HL:(half + 1) * HL],
                                      start=True, stop=True)
            return mm

        def spread(bank, select, rows):
            for half in range(2):
                mm = nc.tensor.matmul(ps[:, bank + half, 0:HL], select, rows[:, half * HL:(half + 1) * HL],
                                      start=True, stop=True)
            return mm

        def weave(first, count, quarter):
            calls = [0]

            def fill(times=1):
                for _ in range(times):
                    b, q = divmod(calls[0], 4)
                    if calls[0] < 4 * count + 6:
                        quarter(first + b, q, b < count, 1 <= b <= count, 2 <= b)
                        calls[0] += 1

            def finish():
                fill(4 * count + 6 - calls[0])

            return fill, finish

        def woven_target(u):
            if u >= U_Z:
                return z[:, u - U_Z, :]
            return (qkv0 if u < U_GDN + 3 * HH else qkv1)[:, (u - U_GDN) % (3 * HH), :]

        GDN_FILLS = [dict(lead=0, sums=2, norm_wait=5, spread=2, head=3, turn=(2, 2), level=1, chunk=[2] * NT),
dict(lead=3, sums=12, norm_wait=3, spread=0, head=2, turn=(1, 0), level=1, chunk=[1] * NT)]
        first_calls = (GDN_FILLS[0]["lead"] + 2 * HH // GDN_FILLS[0]["sums"] + GDN_FILLS[0]["norm_wait"]
                       + GDN_FILLS[0]["spread"] + HH * GDN_FILLS[0]["head"] + sum(GDN_FILLS[0]["turn"])
                       + len(LEVELS) * GDN_FILLS[0]["level"] + sum(GDN_FILLS[0]["chunk"]))
        fox_calls = 2 + 2 + FOX_HEADS * NT + 3
        assert 4 * (3 * HH + 1) + 2 <= fox_calls <= 4 * (3 * HH + 2) + 1
        assert fox_calls + first_calls <= 4 * (3 * HEADS + 1) < fox_calls + first_calls + GDN_FILLS[1]["lead"] - 1
        qk_rows = [("qk", n, n) for n in range(2 * HH)]
        out_rows = [("out", O_ROW + j, j) for j in range(HH)]
        NORM_GROUPS = [qk_rows, out_rows + qk_rows, out_rows]
        NORM_BEFORE = [0, len(qk_rows), 2 * len(qk_rows) + len(out_rows)]
        n_scan = (T - 1).bit_length()
        st_sum, to_end = st[1 + n_scan % 2], st[2 - n_scan % 2]

        def merged(n):
            return (slice(n, min(2 * n, T)), slice(0, n)) if n >= 32 else (slice(0, T), slice(0, T))

        def by_head(bank, rows, width):
            return ps[rows, bank, 0:HH * width].rearrange("p (j t) -> p j t", j=HH)

        QK_ORDER = [b + which * FOX_BLOCKS for b in range(FOX_BLOCKS) for which in range(2)]

        fox_items = [(h, t) for h in range(FOX_HEADS) for t in range(NT)]
        N = len(fox_items)
        PAIR_ITEMS = 2 * NT
        TURNS = NT * len(LEVELS)
        UPDATES = NT * (len(LEVELS) + 1)
        STEPS = NT - 1

        block = ctx.enter_context(nc.Block())

        @block.sync
        def _(sp):
            def load_unit(u, s):
                sp.dma_start(w_raw[:, s, :], w_units[bass.ds(u, 1)].rearrange("o p n -> p (o n)")
                             ).then_inc(W_LOADED[s], 16)

            for i in range(X_PARTS):
                at = slice(i * KD // X_PARTS, (i + 1) * KD // X_PARTS)
                sp.dma_start(x_in[:, at, :], x_t[:, at, :]).then_inc(sem(f"x_loaded{i}"), 16)
            sp.dma_start(small_raw[:], w_small).then_inc(sem("small_loaded"), 16)
            for s in range(2):
                load_unit(s, s)
            with sp.Fori(1, N_UNITS // 2) as p:
                for s in range(2):
                    sp.wait_ge(LO_READY, p * 2 + (s - 1))
                    load_unit(p * 2 + s, s)

        @block.gpsimd
        def _(pool):
            pool.dma_start(prm[:], params).then_inc(sem("params_loaded"), 16)
            pool.wait_ge(sem(f"x_loaded{X_PARTS - 1}"), 16)
            pool.dma_start(cst[:], consts).then_inc(sem("const_loaded"), 16)
            pool.dma_start(sel_raw[:], selects).then_inc(sem("selects_loaded"), 16)
            for s in range(2):
                pool.wait_ge(HI_READY, s + 1)
                nc.gpsimd.tensor_tensor(w_lo[:, s, :], w_raw[:, s, :], w_hi[:, s, :].bitcast(F32),
                                        ALU.subtract).then_inc(LO_READY, 1)
            pool.wait_ge(LO_READY, U_GDN + 2)
            with pool.Fori(U_GDN // 2 + 1, U_MIX // 2 + 1) as p:
                for s in range(2):
                    pool.wait_ge(HI_READY, p * 2 + (s + 1))
                    nc.gpsimd.tensor_tensor(w_lo[:, s, :], w_raw[:, s, :], w_hi[:, s, :].bitcast(F32),
                                            ALU.subtract).then_inc(LO_READY, 1)
            pool.wait_ge(sem("fox_split"), 1)
            nc.gpsimd.tensor_tensor(fox_lo[:], fox_o[:], fox_hi[:].bitcast(F32), ALU.subtract
                                    ).then_inc(sem("fox_split"), 1)
            for n in range(HH, HEADS):
                pool.wait_ge(sem("o_normed"), n + 1)
                pool.wait_ge(sem("ob_lo"), max(n - 1, HH))
                nc.gpsimd.tensor_tensor(zg[:, n % 2, :], z[:, n, :], o_raw[:, n, :], ALU.mult
                                        ).then_inc(sem("gated"), 1)
            pool.wait_ge(sem("gated"), HEADS)
            pool.wait_ge(sem("fox_split"), 2)
            pool.dma_start(x_res[:], x_t).then_inc(sem("x_reloaded"), 16)
            for j in range(KD):
                pool.wait_ge(sem("y_ready"), j + 1)
                pool.dma_start(out_t[j], y_out[:, j % 2, N_META:L]).then_inc(sem(f"stored{j % 2}"), 16)
            for s in range(2):
                pool.wait_ge(sem(f"stored{s}"), 16 * KD // 2)

        @block.tensor
        def _(pe):
            def norm_sums(tag, buf):
                pe.wait_ge(sem(tag + "_summed"), KD)
                for half in range(2):
                    mm = nc.tensor.matmul(ps[:, 4 + half, 0:HL], ones[:], buf[:, half * HL:(half + 1) * HL],
                                          start=True, stop=True)
                mm.then_inc(sem(tag + "_total"), 1)

            def products_of_tile(acc, s, hi, lo, k):
                for n, (w, x) in enumerate(((w_hi, hi), (w_hi, lo), (w_lo, hi))):
                    for half in range(2):
                        mm = nc.tensor.matmul(ps[:, 2 * acc + half, 0:HL], w[:, s, k * P:(k + 1) * P],
                                              x[:, k, half * HL:(half + 1) * HL],
                                              start=(k == 0 and n == 0), stop=(k == KD - 1 and n == 2))
                return mm

            def dense_unit(p, s, hi, lo, slot_tiles=KD):
                pe.wait_ge(LO_READY, p * 2 + (s + 1))
                if not (isinstance(p, int) and p == 0):
                    pe.wait_ge(ACC_FREE[s], p)
                products(s, s, hi, lo, slot_tiles, True, True).then_inc(UNIT_USED, 1)

            def dense_loop(first, count, hi, lo):
                with pe.Fori(first // 2, (first + count) // 2) as p:
                    for s in range(2):
                        dense_unit(p, s, hi, lo)

            pe.wait_ge(sem("ones"), 1)
            norm_sums("n1", sq[:, 2, :])
            def stat_logits(k):
                for n, (w, x) in enumerate(((small_hi, h_hi), (small_hi, h_lo), (small_lo, h_hi))):
                    for half in range(2):
                        mm = nc.tensor.matmul(ps[0:R_END, 6 + half, 0:HL], w[:, k, :],
                                              x[:, k, half * HL:(half + 1) * HL],
                                              start=(k == 0 and n == 0), stop=(k == KD - 1 and n == 2))
                if k == KD - 1:
                    mm.then_inc(sem("small_done"), 1)

            def rising_pair(p, name, beside):
                for step in range(KD + 2):
                    for s, k in ((0, step), (1, step - 2)):
                        if k == 0:
                            pe.wait_ge(LO_READY, p * 2 + s + 1)
                            if p:
                                pe.wait_ge(ACC_FREE[s], p)
                        if s == 0 and k < KD:
                            pe.wait_ge(sem(name), k + 1)
                            beside(k)
                        if 0 <= k < KD:
                            mm = products_of_tile(s, s, h_hi, h_lo, k)
                        if k == KD - 1:
                            mm.then_inc(UNIT_USED, 1)

            pe.wait_ge(sem("small_lo"), 1)
            rising_pair(0, "n1_lo", stat_logits)

            def quarter(u, q, multiplies, takes, finishes):
                if not multiplies:
                    return
                if q == 0:
                    pe.wait_ge(LO_READY, u + 1)
                    pe.wait_ge(ACC_FREE[(u - 1) % 2], (u + 1) // 2)
                for k in range(q * KD // 4, (q + 1) * KD // 4):
                    mm = products_of_tile(0, u % 2, h_hi, h_lo, k)
                if q == 3:
                    mm.then_inc(UNIT_USED, 1)

            def row_sums(stationary, buf, s, first, last):
                for half in range(2):
                    mm = nc.tensor.matmul(ps[0:R_GRP, 2 + half, 0:HL], stationary,
                                          buf[:, s, half * HL:(half + 1) * HL], start=first, stop=last)
                return mm

            def qk_sums(n):
                pe.wait_ge(sem("qk_sq"), n + 1)
                for half in range(2):
                    mm = nc.tensor.matmul(ps[0:R_GRP, 4 + half, 0:HL], row_of(n, "row_of64", 2),
                                          qk_sq[:, n % 2, half * HL:(half + 1) * HL],
                                          start=(n == 0), stop=(n == 2 * FOX_BLOCKS - 1))
                mm.then_inc(sem("qk_sum"), 1)

            pe.wait_ge(sem("const_loaded"), 16)
            qk_sums(0)
            for n in range(2, 2 * FOX_BLOCKS):
                dense_unit(n // 2, n % 2, h_hi, h_lo)
                qk_sums(n - 1)

            pe.wait_ge(sem("stat_in"), 1)

            def turn_v(b):
                pe.wait_ge(ACC_FREE[b % 2], (U_V + b) // 2 + 1)
                if b:
                    pe.wait_ge(sem("v_tok"), b)
                for t in range(NT):
                    mm = nc.tensor.transpose(ps[0:T, 6 + t // TH, (t % TH) * P:(t % TH + 1) * P],
                                             v_chan[:, b % 2, t * T:(t + 1) * T], const("ident"))
                mm.then_inc(sem("v_turned"), 1)

            for b in range(FOX_BLOCKS):
                dense_unit((U_V + b) // 2, b % 2, h_hi, h_lo)
                if b:
                    turn_v(b - 1)
                else:
                    qk_sums(2 * FOX_BLOCKS - 1)
            fill, finish = weave(U_GDN, U_MIX - U_GDN, quarter)
            fill()
            turn_v(FOX_BLOCKS - 1)
            fill()

            pe.wait_ge(sem("qk_rooted"), 1)
            pe.wait_ge(sem("stat_rows"), 4)
            for t in range(NT):
                mm = nc.tensor.transpose(ps[0:T, 4 + t // TH, (t % TH) * S_END:(t % TH + 1) * S_END],
                                         stat[:, t * T:(t + 1) * T], const("ident"))
            mm.then_inc(sem("tok_turned"), 1)
            pe.wait_ge(sem("v_tok"), FOX_BLOCKS)
            pe.wait_ge(sem("qk_split"), 2)
            for i, n in enumerate(QK_ORDER):
                if i == 1:
                    pe.wait_ge(sem("tok_ready"), 1)
                if i >= 2:
                    pe.wait_ge(sem("qk_normed"), i - 1)
                spread(6 - 2 * (i % 2), sel_qk[:, n, :], qk_hl).then_inc(sem("qk_spread"), 1)
                if i % 4 == 1:
                    fill()

            pe.wait_ge(sem("qk_normed"), 2 * FOX_BLOCKS)
            pe.wait_ge(sem("nf_split"), 2)
            pe.wait_ge(sem("masks_r"), 3)
            pe.wait_ge(ACC_FREE[1], U_GDN // 2)

            def scores(n):
                h, t = fox_items[n]
                rows = slice(FOX_DIM * (h % 2), FOX_DIM * (h % 2) + FOX_DIM)
                keys = (t + 1) * T
                wide = keys > 512
                if n:
                    before = n if wide or t == 0 else n - 1
                    if before:
                        pe.wait_ge(sem("prob_ready"), before)
                at = slice(t * T, (t + 1) * T)
                for bank, k0, k1 in [(2, 0, HL), (3, HL, L)] if wide else [(2 + t % 2, 0, keys)]:
                    o = ps[0:T, bank, 0:k1 - k0]
                    last = k1 == keys
                    nc.tensor.matmul(o, qk[rows, h // 2, at], qk[rows, FOX_BLOCKS + h // 2, k0:k1],
                                     start=True, stop=False)
                    mm = nc.tensor.matmul(o, sel_r[:, h, 0:T], nf_hl[:, k0:k1], start=False, stop=not last)
                    if last:
                        mm = nc.tensor.matmul(ps[0:T, bank, k1 - k0 - T:k1 - k0], ident_r[:], neg_r[:],
                                              start=False, stop=True)
                mm.then_inc(sem("scored"), 1)

            def turn_probs(n):
                t = fox_items[n][1]
                pe.wait_ge(sem("prob_scaled"), n + 1)
                if n >= 1:
                    pe.wait_ge(sem("prob_t"), n)
                for j in range(t + 1):
                    mm = nc.tensor.transpose(ps[0:T, 4 + j // TH, (j % TH) * T:(j % TH + 1) * T],
                                             prob[:, n % 3, j * T:(j + 1) * T], const("ident", T, T))
                mm.then_inc(sem("prob_turned"), 1)

            def weigh_values(n):
                h, t = fox_items[n]
                pe.wait_ge(sem("prob_t"), n + 1)
                if n % PAIR_ITEMS == 0 and n:
                    pe.wait_ge(sem("fox_taken"), n // PAIR_ITEMS)
                r0 = FOX_DIM * (h % 2)
                o = ps[r0:r0 + FOX_DIM, 6 + t // TH, (t % TH) * T:(t % TH + 1) * T]
                for j in range(t + 1):
                    mm = nc.tensor.matmul(o, v_tok[:, j, h * FOX_DIM:(h + 1) * FOX_DIM],
                                          prob_t[:, n % 2, j * T:(j + 1) * T], start=(j == 0), stop=(j == t))
                mm.then_inc(sem("weighed"), 1)

            for n in range(N + 3):
                if n < N:
                    scores(n)
                fill()
                if 0 <= n - 2 < N:
                    turn_probs(n - 2)
                if 0 <= n - 3 < N:
                    weigh_values(n - 3)
            pe.wait_ge(sem("prob_ready"), N)
            pe.wait_ge(sem("fox_taken"), FOX_BLOCKS)

            def norm_group_sums(g, between, every):
                items = NORM_GROUPS[g]
                for i, (_, row, _) in enumerate(items):
                    pe.wait_ge(sem("n_sq"), NORM_BEFORE[g] + i + 1)
                    row_sums(row_of(row), work, i % 2, i == 0, i == len(items) - 1).then_inc(sem("n_sum"), 1)
                    if i % every == every - 1:
                        between()

            def spread_out_norm(j, half_no):
                if j >= 2:
                    pe.wait_ge(sem("o_normed"), half_no * HH + j - 1)
                spread(4 + 2 * (j % 2), sel_r[0:2 * R_GRP, O_ROW + j, :], n_hl).then_inc(sem("on_spread"), 1)

            for half_no, qkv in enumerate((qkv0, qkv1)):
                m0 = half_no * HH
                plan = GDN_FILLS[half_no]
                fill(plan["lead"])
                norm_group_sums(half_no, fill, plan["sums"])
                fill(plan["norm_wait"])
                pe.wait_ge(sem("n_split"), 2 * half_no + 2)
                for n in range(2 * HH):
                    if n >= 2:
                        pe.wait_ge(sem("gn_normed"), 2 * m0 + n - 1)
                    spread(4 + 2 * (n % 2), sel_r[0:2 * R_GRP, n, :], n_hl).then_inc(sem("gn_spread"), 1)
                    if n in (2, 5) and plan["spread"]:
                        fill()
                pe.wait_ge(sem("gn_normed"), 2 * m0 + 2 * HH)
                for j in range(HH):
                    m = m0 + j
                    if j:
                        pe.wait_ge(sem("e_g"), 2 * m)
                        pe.wait_ge(sem("decay_diff"), m)
                    spread(2, sel_r[0:2 * R_GRP, m, :], g_hl).then_inc(sem("spread"), 1)
                    if j:
                        pe.wait_ge(sem("mat_taken"), 2 * m)
                    spread(4, sel_r[0:2 * R_GRP, m, :], b_hl).then_inc(sem("spread"), 1)
                    fill()
                    pe.wait_ge(sem("k_b"), m + 1)
                    for which in range(2):
                        for t in range(NT):
                            at = slice(t * T, (t + 1) * T)
                            mm = nc.tensor.matmul(
                                ps[0:T, 6 - 2 * which + t // TH, (t % TH) * T:(t % TH + 1) * T],
                                qkv[:, HH + j, at], work[:, 0, at] if which else qkv[:, j, at],
                                start=True, stop=True)
                        mm.then_inc(sem("mats"), 1)
                    fill(plan["head"] - 1)

                def turn_inv(c, bank):
                    for j in range(HH):
                        mm = nc.tensor.transpose(ps[0:T, bank, j * T:(j + 1) * T], inv_t[:, c, j, :],
                                                 const("ident", T, T))
                    mm.then_inc(sem("inv_turned"), 1)

                turned, updated = half_no * TURNS, half_no * UPDATES
                pe.wait_ge(sem("mat_taken"), 2 * (m0 + HH))
                pe.wait_ge(sem("e_g"), 2 * (m0 + HH))
                pe.wait_ge(sem("decay_diff"), m0 + HH)
                if half_no:
                    for j in range(HH):
                        spread_out_norm(j, 0)
                    pe.wait_ge(sem("o_normed"), HH)
                fill(plan["turn"][0])
                for c in range(NT):
                    pe.wait_ge(sem("inv_t"), updated + c + 1)
                    if c >= 2:
                        pe.wait_ge(sem("inv"), turned + c - 1)
                    turn_inv(c, 6 + c % 2)
                    if c % 2 and c // 2 < plan["turn"][1]:
                        fill()
                for lv in range(len(LEVELS)):
                    rows, cols = merged(LEVELS[lv])
                    for step in range(NT + 4):
                        if step < NT:
                            c, n = step, lv * NT + step
                            pe.wait_ge(sem("inv"), turned + n + 1)
                            if n >= 2:
                                pe.wait_ge(sem("mx"), turned + n - 1)
                            for j in range(HH):
                                mm = nc.tensor.matmul(by_head(2 + n % 2, rows, cols.stop)[:, j, :],
                                                      m_t[cols, c, j, rows], inv[cols, c, j, cols],
                                                      start=True, stop=True)
                            mm.then_inc(sem("mx_done"), 1)
                        if 0 <= step - 2 < NT:
                            c, n = step - 2, lv * NT + step - 2
                            pe.wait_ge(sem("mx"), turned + n + 1)
                            if n >= 2:
                                pe.wait_ge(sem("inv_t"), updated + NT + n - 1)
                            for j in range(HH):
                                mm = nc.tensor.matmul(by_head(4 + n % 2, cols, rows.stop - rows.start)[:, j, :],
                                                      mx[rows, n % 3, j, cols], inv_t[rows, c, j, rows],
                                                      start=True, stop=True)
                            mm.then_inc(sem("change"), 1)
                        if 0 <= step - 4 < NT and lv < len(LEVELS) - 1:
                            c, n = step - 4, lv * NT + step - 4
                            pe.wait_ge(sem("inv_t"), updated + NT + n + 1)
                            pe.wait_ge(sem("inv"), turned + NT + n - 1)
                            turn_inv(c, 6 + n % 2)
                        if step == NT + 1:
                            fill(plan["level"])
                pe.wait_ge(sem("inv_t"), updated + UPDATES)
                pe.wait_ge(sem("inv"), turned + TURNS)
                pe.wait_ge(sem("q_g"), m0 + HH)

                def turn_block(c, which):
                    n = half_no * NT + c
                    if 2 * n + which:
                        pe.wait_ge(sem("vk_taken"), 2 * n + which)
                    for j in range(HH):
                        mm = nc.tensor.transpose(ps[0:T, 7, j * P:(j + 1) * P],
                                                 qkv[:, (HH if which else 2 * HH) + j, c * T:(c + 1) * T],
                                                 const("ident"))
                    mm.then_inc(sem("vk_turned"), 1)

                for which in range(2):
                    turn_block(0, which)
                for c in range(NT):
                    n = half_no * NT + c
                    at = slice(c * T, (c + 1) * T)
                    if c:
                        for j in range(HH):
                            pe.wait_ge(sem("state"), (half_no * STEPS + c - 1) * HH + j + 1)
                            mm = nc.tensor.matmul(ps[0:T, 2, j * DH:(j + 1) * DH], qkv[:, HH + j, at],
                                                  state[:, c % 2, j, :], start=True, stop=True)
                        mm.then_inc(sem("ks_done"), 1)
                    if c + 1 < NT:
                        turn_block(c + 1, 0)
                    if not c:
                        pe.wait_ge(sem("vk_taken"), 2 * n + 2)
                    for j in range(HH):
                        if c:
                            pe.wait_ge(sem("resid"), (half_no * STEPS + c - 1) * HH + j + 1)
                        mm = nc.tensor.matmul(ps[0:T, 3, j * DH:(j + 1) * DH], inv_t[:, c, j, :],
                                              resid[:, j, :] if c else v_b[:, 0, j, :], start=True, stop=True)
                    mm.then_inc(sem("u_done"), 1)
                    if c + 1 < NT:
                        turn_block(c + 1, 1)
                    fill()
                    pe.wait_ge(sem("u_new"), n + 1)
                    if c + 1 < NT:
                        pe.wait_ge(sem("vk_taken"), 2 * n + 2)
                        for j in range(HH):
                            mm = nc.tensor.matmul(ps[:, 4, j * DH:(j + 1) * DH], k_d[:, c % 2, j, :], u_new[:, j, :],
                                                  start=True, stop=True)
                        mm.then_inc(sem("grown"), 1)
                    if c >= 2:
                        pe.wait_ge(sem("o_raw"), n - 1)
                    for j in range(HH):
                        o = ps[:, 5 + c % 2, j * T:(j + 1) * T]
                        if c:
                            nc.tensor.matmul(o, state[:, c % 2, j, :], qkv[:, j, at], start=True, stop=False)
                        mm = nc.tensor.matmul(o, u_new[:, j, :], a_t[:, c, j, :], start=(c == 0), stop=True)
                    mm.then_inc(sem("o_done"), 1)
                    fill(plan["chunk"][c] - 1)
                pe.wait_ge(sem("o_raw"), (half_no + 1) * NT)
            finish()
            pe.wait_ge(ACC_FREE[1], U_MIX // 2)

            norm_group_sums(2, lambda: None, 1)
            p = U_MIX // 2
            dense_unit(p, 0, h_hi, h_lo)
            pe.wait_ge(sem("n_rooted"), 3)
            pe.wait_ge(LO_READY, p * 2 + 2)
            for k in range(KD):
                mm = products_of_tile(1, 1, h_hi, h_lo, k)
                if k in (3, 5):
                    if k == 3:
                        pe.wait_ge(sem("n_split"), 6)
                    for j in range(k - 3, k - 1):
                        spread_out_norm(j, 1)
            mm.then_inc(UNIT_USED, 1)

            def branches(p, first):
                if first:
                    pe.wait_ge(LO_READY, p * 2 + 3)
                    pe.wait_ge(ACC_FREE[0], p + 1)
                    for k in range(HEADS):
                        pe.wait_ge(sem("ob_lo"), k + 1)
                        mm = products_of_tile(0, 0, ob_hi, ob_lo, k)
                    mm.then_inc(UNIT_USED, 1)
                else:
                    dense_unit(p + 1, 0, ob_hi, ob_lo)
                pe.wait_ge(sem("fox_split"), 2)
                dense_unit(p + 1, 1, fox_hi, fox_lo, FOX_BLOCKS)

            branches(p, True)
            with pe.Fori(U_MIX // 2 + 2, U_OUT // 2 - 1, 2) as p:
                for s in range(2):
                    dense_unit(p, s, h_hi, h_lo)
                branches(p, False)
            pe.wait_ge(LO_READY, U_OUT + 1)
            pe.wait_ge(ACC_FREE[0], U_OUT // 2)
            for k in range(KD):
                pe.wait_ge(sem("mix_lo"), k + 1)
                mm = products_of_tile(0, 0, mix_hi, mix_lo, k)
            mm.then_inc(UNIT_USED, 1)
            dense_unit(U_OUT // 2, 1, mix_hi, mix_lo)
            dense_loop(U_OUT + 2, KD - 2, mix_hi, mix_lo)

            rising_pair(U_UP // 2, "n2_lo", lambda k: norm_sums("n2", z[:, 2, :]) if k == 5 else None)
            dense_loop(U_UP + 2, 2 * FF_BLOCKS - 2, h_hi, h_lo)
            pe.wait_ge(sem("u_lo"), (DOWN_UNITS - 1) * KD)
            with pe.Fori(0, KD // 2) as q:
                for s in range(2):
                    pe.wait_ge(ACC_FREE[s], q + U_DOWN // 2)
                    for part in range(DOWN_UNITS):
                        n = s * DOWN_UNITS + part
                        if part == DOWN_UNITS - 1:
                            pe.wait_ge(sem("u_lo"), FF_BLOCKS)
                        pe.wait_ge(LO_READY, q * 2 * DOWN_UNITS + (U_DOWN + n + 1))
                        tiles = min(KD, FF_BLOCKS - part * KD)
                        mm = products(s, n % 2, u_hi, u_lo, tiles, part == 0, part == DOWN_UNITS - 1, at=part * KD)
                        mm.then_inc(UNIT_USED, 1)

        @block.scalar
        def _(act):
            def norm_root(tag, root):
                act.wait_ge(sem(tag + "_total"), 1)
                nc.scalar.activation(halves(root), pair(2), ACT.Sqrt, bias=param("eps"),
                                     scale=1.0 / D).then_inc(sem(tag + "_rooted"), 1)

            def norm_hi(tag, h):
                for k in range(KD):
                    act.wait_ge(sem(tag + "_h"), k + 1)
                    nc.scalar.copy(h_hi[:, k, :], h[:, k % 2, :]).then_inc(sem(tag + "_hi"), 1)

            act.wait_ge(sem("params_loaded"), 16)
            for k in range(KD):
                if k % (KD // X_PARTS) == 0:
                    act.wait_ge(sem(f"x_loaded{k * X_PARTS // KD}"), 16)
                if k >= 2:
                    act.wait_ge(sem("n1_summed"), k - 1)
                nc.scalar.activation(sq[:, k % 2, :], x_in[:, k, :], ACT.Square).then_inc(sem("n1_sq"), 1)
            norm_root("n1", root1[:])
            for s in range(2):
                split_hi(act, 0, s, first=True)
            act.wait_ge(sem("small_loaded"), 16)
            nc.scalar.copy(small_hi[:], small_raw[:]).then_inc(sem("small_hi"), 1)
            norm_hi("n1", h32)

            def split_rows(src, dst, base, name):
                nc.scalar.copy(dst[base:base + R_GRP, :], src).then_inc(sem(name), 1)

            act.wait_ge(sem("n1_lo"), KD)
            act.wait_ge(sem("small_done"), 1)
            act.wait_ge(sem("small_lo"), 1)
            act.wait_ge(sem("const_loaded"), 16)
            act.wait_ge(sem("selects_loaded"), 16)
            nc.scalar.copy(sel_r[:], sel_raw[:, 0:SELECTS, :]).then_inc(sem("selects"), 1)
            nc.scalar.copy(sel_qk[:], sel_raw[0:2 * R_GRP, SELECTS:, :]).then_inc(sem("selects"), 1)
            act.wait_ge(sem("selects"), 2)
            for n in range(2 * FOX_BLOCKS):
                act.wait_ge(UNIT_USED, n + 1)
                nc.scalar.copy(halves(qk[:, n, :]), pair(n % 2)).then_inc(sem("qk_raw"), 1)
                if n >= 2:
                    act.wait_ge(sem("qk_sum"), n - 1)
                nc.scalar.activation(halves(qk_sq[:, n % 2, :]), pair(n % 2), ACT.Square).then_inc(sem("qk_sq"), 1)
                act.wait_ge(sem("qk_sq"), n + 1)
                nc.scalar.sem_inc(ACC_FREE[n % 2], 1)
                split_hi(act, n // 2 + 1, n % 2)
                if n == 2:
                    nc.scalar.copy(ident_r[:], const("ident", T, T)).then_inc(sem("masks_r"), 1)
                    nc.scalar.copy(neg_r[:], const("neg", T)).then_inc(sem("masks_r"), 1)
                if n == 3:
                    act.wait_ge(sem("stat_in"), 1)
                    nc.scalar.activation(st[1][:], st[0][:], ACT.Abs).then_inc(sem("stat_abs"), 1)
                    act.wait_ge(sem("stat_abs"), 1)
                    nc.scalar.activation(st[2][:], st[1][:], ACT.Exp, scale=-1.0).then_inc(sem("stat_exp"), 1)
                    nc.scalar.activation(st[3][R_B:R_G, :], st[0][R_B:R_G, :], ACT.Exp).then_inc(sem("beta_exp"), 1)
                    nc.scalar.activation(coef[:, 0:1], param("a_log", rows=R_END), ACT.Exp).then_inc(sem("coef"), 1)
                    act.wait_ge(sem("stat_exp"), 1)
                    nc.scalar.activation(st[1][:], st[2][:], ACT.Ln, bias=1.0).then_inc(sem("stat_ln"), 1)

            for b in range(FOX_BLOCKS):
                p, s = (U_V + b) // 2, b % 2
                act.wait_ge(UNIT_USED, U_V + b + 1)
                if b >= 2:
                    act.wait_ge(sem("v_turned"), b - 1)
                nc.scalar.copy(halves(v_chan[:, s, :]), pair(s)).then_inc(ACC_FREE[s], 1)
                split_hi(act, p + 1, s)
                if b == 0:
                    act.wait_ge(sem("qk_sum"), 2 * FOX_BLOCKS)
                    nc.scalar.activation(halves(qk_root[:]), pair(2, R_GRP), ACT.Sqrt,
                                         bias=param("qk_bias", rows=R_GRP), scale=param("qk_scale", rows=R_GRP)
                                         ).then_inc(sem("qk_rooted"), 1)
                if b == 1:
                    act.wait_ge(sem("qk_rec"), 1)
                    split_rows(qk_root[:], qk_hl, 0, "qk_split")
                if b == 2:
                    act.wait_ge(sem("g_row"), 1)
                    act.wait_ge(sem("to_end"), 1)
                    nc.scalar.activation(st[3][R_B:R_G, :], stat[0:R_B, :], ACT.Exp).then_inc(sem("e_rows"), 1)
                    nc.scalar.activation(stat[R_G:R_END, :], to_end[R_G:R_END, :], ACT.Exp
                                         ).then_inc(sem("stat_rows"), 1)
                    split_rows(stat[0:R_B, :], g_hl, 0, "g_split")
                    split_rows(stat[R_B:R_G, :], b_hl, R_GRP, "b_split")
            act.wait_ge(sem("f_ready"), 1)
            split_rows(nf_sum[:], nf_hl, 0, "nf_split")

            def quarter(u, q, multiplies, takes, finishes):
                v = u - 1
                b = v - U_GDN
                if q == 1 and takes:
                    split_hi(act, (v + 2) // 2, v % 2)
                def finish_silu():
                    act.wait_ge(sem("conv"), b * GDN_TAPS)
                    if b >= 2:
                        act.wait_ge(sem("woven"), b - 1)
                    nc.scalar.activation(tanh_out[:], conv_out[:], ACT.Tanh).then_inc(sem("tanh"), 1)

                if q == 0 and v == U_Z:
                    finish_silu()
                if q == 0 and takes:
                    act.wait_ge(UNIT_USED, v + 1)
                    if v < U_Z:
                        if b >= 2:
                            act.wait_ge(sem("conv"), (b - 1) * GDN_TAPS)
                        nc.scalar.copy(halves(conv_in[:, b % 2, GDN_TAPS - 1:]), pair(0)
                                       ).then_inc(ACC_FREE[v % 2], 1)
                    else:
                        act.wait_ge(sem("woven"), b)
                        nc.scalar.activation(halves(conv_out[:]), pair(0), ACT.Copy, scale=0.5
                                             ).then_inc(sem("z_half"), 1)
                        act.wait_ge(sem("z_half"), v - U_Z + 1)
                        nc.scalar.activation(halves(tanh_out[:]), pair(0), ACT.Tanh, scale=0.5
                                             ).then_inc(ACC_FREE[v % 2], 1)
                if q == 0 and finishes and v < U_Z:
                    finish_silu()

            fill, finish = weave(U_GDN, U_MIX - U_GDN, quarter)
            act.wait_ge(sem("pads"), 1)
            fill(2)
            for i in range(2 * FOX_BLOCKS):
                if i % 4 == 1:
                    fill()

            def exponentials(n):
                t = fox_items[n][1]
                keys = (t + 1) * T
                act.wait_ge(sem("neg_max"), n + 1)
                if n >= 3:
                    act.wait_ge(sem("prob_turned"), n - 2)
                src, dst = (ps[0:T, 2 + t % 2, 0:keys], prob[:, n % 3, 0:keys]) if keys <= 512 else (
                    pair(1, T), halves(prob[:, n % 3, :]))
                nc.scalar.activation(dst, src, ACT.Exp, bias=neg_max[:, n:n + 1],
                                     accum_out=p_sum[:, n:n + 1]).then_inc(sem("prob_ready"), 1)

            def take_turned(n):
                keys = (fox_items[n][1] + 1) * T
                act.wait_ge(sem("prob_turned"), n + 1)
                if n >= 2:
                    act.wait_ge(sem("weighed"), n - 1)
                if keys <= HL:
                    mm = nc.scalar.copy(prob_t[:, n % 2, 0:keys], ps[0:T, 4, 0:keys])
                else:
                    nc.scalar.copy(prob_t[:, n % 2, 0:HL], ps[0:T, 4, 0:HL])
                    mm = nc.scalar.copy(prob_t[:, n % 2, HL:keys], ps[0:T, 5, 0:keys - HL])
                mm.then_inc(sem("prob_t"), 1)

            for n in range(N + 3):
                fill()
                if n < N:
                    exponentials(n)
                if 0 <= n - 2 < N:
                    take_turned(n - 2)

            act.wait_ge(sem("fox_taken"), FOX_BLOCKS)
            def norm_squares(g, qkv, between, every):
                for i, (what, _, j) in enumerate(NORM_GROUPS[g]):
                    if i >= 2:
                        act.wait_ge(sem("n_sum"), NORM_BEFORE[g] + i - 1)
                    if what == "qk":
                        act.wait_ge(sem("woven"), g * 3 * HH + j + 1)
                    src = qkv[:, j, :] if what == "qk" else o_raw[:, (g - 1) * HH + j, :]
                    nc.scalar.activation(work[:, i % 2, :], src, ACT.Square).then_inc(sem("n_sq"), 1)
                    if i % every == every - 1:
                        between()

            def group_root(g):
                act.wait_ge(sem("n_sum"), NORM_BEFORE[g] + len(NORM_GROUPS[g]))
                nc.scalar.activation(halves(n_root[:]), pair(1, R_GRP), ACT.Sqrt,
                                     bias=param("n_bias", rows=R_GRP), scale=param("n_scale", rows=R_GRP)
                                     ).then_inc(sem("n_rooted"), 1)

            def norm_split(g):
                act.wait_ge(sem("n_rec"), g + 1)
                split_rows(n_root[:], n_hl, 0, "n_split")

            for half_no, qkv in enumerate((qkv0, qkv1)):
                m0 = half_no * HH
                plan = GDN_FILLS[half_no]
                fill(plan["lead"])
                norm_squares(half_no, qkv, fill, plan["sums"])
                group_root(half_no)
                fill(1)
                norm_split(half_no)
                fill(plan["norm_wait"] - 1)
                for n in range(2 * HH):
                    if n in (2, 5) and plan["spread"]:
                        fill()
                act.wait_ge(sem("gn_normed"), 2 * m0 + 1)
                for j in range(HH):
                    m = m0 + j
                    act.wait_ge(sem("spread"), 2 * m + 1)
                    if j:
                        act.wait_ge(sem("q_g"), m)
                    nc.scalar.activation(halves(work[:, 1, :]), pair(1), ACT.Exp).then_inc(sem("e_g"), 1)
                    nc.scalar.activation(g_end[:, j, :].rearrange("p (h t) -> p h t", h=2),
                                         pair(1)[:, :, T - 1::T], ACT.Exp).then_inc(sem("e_g"), 1)
                    fill()
                    act.wait_ge(sem("decay_diff"), m + 1)
                    nc.scalar.activation(decay[:], decay[:], ACT.Relu).then_inc(sem("decay_relu"), 1)
                    act.wait_ge(sem("decay_relu"), m + 1)
                    nc.scalar.activation(decay[:], decay[:], ACT.Exp, scale=-1.0).then_inc(sem("decay_exp"), 1)
                    fill(plan["head"] - 1)
                turned = half_no * TURNS

                def take_inv(c, n):
                    act.wait_ge(sem("inv_turned"), turned + n + 1)
                    nc.scalar.copy(inv[:, c, :, :].rearrange("p j t -> p (j t)"), ps[0:T, 6 + n % 2, 0:HH * T]
                                   ).then_inc(sem("inv"), 1)

                fill(plan["turn"][0])
                for c in range(NT):
                    take_inv(c, c)
                    if c % 2 and c // 2 < plan["turn"][1]:
                        fill()
                for lv in range(len(LEVELS)):
                    for step in range(NT + 4):
                        if 0 <= step - 4 < NT and lv < len(LEVELS) - 1:
                            c = step - 4
                            take_inv(c, (lv + 1) * NT + c)
                        if step == NT + 1:
                            fill(plan["level"])
                for c in range(NT):
                    n = half_no * NT + c
                    act.wait_ge(sem("u_done"), n + 1)
                    if n:
                        act.wait_ge(sem("o_done"), n)
                    nc.scalar.copy(u_new[:].rearrange("p j d -> p (j d)"), ps[0:T, 3, :]).then_inc(sem("u_new"), 1)
                    fill()
                    act.wait_ge(sem("o_done"), n + 1)
                    nc.scalar.copy(o_raw[:, m0:m0 + HH, c * T:(c + 1) * T],
                                   ps[:, 5 + c % 2, 0:HH * T].rearrange("p (j t) -> p j t", j=HH)
                                   ).then_inc(sem("o_raw"), 1)
                    fill(plan["chunk"][c] - 1)
                act.wait_ge(sem("o_raw"), (half_no + 1) * NT)
            finish()
            act.wait_ge(sem("woven"), 3 * HEADS + HEADS)

            def split_ob(first, end):
                for n in range(first, end):
                    act.wait_ge(sem("gated"), n + 1)
                    nc.scalar.copy(ob_hi[:, n, :], zg[:, n % 2, :]).then_inc(sem("ob_hi"), 1)

            norm_squares(2, None, lambda: None, 1)
            group_root(2)
            nc.scalar.copy(fox_hi[:], fox_o[:]).then_inc(sem("fox_split"), 1)
            norm_split(2)
            split_ob(0, HH // 2)

            def mixing_block(p, j, first):
                for s, gate in enumerate((gate_a, gate_b)):
                    act.wait_ge(UNIT_USED, p * 2 + (s + 1))
                    if not first:
                        act.wait_ge(sem("mix_lo"), j)
                    nc.scalar.activation(halves(gate[:]), pair(s), ACT.Tanh, scale=0.5).then_inc(ACC_FREE[s], 1)
                    split_hi(act, p + 1, s)
                    if first:
                        split_ob(*((HH // 2, HH), (HH, HEADS))[s])
                for s in range(2):
                    split_hi(act, p + 2, s)
                act.wait_ge(sem("mixed"), j + 1)
                nc.scalar.activation(flat(mix_hi, j), gate_a[:], ACT.Copy, scale=0.5).then_inc(sem("mix_hi"), 1)

            mixing_block(U_MIX // 2, 0, True)
            with act.Fori(1, KD) as j:
                mixing_block(j * (MIX_UNITS // 2) + U_MIX // 2, j, False)

            def square_block(p, s, first):
                split_hi(act, p + (U_OUT // 2 + 1), s)
                act.wait_ge(ACC_FREE[s], p + (U_OUT // 2 + 1))
                if not first:
                    act.wait_ge(sem("n2_summed"), p * 2 + (s - 1))
                nc.scalar.activation(z[:, s, :], flat(x_res, p * 2 + s), ACT.Square).then_inc(sem("n2_sq"), 1)
                if not first:
                    act.wait_ge(sem("n2_lo"), p * 2 + (s - 1))
                nc.scalar.activation(z[:, 3 + s, :], flat(x_res, p * 2 + s), ACT.Copy,
                                     scale=param("norm2", p * 2 + s)).then_inc(sem("n2_h"), 1)
                act.wait_ge(sem("n2_h"), p * 2 + (s + 1))
                nc.scalar.copy(flat(h_hi, p * 2 + s), z[:, 3 + s, :]).then_inc(sem("n2_hi"), 1)

            for s in range(2):
                square_block(0, s, True)
            with act.Fori(1, KD // 2) as p:
                for s in range(2):
                    square_block(p, s, False)

            norm_root("n2", r_norm2[:])

            def split_u(b):
                act.wait_ge(sem("ff_u"), b + 1)
                nc.scalar.copy(flat(u_hi, b), ff_u[:, 0, :]).then_inc(sem("u_hi"), 1)

            def up_block(p, b, first):
                split_hi(act, p + 1, 0)
                if not first:
                    split_u(b - 1)
                act.wait_ge(sem("ff_g"), b * 3 + 3)
                nc.scalar.activation(ff_silu[:], ff_conv[:, 0, :], ACT.Silu).then_inc(sem("ff_silu"), 1)
                split_hi(act, p + 1, 1)

            up_block(U_UP // 2, 0, True)
            with act.Fori(1, FF_BLOCKS) as b:
                up_block(b + U_UP // 2, b, False)
            split_u(FF_BLOCKS - 1)
            with act.Fori(U_DOWN // 2 + 1, N_UNITS // 2) as p:
                for s in range(2):
                    split_hi(act, p, s)

        @block.vector
        def _(dve):
            def add_square(tag, buf, s, k, first):
                dve.wait_ge(sem(tag + "_sq"), k + 1)
                if first:
                    nc.vector.tensor_copy(buf[:, 2, :], buf[:, s, :]).then_inc(sem(tag + "_summed"), 1)
                else:
                    dve.wait_ge(sem(tag + "_summed"), k)
                    nc.vector.tensor_tensor(buf[:, 2, :], buf[:, 2, :], buf[:, s, :], ALU.add
                                            ).then_inc(sem(tag + "_summed"), 1)

            def norm(tag, x, gain, root, h, beside=None):
                dve.wait_ge(sem(tag + "_rooted"), 1)
                nc.vector.reciprocal(root, root).then_inc(sem(tag + "_rec"), 1)
                if beside:
                    beside()
                dve.wait_ge(sem(tag + "_rec"), 1)
                for k in range(KD + 1):
                    if k < KD:
                        if k >= 2:
                            dve.wait_ge(sem(tag + "_lo"), k - 1)
                        nc.vector.scalar_tensor_tensor(h[:, k % 2, :], x[:, k, :], param(gain, k), root,
                                                       ALU.mult, ALU.mult).then_inc(sem(tag + "_h"), 1)
                    if k:
                        dve.wait_ge(sem(tag + "_hi"), k)
                        nc.vector.tensor_tensor(h_lo[:, k - 1, :], h[:, (k - 1) % 2, :],
                                                h_hi[:, k - 1, :].bitcast(F32), ALU.subtract
                                                ).then_inc(sem(tag + "_lo"), 1)

            def split_small():
                dve.wait_ge(sem("small_hi"), 1)
                nc.vector.tensor_tensor(small_lo[:], small_raw[:], small_hi[:].bitcast(F32),
                                        ALU.subtract).then_inc(sem("small_lo"), 1)

            nc.vector.memset(ones[:], 1.0).then_inc(sem("ones"), 1)
            for k in range(KD):
                add_square("n1", sq, k % 2, k, k == 0)
            dve.wait_ge(sem("params_loaded"), 16)
            norm("n1", x_in, "norm1", root1[:], h32, split_small)
            dve.wait_ge(sem("small_done"), 1)
            nc.vector.tensor_scalar(halves(st[0][:]), pair(3, R_END), param("stat_bias", rows=R_END),
                                    param("stat_sign", rows=R_END), ALU.add, ALU.mult).then_inc(sem("stat_in"), 1)

            def split_rows(src, dst, hi, lo, name, wait):
                dve.wait_ge(sem(name), wait)
                nc.vector.tensor_tensor(dst[lo:lo + R_GRP, :], src, dst[hi:hi + R_GRP, :].bitcast(F32),
                                        ALU.subtract).then_inc(sem(name), 1)

            taps_at = slice(PARAM["gdn_taps"], PARAM["gdn_taps"] + GDN_TAPS * 3 * HEADS)
            nc.vector.tensor_scalar(prm[:, taps_at], prm[:, taps_at], 0.5, None, ALU.mult
                                    ).then_inc(sem("taps_halved"), 1)
            nc.vector.memset(nf_hl[2 * R_GRP:P, :].bitcast(F32), 0.0).then_inc(sem("masks_r"), 1)
            nc.vector.memset(conv_in[:, :, 0:GDN_TAPS - 1], 0.0).then_inc(sem("pads"), 1)

            def take_v(b):
                dve.wait_ge(sem("v_turned"), b + 1)
                nc.vector.tensor_copy(v_tok[:, :, b * P:(b + 1) * P].rearrange("p (h t) c -> p h t c", h=2),
                                      tiles_of(ps[0:T, 6:8, 0:TH * P], P)).then_inc(sem("v_tok"), 1)

            def log_gates():
                dve.wait_ge(sem("stat_ln"), 1)
                nc.vector.scalar_tensor_tensor(st[2][:], st[0][:], 0.0, st[1][:], ALU.max, ALU.add
                                               ).then_inc(sem("softplus"), 1)
                dve.wait_ge(sem("coef"), 1)
                nc.vector.tensor_scalar(coef[:, 1:2], coef[:, 0:1], -1.0, None, ALU.mult).then_inc(sem("coef"), 1)
                dve.wait_ge(sem("softplus"), 1)
                dve.wait_ge(sem("coef"), 2)
                nc.vector.tensor_scalar(st[1][:], st[2][:], coef[:, 1:2], None, ALU.mult
                                        ).then_inc(sem("log_gates"), 1)
                dve.wait_ge(sem("log_gates"), 1)

            def betas():
                dve.wait_ge(sem("beta_exp"), 1)
                nc.vector.tensor_scalar(st[3][R_B:R_G, :], st[3][R_B:R_G, :], 1.0, None, ALU.add
                                        ).then_inc(sem("beta"), 1)
                dve.wait_ge(sem("beta"), 1)
                nc.vector.reciprocal(stat[R_B:R_G, :], st[3][R_B:R_G, :]).then_inc(sem("stat_rows"), 1)

            def cumsum(steps):
                for i in steps:
                    src, dst, shift = 1 + i % 2, 2 - i % 2, 2 ** i
                    a, b = (st[k][:].rearrange("p (t c) -> p t c", c=T) for k in (src, dst))
                    nc.vector.tensor_tensor(b[:, :, shift:], a[:, :, shift:], a[:, :, :T - shift], ALU.add
                                            ).then_inc(sem("cumsum"), 1)
                    nc.vector.tensor_copy(b[:, :, :shift], a[:, :, :shift]).then_inc(sem("cumsum"), 1)
                    dve.wait_ge(sem("cumsum"), 2 * i + 2)

            def decay_rows():
                g_rows = st_sum[R_G:R_END, :].rearrange("p (t c) -> p t c", c=T)
                nc.vector.tensor_copy(stat[0:R_B, :], st_sum[R_G:R_END, :]).then_inc(sem("g_row"), 1)
                nc.vector.tensor_tensor(to_end[R_G:R_END, :].rearrange("p (t c) -> p t c", c=T),
                                        g_rows[:, :, T - 1:T].broadcast_to([R_END - R_G, NT, T]), g_rows,
                                        ALU.subtract).then_inc(sem("to_end"), 1)

            def forget_sums():
                nc.vector.tensor_copy(f_sum[:, 0:T], st_sum[0:R_GRP, 0:T]).then_inc(sem("f_tile"), 1)
                for t in range(1, NT):
                    dve.wait_ge(sem("f_tile"), t)
                    nc.vector.tensor_scalar(f_sum[:, t * T:(t + 1) * T], st_sum[0:R_GRP, t * T:(t + 1) * T],
                                            f_sum[:, t * T - 1:t * T], None, ALU.add).then_inc(sem("f_tile"), 1)
                dve.wait_ge(sem("f_tile"), NT)
                nc.vector.tensor_scalar(nf_sum[:], f_sum[:], -1.0, None, ALU.mult).then_inc(sem("f_ready"), 1)

            dve.wait_ge(LO_READY, 2)
            for n in range(2 * FOX_BLOCKS):
                split_lo(dve, n // 2 + 1, n % 2)
                if n == 4:
                    log_gates()
                    cumsum(range(0, 2))
                if n == 5:
                    cumsum(range(2, 5))
                if n == 6:
                    cumsum(range(5, n_scan))
                    decay_rows()
                if n == 7:
                    betas()
            for b in range(FOX_BLOCKS):
                split_lo(dve, (U_V + b) // 2 + 1, b % 2)
                if b:
                    take_v(b - 1)
                if b == 0:
                    dve.wait_ge(sem("qk_rooted"), 1)
                    nc.vector.reciprocal(qk_root[:], qk_root[:]).then_inc(sem("qk_rec"), 1)
                if b == 1:
                    forget_sums()
                if b == 2:
                    split_rows(qk_root[:], qk_hl, 0, R_GRP, "qk_split", 1)
            dve.wait_ge(sem("e_rows"), 1)
            dve.wait_ge(sem("stat_rows"), 2)
            nc.vector.scalar_tensor_tensor(stat[R_BE:S_END, :], st[3][R_B:R_G, :], -1.0, stat[R_B:R_G, :], ALU.mult,
                                           ALU.mult).then_inc(sem("stat_rows"), 2)
            take_v(FOX_BLOCKS - 1)
            split_rows(stat[0:R_B, :], g_hl, 0, R_GRP, "g_split", 1)
            split_rows(stat[R_B:R_G, :], b_hl, R_GRP, 0, "b_split", 1)
            split_rows(nf_sum[:], nf_hl, 0, R_GRP, "nf_split", 1)
            dve.wait_ge(sem("tok_turned"), 1)
            nc.vector.tensor_copy(tok[:].rearrange("p (h t) r -> p h t r", h=2),
                                  tiles_of(ps[0:T, 4:6, 0:TH * S_END], S_END)).then_inc(sem("tok_ready"), 1)

            def quarter(u, q, multiplies, takes, finishes):
                v = u - 1
                b = v - U_GDN
                if q == 1 and finishes and v - 1 < U_Z:
                    dve.wait_ge(sem("tanh"), b)
                    nc.vector.scalar_tensor_tensor(woven_target(v - 1), tanh_out[:], 1.0, conv_out[:], ALU.add,
                                                   ALU.mult).then_inc(sem("woven"), 1)
                if not takes:
                    return
                if q == 1 and v >= U_Z:
                    dve.wait_ge(ACC_FREE[v % 2], v // 2 + 1)
                    nc.vector.scalar_tensor_tensor(woven_target(v), tanh_out[:], 1.0, conv_out[:], ALU.add,
                                                   ALU.mult).then_inc(sem("woven"), 1)
                if q and v < U_Z:
                    if q == 1:
                        dve.wait_ge(ACC_FREE[v % 2], v // 2 + 1)
                    for i in ((0,), (1, 2), (3,))[q - 1]:
                        at = GDN_TAPS - 1 - i
                        tap = param("gdn_taps", b * GDN_TAPS + at)
                        if i == 0:
                            if b:
                                dve.wait_ge(sem("woven"), b)
                            nc.vector.tensor_scalar(conv_out[:], conv_in[:, b % 2, at:at + L], tap, None, ALU.mult
                                                    ).then_inc(sem("conv"), 1)
                        else:
                            dve.wait_ge(sem("conv"), b * GDN_TAPS + i)
                            nc.vector.scalar_tensor_tensor(conv_out[:], conv_in[:, b % 2, at:at + L], tap,
                                                           conv_out[:], ALU.mult, ALU.add
                                                           ).then_inc(sem("conv"), 1)

            fill, finish = weave(U_GDN, U_MIX - U_GDN, quarter)
            dve.wait_ge(sem("taps_halved"), 1)
            fill(2)
            for i, n in enumerate(QK_ORDER):
                dve.wait_ge(sem("qk_spread"), i + 1)
                nc.vector.scalar_tensor_tensor(halves(qk[:, n, :]), halves(qk[:, n, :]), param("qk", n),
                                               pair(3 - i % 2), ALU.mult, ALU.mult).then_inc(sem("qk_normed"), 1)
                if i % 4 == 1:
                    fill()

            for n in range(N + 4):
                if n >= 4 and (n - 4) % PAIR_ITEMS == PAIR_ITEMS - 1:
                    b = (n - 4) // PAIR_ITEMS
                    dve.wait_ge(sem("weighed"), (b + 1) * PAIR_ITEMS)
                    nc.vector.tensor_copy(halves(fox_o[:, b, :]), pair(3)).then_inc(sem("fox_taken"), 1)
                if n < N:
                    t = fox_items[n][1]
                    keys = (t + 1) * T
                    dve.wait_ge(sem("scored"), n + 1)
                    if keys <= 512:
                        nc.vector.tensor_reduce(neg_max[:, n:n + 1], ps[0:T, 2 + t % 2, 0:keys], AX.X, ALU.max,
                                                negate=True).then_inc(sem("neg_max"), 1)
                    else:
                        nc.vector.tensor_reduce(neg_max[:, n:n + 1], pair(1, T), AX.XY, ALU.max,
                                                negate=True).then_inc(sem("neg_max"), 1)
                if 1 <= n <= N:
                    i = n - 1
                    keys = (fox_items[i][1] + 1) * T
                    dve.wait_ge(sem("prob_ready"), i + 1)
                    nc.vector.reciprocal(p_rec[:, i:i + 1], p_sum[:, i:i + 1]).then_inc(sem("p_rec"), 1)
                    dve.wait_ge(sem("p_rec"), i + 1)
                    nc.vector.tensor_scalar(prob[:, i % 3, 0:keys], prob[:, i % 3, 0:keys], p_rec[:, i:i + 1], None,
                                            ALU.mult).then_inc(sem("prob_scaled"), 1)
                if n < N + 3:
                    fill()

            def norm_reciprocal(g):
                dve.wait_ge(sem("n_rooted"), g + 1)
                nc.vector.reciprocal(n_root[:], n_root[:]).then_inc(sem("n_rec"), 1)

            def norm_split(g):
                split_rows(n_root[:], n_hl, 0, R_GRP, "n_split", 2 * g + 1)

            def normalize_output(m):
                dve.wait_ge(sem("on_spread"), m + 1)
                nc.vector.scalar_tensor_tensor(halves(o_raw[:, m, :]), halves(o_raw[:, m, :]), param("gdn_norm"),
                                               pair(2 + m % 2), ALU.mult, ALU.mult).then_inc(sem("o_normed"), 1)

            for half_no, qkv in enumerate((qkv0, qkv1)):
                m0 = half_no * HH
                plan = GDN_FILLS[half_no]

                fill(plan["lead"])
                fill(len(NORM_GROUPS[half_no]) // plan["sums"])
                norm_reciprocal(half_no)
                fill(1)
                norm_split(half_no)
                fill(plan["norm_wait"] - 1)
                for n in range(2 * HH):
                    dve.wait_ge(sem("gn_spread"), 2 * m0 + n + 1)
                    nc.vector.tensor_tensor(halves(qkv[:, n, :]), halves(qkv[:, n, :]), pair(2 + n % 2), ALU.mult
                                            ).then_inc(sem("gn_normed"), 1)
                    if n in (2, 5) and plan["spread"]:
                        fill()
                dve.wait_ge(sem("tok_ready"), 1)
                dve.wait_ge(sem("gn_normed"), 2 * m0 + 2 * HH)
                for j in range(HH):
                    m = m0 + j
                    dve.wait_ge(sem("spread"), 2 * m + 2)
                    if j:
                        dve.wait_ge(sem("mats"), 2 * m)
                    nc.vector.tensor_tensor(halves(work[:, 0, :]), pair(2), halves(qkv[:, HH + j, :]), ALU.mult
                                            ).then_inc(sem("k_b"), 1)
                    dve.wait_ge(sem("e_g"), 2 * m + 2)
                    d = decay[:].rearrange("p (h t) c -> p h t c", h=2)
                    nc.vector.tensor_tensor(d, tok[:, :, m:m + 1].broadcast_to([T, NT, T]).rearrange(
                        "p (h t) c -> p h t c", h=2), tiles_of(pair(1, T), T), ALU.subtract
                        ).then_inc(sem("decay_diff"), 1)
                    fill()
                    dve.wait_ge(sem("decay_exp"), m + 1)
                    dve.wait_ge(sem("mats"), 2 * m + 2)
                    nc.vector.tensor_tensor(m_t[:, :, j, :].rearrange("p (h t) c -> p h t c", h=2),
                                            tiles_of(pair(2, T), T), d, ALU.mult).then_inc(sem("mat_taken"), 1)
                    nc.vector.tensor_tensor(decay[:], decay[:],
                                            const("incl", T).unsqueeze(1).broadcast_to([T, NT, T]), ALU.mult
                                            ).then_inc(sem("decay_i"), 1)
                    nc.vector.tensor_tensor(qkv[:, j, :], qkv[:, j, :], work[:, 1, :], ALU.mult
                                            ).then_inc(sem("q_g"), 1)
                    dve.wait_ge(sem("decay_i"), m + 1)
                    nc.vector.tensor_tensor(a_t[:, :, j, :].rearrange("p (h t) c -> p h t c", h=2),
                                            tiles_of(pair(3, T), T), d, ALU.mult).then_inc(sem("mat_taken"), 1)
                    fill(plan["head"] - 1)
                turned, updated = half_no * TURNS, half_no * UPDATES
                if half_no:
                    for j in range(HH):
                        normalize_output(j)
                dve.wait_ge(sem("mat_taken"), 2 * (m0 + HH))
                for c in range(NT):
                    nc.vector.tensor_tensor(mx[:, c % 3, :, :], m_t[:, c, :, :], over_heads(const("pair", T)),
                                            ALU.mult).then_inc(sem("pair_m"), 1)
                    dve.wait_ge(sem("pair_m"), half_no * NT + c + 1)
                    nc.vector.tensor_tensor(inv_t[:, c, :, :], over_heads(const("ident", T, T)), mx[:, c % 3, :, :],
                                            ALU.subtract).then_inc(sem("inv_t"), 1)
                fill(sum(plan["turn"]))
                for lv in range(len(LEVELS)):
                    rows, cols = merged(LEVELS[lv])
                    for step in range(NT + 2):
                        if step < NT:
                            n = lv * NT + step
                            dve.wait_ge(sem("mx_done"), turned + n + 1)
                            if n >= 3:
                                dve.wait_ge(sem("change"), turned + n - 2)
                            product = by_head(2 + n % 2, rows, cols.stop)
                            if LEVELS[lv] < 32:
                                nc.vector.tensor_tensor(mx[:, n % 3, :, :], product, over_heads(level_mask(lv)),
                                                        ALU.mult).then_inc(sem("mx"), 1)
                            else:
                                nc.vector.tensor_copy(mx[rows, n % 3, :, cols], product).then_inc(sem("mx"), 1)
                        if step >= 2:
                            c, n = step - 2, lv * NT + step - 2
                            dve.wait_ge(sem("change"), turned + n + 1)
                            nc.vector.tensor_tensor(inv_t[cols, c, :, rows], inv_t[cols, c, :, rows],
                                                    by_head(4 + n % 2, cols, rows.stop - rows.start),
                                                    ALU.subtract).then_inc(sem("inv_t"), 1)
                    fill(plan["level"])

                def take_block(c, which):
                    n = half_no * NT + c
                    o, row = ((v_b, R_B), (k_d, R_G))[which]
                    dve.wait_ge(sem("vk_turned"), 2 * n + which + 1)
                    scale = tok[:, c, row + m0:row + m0 + HH].unsqueeze(2).broadcast_to([T, HH, DH])
                    nc.vector.tensor_tensor(o[:, c % 2, :, :], ps[0:T, 7, :].rearrange("p (j d) -> p j d", j=HH),
                                            scale, ALU.mult).then_inc(sem("vk_taken"), 1)

                dve.wait_ge(sem("e_g"), 2 * (m0 + HH))
                for which in range(2):
                    take_block(0, which)
                for c in range(NT):
                    n = half_no * NT + c
                    if c:
                        dve.wait_ge(sem("ks_done"), half_no * STEPS + c)
                        dve.wait_ge(sem("vk_taken"), 2 * n + 1)
                        for j in range(HH):
                            nc.vector.scalar_tensor_tensor(resid[:, j, :], ps[0:T, 2, j * DH:(j + 1) * DH],
                                                           tok[:, c, R_BE + m0 + j:R_BE + m0 + j + 1],
                                                           v_b[:, c % 2, j, :], ALU.mult, ALU.add
                                                           ).then_inc(sem("resid"), 1)
                    if c + 1 < NT:
                        take_block(c + 1, 0)
                    fill()
                    if c + 1 < NT:
                        dve.wait_ge(sem("grown"), half_no * STEPS + c + 1)
                        if c:
                            dve.wait_ge(sem("state"), (half_no * STEPS + c) * HH)
                        for j in range(HH):
                            new = state[:, (c + 1) % 2, j, :]
                            grown = ps[:, 4, j * DH:(j + 1) * DH]
                            if c:
                                nc.vector.scalar_tensor_tensor(new, state[:, c % 2, j, :], g_end[:, j, c:c + 1],
                                                               grown, ALU.mult, ALU.add).then_inc(sem("state"), 1)
                            else:
                                nc.vector.tensor_copy(new, grown).then_inc(sem("state"), 1)
                        take_block(c + 1, 1)
                    fill(plan["chunk"][c] - 1)
                dve.wait_ge(sem("o_raw"), (half_no + 1) * NT)
            finish()

            dve.wait_ge(sem("o_normed"), HH)
            dve.wait_ge(sem("woven"), 4 * HEADS)

            def gate_outputs(first, end):
                for n in range(first, end + 1):
                    if n < min(end, HH):
                        if n >= 2:
                            dve.wait_ge(sem("ob_lo"), n - 1)
                        nc.vector.tensor_tensor(zg[:, n % 2, :], z[:, n, :], o_raw[:, n, :], ALU.mult
                                                ).then_inc(sem("gated"), 1)
                    if n > first:
                        dve.wait_ge(sem("ob_hi"), n)
                        nc.vector.tensor_tensor(ob_lo[:, n - 1, :], zg[:, (n - 1) % 2, :],
                                                ob_hi[:, n - 1, :].bitcast(F32), ALU.subtract
                                                ).then_inc(sem("ob_lo"), 1)

            dve.wait_ge(sem("n_sq"), sum(len(g) for g in NORM_GROUPS))
            norm_reciprocal(2)
            norm_split(2)
            gate_outputs(0, HH // 2)
            for m in range(HH, HEADS):
                normalize_output(m)
            dve.wait_ge(LO_READY, U_MIX + 2)

            def mixing_block(p, j, first):
                for s in range(2):
                    split_lo(dve, p + 1, s)
                    if first:
                        gate_outputs(*((HH // 2, HH), (HH, HEADS))[s])
                for s, gate in enumerate((gate_b, gate_a)):
                    dve.wait_ge(ACC_FREE[1 - s], p + 1)
                    dve.wait_ge(UNIT_USED, p * 2 + (s + 3))
                    nc.vector.scalar_tensor_tensor(halves(gate[:]), halves(gate[:]), 1.0, pair(s), ALU.add, ALU.mult
                                                   ).then_inc(ACC_FREE[s], 1)
                    split_lo(dve, p + 2, s)
                for s in range(2):
                    dve.wait_ge(ACC_FREE[s], p + 2)
                nc.vector.tensor_tensor(gate_a[:], gate_a[:], gate_b[:], ALU.add).then_inc(sem("mixed"), 1)
                dve.wait_ge(sem("mix_hi"), j + 1)
                nc.vector.scalar_tensor_tensor(flat(mix_lo, j), gate_a[:], 0.5, flat(mix_hi, j).bitcast(F32),
                                               ALU.mult, ALU.subtract).then_inc(sem("mix_lo"), 1)

            mixing_block(U_MIX // 2, 0, True)
            with dve.Fori(1, KD) as j:
                mixing_block(j * (MIX_UNITS // 2) + U_MIX // 2, j, False)

            dve.wait_ge(sem("x_reloaded"), 16)

            def split_h(j, s):
                dve.wait_ge(sem("n2_hi"), j + 1)
                nc.vector.tensor_tensor(flat(h_lo, j), z[:, 3 + s, :], flat(h_hi, j).bitcast(F32), ALU.subtract
                                        ).then_inc(sem("n2_lo"), 1)

            def residual_block(p, s, first):
                j = p * 2 + s
                dve.wait_ge(UNIT_USED, j + (U_OUT + 1))
                nc.vector.tensor_tensor(block_of(x_res, j), pair(s), block_of(x_res, j), ALU.add
                                        ).then_inc(ACC_FREE[s], 1)
                split_lo(dve, p + (U_OUT // 2 + 1), s)
                if not first:
                    add_square("n2", z, 1 - s, p * 2 + (s - 1), False)
                    split_h(p * 2 + (s - 1), 1 - s)

            for s in range(2):
                residual_block(0, s, True)
            add_square("n2", z, 0, 0, True)
            split_h(0, 0)
            with dve.Fori(1, KD // 2) as p:
                for s in range(2):
                    residual_block(p, s, False)
            add_square("n2", z, (KD - 1) % 2, KD - 1, False)
            split_h(KD - 1, (KD - 1) % 2)
            nc.vector.memset(ff_in[:, :, 0:FFN_TAPS - 1], 0.0).then_inc(sem("ff_pads"), 1)
            dve.wait_ge(sem("n2_rooted"), 1)
            nc.vector.reciprocal(r_norm2[:], r_norm2[:]).then_inc(sem("n2_rec"), 1)

            dve.wait_ge(sem("ff_pads"), 1)
            dve.wait_ge(sem("n2_rec"), 1)

            def ff_conv_block(p, b, s, name, first):
                dve.wait_ge(UNIT_USED, p * 2 + (s + 1))
                nc.vector.tensor_tensor(halves(ff_in[:, s, FFN_TAPS - 1:]), pair(s), halves(r_norm2[:]), ALU.mult
                                        ).then_inc(ACC_FREE[s], 1)
                split_lo(dve, p + 1, s)
                dve.wait_ge(ACC_FREE[s], p + 1)
                taps = [param("ffn_taps", b * (2 * FFN_TAPS) + (s * FFN_TAPS + i)) for i in range(FFN_TAPS)]
                o = ff_conv[:, s, :]
                if s == 0 and not first:
                    dve.wait_ge(sem("ff_silu"), b)
                nc.vector.tensor_scalar(o, ff_in[:, s, FFN_TAPS - 1:], taps[-1], None, ALU.mult
                                        ).then_inc(sem(name), 1)
                for i in range(1, FFN_TAPS):
                    at = FFN_TAPS - 1 - i
                    dve.wait_ge(sem(name), b * FFN_TAPS + i)
                    nc.vector.scalar_tensor_tensor(o, ff_in[:, s, at:at + L], taps[at], o, ALU.mult, ALU.add
                                                   ).then_inc(sem(name), 1)

            def split_u(b):
                dve.wait_ge(sem("u_hi"), b + 1)
                nc.vector.tensor_tensor(flat(u_lo, b), ff_u[:, 0, :], flat(u_hi, b).bitcast(F32), ALU.subtract
                                        ).then_inc(sem("u_lo"), 1)

            def up_block(p, b, first):
                ff_conv_block(p, b, 0, "ff_g", first)
                if not first:
                    split_u(b - 1)
                ff_conv_block(p, b, 1, "ff_v", first)
                dve.wait_ge(sem("ff_silu"), b + 1)
                dve.wait_ge(sem("ff_v"), b * FFN_TAPS + FFN_TAPS)
                if not first:
                    dve.wait_ge(sem("u_lo"), b)
                nc.vector.tensor_tensor(ff_u[:, 0, :], ff_silu[:], ff_conv[:, 1, :], ALU.mult
                                        ).then_inc(sem("ff_u"), 1)

            up_block(U_UP // 2, 0, True)
            with dve.Fori(1, FF_BLOCKS) as b:
                up_block(b + U_UP // 2, b, False)
            split_u(FF_BLOCKS - 1)

            def down_block(q, s, first, last):
                for part in range(DOWN_UNITS):
                    n = s * DOWN_UNITS + part
                    if not (last and n + 2 >= 2 * DOWN_UNITS):
                        split_lo(dve, q * DOWN_UNITS + (U_DOWN // 2 + n // 2 + 1), n % 2)
                dve.wait_ge(UNIT_USED, q * 2 * DOWN_UNITS + (U_DOWN + (s + 1) * DOWN_UNITS))
                if not first:
                    dve.wait_ge(sem(f"stored{s}"), q * 16)
                nc.vector.tensor_tensor(halves(y_out[:, s, :]), pair(s), block_of(x_res, q * 2 + s), ALU.add
                                        ).then_inc(sem("y_ready"), 1)
                dve.wait_ge(sem("y_ready"), q * 2 + (s + 1))
                nc.vector.sem_inc(ACC_FREE[s], 1)

            for s in range(2):
                down_block(0, s, True, False)
            with dve.Fori(1, KD // 2 - 1) as q:
                for s in range(2):
                    down_block(q, s, False, False)
            for s in range(2):
                down_block(KD // 2 - 1, s, False, True)


def constants():
    c = np.zeros((P, C_COLS), np.float32)

    def put(name, value):
        c[:value.shape[0], CONST[name]:CONST[name] + value.shape[1]] = value

    r, k = np.arange(T)[:, None], np.arange(T)[None, :]
    put("ident", np.eye(P, dtype=np.float32))
    put("row_of", np.eye(1, 2 * R_GRP, R_GRP - 1, dtype=np.float32).repeat(P, 0))
    put("row_of64", np.eye(2, 2 * R_GRP, R_GRP - 1, dtype=np.float32).repeat(FOX_DIM, 0))
    put("incl", (r <= k).astype(np.float32))
    put("pair", ((k % 2 == 1) & (r == k - 1)).astype(np.float32))
    put("neg", np.where(k > r, np.float32(-1e30), np.float32(0)))
    put("levels", np.concatenate([((r // n % 2 == 1) & (k // n == r // n - 1)) for n in MASKED], 1
                                 ).astype(np.float32))
    return c


def row_selections():
    s = np.zeros((P, SELECTS + 2 * FOX_BLOCKS, P), np.float32)
    for base in (0, R_GRP):
        for n in range(SELECTS):
            s[base + n, n] = 1
        for n in range(2 * FOX_BLOCKS):
            for side in range(2):
                s[base + 2 * n + side, SELECTS + n, side * FOX_DIM:(side + 1) * FOX_DIM] = 1
    return s


def lay_out(inputs):
    a = {k: np.asarray(v) for k, v in inputs.items()}
    tokens = np.concatenate([a["meta_tokens"], a["x"][0]])
    x_t = np.ascontiguousarray(tokens.T.reshape(KD, P, L).transpose(1, 0, 2))
    w_in = a["w_in"][0]
    fox_w, gdn_w = FOX_HEADS * FOX_DIM, HEADS * DH
    o_f = 3 * fox_w
    o_g = o_f + FOX_HEADS
    o_b = o_g + 3 * gdn_w
    o_z = o_b + 2 * HEADS
    o_gate = o_z + gdn_w

    def rows(w):
        return w.reshape(-1, P, w.shape[1]).transpose(1, 0, 2)

    def unit(w):
        u = np.zeros((P, UNIT), w.dtype)
        u[:, :w.shape[0]] = rows(w).reshape(P, -1)
        return u

    small = np.zeros((D, R_END), w_in.dtype)
    small[:, R_F:R_F + HEADS] = w_in[:, o_f:o_f + HEADS]
    small[:, R_B:R_B + HEADS] = w_in[:, o_b:o_b + HEADS]
    small[:, R_G:R_G + HEADS] = w_in[:, o_b + HEADS:o_z]

    units = [w_in[:, b * P:(b + 1) * P] for b in range(3 * FOX_BLOCKS)]
    gdn_cols = [which * gdn_w + (half * HH + j) * DH for half in range(2) for which in range(3) for j in range(HH)]
    units += [w_in[:, o_g + c:o_g + c + P] for c in gdn_cols]
    units += [w_in[:, o_z + j * P:o_z + (j + 1) * P] for j in range(HEADS)]
    for j in range(KD):
        at = slice(j * P, (j + 1) * P)
        units += [w_in[:, o_gate:o_gate + D][:, at], w_in[:, o_gate + D:][:, at],
                  a["w_branch_b"][0][:, at], a["w_branch_a"][0][:, at]]
    units += [a["w_out"][0][:, j * P:(j + 1) * P] for j in range(KD)]
    for b in range(FF_BLOCKS):
        for s in range(2):
            units.append(a["w_up"][0][:, s * D_FF + b * P:s * D_FF + (b + 1) * P])
    for j in range(KD):
        for part in range(DOWN_UNITS):
            units.append(a["w_down"][0][part * D:(part + 1) * D, j * P:(j + 1) * P])
    w_units = np.stack([unit(u) for u in units])

    prm = np.zeros((P, P_COLS), np.float32)

    def put(name, value, i=0, rows_at=0):
        prm[rows_at:rows_at + value.shape[0], PARAM[name] + i:PARAM[name] + i + value.shape[1]] = value

    put("norm1", a["norm1_g"][0].reshape(KD, P).T)
    put("norm2", a["norm2_g"][0].reshape(KD, P).T)
    put("gdn_norm", a["gdn_norm_g"][0][:, None])
    put("stat_bias", a["fox_f_bias"][0][:, None], rows_at=R_F)
    put("stat_bias", a["gdn_dt_bias"][0][:, None], rows_at=R_G)
    for at, sign in ((R_F, -1), (R_B, -1), (R_G, 1)):
        put("stat_sign", np.full((HEADS, 1), sign, np.float32), rows_at=at)
    put("a_log", a["gdn_a_log"][0][:, None], rows_at=R_G)
    put("eps", np.full((P, 1), EPS, np.float32))
    row = np.arange(R_GRP)
    put("n_scale", np.where(row < HH, DH, np.where(row < O_ROW, 1, 1.0 / DH))[:, None])
    put("n_bias", np.where(row < HH, EPS * DH, EPS)[:, None])
    put("qk_scale", np.where(np.arange(R_GRP) < FOX_HEADS, 1, 1.0 / FOX_DIM)[:, None])
    put("qk_bias", np.where(np.arange(R_GRP) < FOX_HEADS, EPS * FOX_DIM, EPS)[:, None])
    for b in range(2 * FOX_BLOCKS):
        gain = a["fox_q_norm_g" if b < FOX_BLOCKS else "fox_k_norm_g"][0]
        put("qk", np.concatenate([gain, gain])[:, None], b)
    for n, c in enumerate(gdn_cols):
        put("gdn_taps", a["gdn_conv_w"][0][:, c:c + P].T, GDN_TAPS * n)
    for b in range(FF_BLOCKS):
        for s in range(2):
            c = s * D_FF + b * P
            put("ffn_taps", a["ffn_conv_w"][0][:, c:c + P].T, FFN_TAPS * (2 * b + s))
    return {"x_t": x_t, "w_small": np.ascontiguousarray(rows(small)), "w_units": w_units, "params": prm,
            "consts": constants(), "selects": row_selections()}


def kernel(**inputs):
    import concourse.bacc as bacc
    from concourse.bass_utils import run_bass_kernel_spmd

    nc = bacc.Bacc("TRN2", target_bir_lowering=False, num_devices=1)
    arrays = {f"in_{k}": v for k, v in lay_out(inputs).items()}
    args = [nc.dram_tensor(k, v.shape, mybir.dt.from_np(v.dtype), kind="ExternalInput").ap()
            for k, v in arrays.items()]
    out = nc.dram_tensor("out_y", (KD, P, SEQ), F32, kind="ExternalOutput").ap()
    build_trunk(nc, *args, out)
    r = run_bass_kernel_spmd(nc, [arrays], core_ids=[0])
    return np.ascontiguousarray(r.results[0]["out_y"].reshape(1, D, SEQ).transpose(0, 2, 1))
```
